# Optimizing a Trainium2 kernel written in Bass

```python
import math
import jax, jax.numpy as jnp
from jax import lax
import numpy as np
import jax
import jax.numpy as jnp

D_MODEL = 2048
BATCH = 1
SEQ = 256
DEPTH = 1

D_MIX = D_MODEL
C_CONV = D_MIX // 2
HEAD_DIM = 64
N_HEADS = (D_MIX - C_CONV) // HEAD_DIM
N_KV = 2
GROUP = N_HEADS // N_KV
ATTN_W = N_HEADS * HEAD_DIM
KV_W = N_KV * HEAD_DIM
CONV_WIDTH = 31
WINDOW = 128
BLOCK = 128
LN_EPS = 1e-5
NEG_INF = -1e30
DEEPNORM_ALPHA = (2 * DEPTH) ** 0.25
DEEPNORM_BETA = (8 * DEPTH) ** -0.25

SPLIT_SIZES = (C_CONV, C_CONV, C_CONV, ATTN_W, KV_W, KV_W, ATTN_W)
D_IN = sum(SPLIT_SIZES)
SPLIT_POINTS = tuple(int(p) for p in np.cumsum(SPLIT_SIZES)[:-1])


def layer_norm(x, g, b):
    xf = x.astype(jnp.float32)
    mu = jnp.mean(xf, axis=-1, keepdims=True)
    var = jnp.mean(jnp.square(xf - mu), axis=-1, keepdims=True)
    y = (xf - mu) * lax.rsqrt(var + LN_EPS)
    return (y * g.astype(jnp.float32) + b.astype(jnp.float32)).astype(x.dtype)

def conformer_conv_branch(u_val, u_glu, conv_w, conv_b, ln_g, ln_b):
    h = u_val * jax.nn.sigmoid(u_glu)
    h = lax.conv_general_dilated(
        h, conv_w[:, None, :].astype(h.dtype), window_strides=(1,),
        padding=[(CONV_WIDTH - 1, 0)],
        dimension_numbers=("NWC", "WIO", "NWC"),
        feature_group_count=C_CONV) + conv_b
    h = layer_norm(h, ln_g, ln_b)
    return jax.nn.silu(h)

def swa_sink_attention(q, k, v, sinks):
    B, S, _ = q.shape
    nb = S // BLOCK
    q = q.reshape(B, nb, BLOCK, N_KV, GROUP, HEAD_DIM)
    k = k.reshape(B, nb, BLOCK, N_KV, HEAD_DIM)
    v = v.reshape(B, nb, BLOCK, N_KV, HEAD_DIM)
    pad = ((0, 0), (1, 0), (0, 0), (0, 0), (0, 0))
    kk = jnp.concatenate([jnp.pad(k, pad)[:, :-1], k], axis=2)
    vv = jnp.concatenate([jnp.pad(v, pad)[:, :-1], v], axis=2)
    scale = HEAD_DIM ** -0.5
    scores = jnp.einsum("bnqkgd,bnskd->bnkgqs", q, kk).astype(jnp.float32) * scale
    qi = jnp.arange(BLOCK)[:, None]
    si = jnp.arange(2 * BLOCK)[None, :]
    diff = qi + BLOCK - si
    band = (diff >= 0) & (diff < WINDOW)
    blk = jnp.arange(nb)[:, None, None]
    valid = band[None] & ((blk > 0) | (si >= BLOCK)[None])
    scores = jnp.where(valid[None, :, None, None], scores, NEG_INF)
    sink = sinks.astype(jnp.float32).reshape(1, 1, N_KV, GROUP, 1, 1)
    m = jnp.maximum(jnp.max(scores, axis=-1, keepdims=True), sink)
    p = jnp.exp(scores - m)
    denom = jnp.sum(p, axis=-1, keepdims=True) + jnp.exp(sink - m)
    probs = (p / denom).astype(vv.dtype)
    out = jnp.einsum("bnkgqs,bnskd->bnqkgd", probs, vv)
    return out.reshape(B, S, ATTN_W)

def hybrid_layer(x, w_in, b_in, conv_w, conv_b, conv_ln_g, conv_ln_b, sinks,
                 w_out, b_out, ln_g, ln_b):
    proj = jnp.einsum("bsd,de->bse", x, w_in) + b_in
    c_val, c_glu, c_gate, q, k, v, a_gate = jnp.split(proj, SPLIT_POINTS, axis=-1)
    y_conv = conformer_conv_branch(c_val, c_glu, conv_w, conv_b, conv_ln_g, conv_ln_b)
    y_conv = y_conv * jax.nn.silu(c_gate)
    y_attn = swa_sink_attention(q, k, v, sinks) * jax.nn.silu(a_gate)
    y = jnp.concatenate([y_conv, y_attn], axis=-1)
    y = jnp.einsum("bse,ed->bsd", y, w_out) + b_out
    return layer_norm(DEEPNORM_ALPHA * x + y, ln_g, ln_b)

def first_inputs(seed: int = 0) -> dict:
    key = jax.random.key(seed)
    ks = jax.random.split(key, 12)
    f32 = jnp.float32
    x = jax.random.normal(ks[0], (BATCH, SEQ, D_MODEL), f32)
    w_in = jax.random.normal(ks[1], (DEPTH, D_MODEL, D_IN), f32) * D_MODEL ** -0.5
    b_in = jax.random.normal(ks[2], (DEPTH, D_IN), f32) * 0.02
    conv_w = jax.random.normal(ks[3], (DEPTH, CONV_WIDTH, C_CONV), f32) * CONV_WIDTH ** -0.5
    conv_b = jax.random.normal(ks[4], (DEPTH, C_CONV), f32) * 0.02
    conv_ln_g = 1.0 + 0.1 * jax.random.normal(ks[5], (DEPTH, C_CONV), f32)
    conv_ln_b = 0.02 * jax.random.normal(ks[6], (DEPTH, C_CONV), f32)
    sinks = 0.5 * jax.random.normal(ks[7], (DEPTH, N_HEADS), f32)
    w_out = (jax.random.normal(ks[8], (DEPTH, D_MIX, D_MODEL), f32)
             * D_MIX ** -0.5 * DEEPNORM_BETA)
    b_out = jax.random.normal(ks[9], (DEPTH, D_MODEL), f32) * 0.02
    ln_g = 1.0 + 0.1 * jax.random.normal(ks[10], (DEPTH, D_MODEL), f32)
    ln_b = 0.02 * jax.random.normal(ks[11], (DEPTH, D_MODEL), f32)
    return {"x": x, "w_in": w_in, "b_in": b_in, "conv_w": conv_w, "conv_b": conv_b,
            "conv_ln_g": conv_ln_g, "conv_ln_b": conv_ln_b, "sinks": sinks,
            "w_out": w_out, "b_out": b_out, "ln_g": ln_g, "ln_b": ln_b}

def first_block(x, w_in, b_in, conv_w, conv_b, conv_ln_g, conv_ln_b, sinks,
              w_out, b_out, ln_g, ln_b):
    h = x
    for l in range(DEPTH):
        h = hybrid_layer(h, w_in[l], b_in[l], conv_w[l], conv_b[l], conv_ln_g[l],
                         conv_ln_b[l], sinks[l], w_out[l], b_out[l], ln_g[l], ln_b[l])
    return h


MEM_LEN = 256
EPS = 1e-6
NEG = -1e30
BIG = 1e30
NSA_HEADS = 8
NSA_KV_HEADS = 2
NSA_GROUP = NSA_HEADS // NSA_KV_HEADS
NSA_DK = 128
NSA_DV = 128
CMP_LEN = 32
CMP_STRIDE = 16
CMP_HIDDEN = 256
SEL_BLOCK = 64
SEL_TOP = 16
WINDOW_2 = 512
NSA_QBLOCK = 64
GLA_HEADS = 4
GLA_DK = 128
GLA_DV = 256
GLA_GATE_RANK = 16
GLA_GATE_NORM = 16.0
GLA_CHUNK = 64
D_MIX_2 = NSA_HEADS * NSA_DV + GLA_HEADS * GLA_DV
MEM_HEADS = 4
MEM_DH = 128
D_FF = -(-8 * D_MODEL // (3 * 256)) * 256
IN_SIZES = (
    NSA_HEADS * NSA_DK,
    NSA_KV_HEADS * NSA_DK, NSA_KV_HEADS * NSA_DV,
    NSA_KV_HEADS * NSA_DK, NSA_KV_HEADS * NSA_DV,
    NSA_KV_HEADS * NSA_DK, NSA_KV_HEADS * NSA_DV,
    3 * NSA_HEADS,
    GLA_HEADS * GLA_DK, GLA_HEADS * GLA_DK,
    GLA_HEADS * GLA_DV,
    GLA_GATE_RANK,
    GLA_HEADS * GLA_DV,
)
D_IN_2 = sum(IN_SIZES)


def rms_norm(u, g):
    uf = u.astype(jnp.float32)
    y = uf * lax.rsqrt(jnp.mean(uf * uf, axis=-1, keepdims=True) + EPS)
    return (y * g.astype(jnp.float32)).astype(u.dtype)

def alibi_slopes(n):
    return jnp.exp2(-8.0 * jnp.arange(1, n + 1, dtype=jnp.float32) / n)

def split_points():
    return np.cumsum(np.array(IN_SIZES))[:-1].tolist()

def nsa_mixer(q, k_cmp, v_cmp, k_slc, v_slc, k_win, v_win, gates,
              g_q, g_kc, g_ks, g_kw, pe_k, pe_v, w_ck1, w_ck2, w_cv1, w_cv2):
    f32 = jnp.float32
    B, T = q.shape[0], q.shape[1]
    HKV, G, QB = NSA_KV_HEADS, NSA_GROUP, NSA_QBLOCK
    n_cmp = (T - CMP_LEN) // CMP_STRIDE + 1
    n_sel = T // SEL_BLOCK
    n_top = min(SEL_TOP, n_sel)
    n_qb = T // QB
    ratio = SEL_BLOCK // CMP_STRIDE
    lead = CMP_LEN // CMP_STRIDE - 1

    tok = jnp.arange(n_cmp)[:, None] * CMP_STRIDE + jnp.arange(CMP_LEN)[None, :]

    def compress(u, pe, w1, w2):
        blk = u[:, tok] + pe[None, None, :, None, :]
        blk = blk.transpose(0, 1, 3, 2, 4).reshape(B, n_cmp, HKV, -1)
        return (jax.nn.silu(blk @ w1) @ w2).transpose(0, 2, 1, 3)

    kc = rms_norm(compress(k_cmp, pe_k, w_ck1, w_ck2), g_kc)
    vc = compress(v_cmp, pe_v, w_cv1, w_cv2)
    cmp_end = jnp.arange(n_cmp) * CMP_STRIDE + (CMP_LEN - 1)
    cmp_mid = jnp.arange(n_cmp).astype(f32) * CMP_STRIDE + 0.5 * (CMP_LEN - 1)

    r = np.arange(ratio + lead)
    st = CMP_STRIDE * (r - lead)
    ov = jnp.asarray((np.minimum(st + CMP_LEN, SEL_BLOCK) - np.maximum(st, 0)) / CMP_STRIDE, f32)
    sel_idx = jnp.arange(n_sel)[:, None] * ratio + jnp.asarray(r)[None, :]

    ksb = rms_norm(k_slc, g_ks).reshape(B, n_sel, SEL_BLOCK, HKV, NSA_DK).transpose(0, 3, 1, 2, 4)
    vsb = v_slc.reshape(B, n_sel, SEL_BLOCK, HKV, NSA_DV).transpose(0, 3, 1, 2, 4)
    pad_t = ((0, 0), (0, 0), (WINDOW_2, 0), (0, 0))
    kwp = jnp.pad(rms_norm(k_win, g_kw).transpose(0, 2, 1, 3), pad_t)
    vwp = jnp.pad(v_win.transpose(0, 2, 1, 3), pad_t)

    slopes = alibi_slopes(NSA_HEADS).reshape(HKV, G)
    sl5 = slopes[None, :, :, None, None]
    sl6 = slopes[None, :, :, None, None, None]
    jb = jnp.arange(n_sel)
    bi = jnp.arange(B)[:, None, None, None]
    hi = jnp.arange(HKV)[None, :, None, None]

    qn = rms_norm(q, g_q) * (NSA_DK ** -0.5)
    qs = qn.reshape(B, n_qb, QB, HKV, G, NSA_DK).transpose(1, 0, 3, 4, 2, 5)
    gs = gates.reshape(B, n_qb, QB, HKV, G, 3).transpose(1, 0, 3, 4, 2, 5)

    def block(args):
        c, qb, gb = args
        t = c * QB + jnp.arange(QB)
        s = jnp.einsum('bkgtd,bknd->bkgtn', qb, kc).astype(f32)
        vis = t[:, None] >= cmp_end[None, :]
        s = jnp.where(vis, s - sl5 * (t[:, None].astype(f32) - cmp_mid[None, :]), NEG)
        p = jax.nn.softmax(s, axis=-1)
        p = jnp.where(jnp.any(vis, axis=-1)[:, None], p, 0.0)
        o_cmp = jnp.einsum('bkgtn,bknd->bkgtd', p.astype(vc.dtype), vc)
        imp = jnp.pad(p.sum(2), ((0, 0), (0, 0), (0, 0), (lead, lead)))
        imp = jnp.einsum('bktjr,r->bktj', imp[..., sel_idx], ov)
        cur = (t // SEL_BLOCK)[:, None]
        forced = (jb == 0) | (jb == cur) | (jb == cur - 1)
        score = jnp.where(forced, BIG, jnp.where(jb <= cur, imp, NEG))
        top_s, top_i = lax.top_k(score, n_top)
        ks_g = ksb[bi, hi, top_i]
        vs_g = vsb[bi, hi, top_i]
        pos = top_i[..., None] * SEL_BLOCK + jnp.arange(SEL_BLOCK)
        tt = t[:, None, None]
        ok = (top_s > 0.5 * NEG)[..., None] & (pos <= tt)
        s = jnp.einsum('bkgtd,bktnsd->bkgtns', qb, ks_g).astype(f32)
        s = jnp.where(ok[:, :, None], s - sl6 * (tt - pos).astype(f32)[:, :, None], NEG)
        p = jax.nn.softmax(s.reshape(s.shape[:4] + (-1,)), axis=-1).reshape(s.shape)
        o_slc = jnp.einsum('bkgtns,bktnsd->bkgtd', p.astype(vs_g.dtype), vs_g)
        kw = lax.dynamic_slice_in_dim(kwp, c * QB, QB + WINDOW_2, axis=2)
        vw = lax.dynamic_slice_in_dim(vwp, c * QB, QB + WINDOW_2, axis=2)
        pos_w = c * QB - WINDOW_2 + jnp.arange(QB + WINDOW_2)
        dw = t[:, None] - pos_w[None, :]
        okw = (dw >= 0) & (dw < WINDOW_2) & (pos_w >= 0)[None, :]
        s = jnp.einsum('bkgtd,bksd->bkgts', qb, kw).astype(f32)
        s = jnp.where(okw, s - sl5 * dw.astype(f32), NEG)
        p = jax.nn.softmax(s, axis=-1)
        o_win = jnp.einsum('bkgts,bksd->bkgtd', p.astype(vw.dtype), vw)
        return gb[..., 0:1] * o_cmp + gb[..., 1:2] * o_slc + gb[..., 2:3] * o_win

    out = lax.map(block, (jnp.arange(n_qb), qs, gs))
    return out.transpose(1, 0, 4, 2, 3, 5).reshape(B, T, NSA_HEADS, NSA_DV)

def gla_mixer(q, k, v, log_a):
    B, T, H, DK = q.shape
    DV = v.shape[-1]
    C = GLA_CHUNK
    n = T // C

    def chunks(u):
        return u.astype(jnp.float32).reshape(B, n, C, H, -1).transpose(1, 0, 3, 2, 4)

    causal = jnp.tril(jnp.ones((C, C), bool))[:, :, None]

    def step(S, inp):
        qc, kc, vc, ac = inp
        b = jnp.cumsum(ac, axis=2)
        decay = jnp.exp(jnp.where(causal, b[:, :, :, None, :] - b[:, :, None, :, :], -jnp.inf))
        attn = jnp.einsum('bhid,bhjd,bhijd->bhij', qc, kc, decay)
        o = (jnp.einsum('bhij,bhjv->bhiv', attn, vc)
             + jnp.einsum('bhid,bhdv->bhiv', qc * jnp.exp(b), S))
        b_end = b[:, :, -1:, :]
        S = (S * jnp.exp(b_end[:, :, 0, :, None])
             + jnp.einsum('bhjd,bhjv->bhdv', kc * jnp.exp(b_end - b), vc))
        return S, o

    S0 = jnp.zeros((B, H, DK, DV), jnp.float32)
    _, o = lax.scan(step, S0, (chunks(q), chunks(k), chunks(v), chunks(log_a)))
    return o.transpose(1, 0, 3, 2, 4).reshape(B, T, H, DV)

def hybrid_layer_2(x, mem, g_mix, w_in, b_nsa_gate, g_q, g_kc, g_ks, g_kw, pe_k, pe_v,
                 w_ck1, w_ck2, w_cv1, w_cv2, g_nsa_out, w_gk2, b_gk, g_gla_out, w_out,
                 g_cross, g_mem, w_cq, w_ck, w_cv, g_cq, g_ck, w_co, g_ffn, w_gu, w_down):
    B, T, _ = x.shape
    M = mem.shape[1]
    h = rms_norm(x, g_mix)
    (q, k_c, v_c, k_s, v_s, k_w, v_w, g_logit,
     q_l, k_l, v_l, a_l, r_l) = jnp.split(h @ w_in, split_points(), axis=-1)

    def heads(u, nh):
        return u.reshape(B, T, nh, -1)

    hkv = NSA_KV_HEADS
    gates = jax.nn.sigmoid(g_logit + b_nsa_gate).reshape(B, T, NSA_HEADS, 3)
    o_nsa = nsa_mixer(heads(q, NSA_HEADS), heads(k_c, hkv), heads(v_c, hkv), heads(k_s, hkv),
                      heads(v_s, hkv), heads(k_w, hkv), heads(v_w, hkv), gates,
                      g_q, g_kc, g_ks, g_kw, pe_k, pe_v, w_ck1, w_ck2, w_cv1, w_cv2)
    o_nsa = rms_norm(o_nsa, g_nsa_out).reshape(B, T, -1)

    log_a = jax.nn.log_sigmoid((a_l @ w_gk2 + b_gk).astype(jnp.float32)) / GLA_GATE_NORM
    o_gla = gla_mixer(heads(q_l, GLA_HEADS) * (GLA_DK ** -0.5), heads(k_l, GLA_HEADS),
                      heads(v_l, GLA_HEADS), heads(log_a, GLA_HEADS))
    o_gla = rms_norm(o_gla, g_gla_out).astype(x.dtype).reshape(B, T, -1) * jax.nn.silu(r_l)
    x = x + jnp.concatenate([o_nsa, o_gla], axis=-1) @ w_out

    hq = rms_norm(x, g_cross)
    hm = rms_norm(mem, g_mem)
    cq = rms_norm((hq @ w_cq).reshape(B, T, MEM_HEADS, MEM_DH), g_cq) * (MEM_DH ** -0.5)
    ck = rms_norm((hm @ w_ck).reshape(B, M, MEM_HEADS, MEM_DH), g_ck)
    cv = (hm @ w_cv).reshape(B, M, MEM_HEADS, MEM_DH)
    s = jnp.einsum('bthd,bmhd->bhtm', cq, ck).astype(jnp.float32)
    p = jax.nn.softmax(s, axis=-1).astype(cv.dtype)
    x = x + jnp.einsum('bhtm,bmhd->bthd', p, cv).reshape(B, T, -1) @ w_co

    hf = rms_norm(x, g_ffn)
    gg, uu = jnp.split(hf @ w_gu, 2, axis=-1)
    return x + (jax.nn.silu(gg) * uu) @ w_down

def second_inputs(seed: int = 0) -> dict:
    key = jax.random.key(seed)
    keys = iter(jax.random.split(key, 40))
    L = DEPTH

    def nrm(shape, scale):
        return scale * jax.random.normal(next(keys), shape, jnp.float32)

    def gain(n):
        return 1.0 + nrm((L, n), 0.05)

    return {
        'x': nrm((BATCH, SEQ, D_MODEL), 1.0),
        'mem': nrm((BATCH, MEM_LEN, D_MODEL), 1.0),
        'g_mix': gain(D_MODEL),
        'w_in': nrm((L, D_MODEL, D_IN_2), D_MODEL ** -0.5),
        'b_nsa_gate': nrm((L, 3 * NSA_HEADS), 0.1),
        'g_q': gain(NSA_DK),
        'g_kc': gain(NSA_DK),
        'g_ks': gain(NSA_DK),
        'g_kw': gain(NSA_DK),
        'pe_k': nrm((L, CMP_LEN, NSA_DK), 0.5),
        'pe_v': nrm((L, CMP_LEN, NSA_DV), 0.5),
        'w_ck1': nrm((L, CMP_LEN * NSA_DK, CMP_HIDDEN), (CMP_LEN * NSA_DK) ** -0.5),
        'w_ck2': nrm((L, CMP_HIDDEN, NSA_DK), CMP_HIDDEN ** -0.5),
        'w_cv1': nrm((L, CMP_LEN * NSA_DV, CMP_HIDDEN), (CMP_LEN * NSA_DV) ** -0.5),
        'w_cv2': nrm((L, CMP_HIDDEN, NSA_DV), CMP_HIDDEN ** -0.5),
        'g_nsa_out': gain(NSA_DV),
        'w_gk2': nrm((L, GLA_GATE_RANK, GLA_HEADS * GLA_DK), GLA_GATE_RANK ** -0.5),
        'b_gk': nrm((L, GLA_HEADS * GLA_DK), 0.1),
        'g_gla_out': gain(GLA_DV),
        'w_out': nrm((L, D_MIX_2, D_MODEL), D_MIX_2 ** -0.5),
        'g_cross': gain(D_MODEL),
        'g_mem': gain(D_MODEL),
        'w_cq': nrm((L, D_MODEL, MEM_HEADS * MEM_DH), D_MODEL ** -0.5),
        'w_ck': nrm((L, D_MODEL, MEM_HEADS * MEM_DH), D_MODEL ** -0.5),
        'w_cv': nrm((L, D_MODEL, MEM_HEADS * MEM_DH), D_MODEL ** -0.5),
        'g_cq': gain(MEM_DH),
        'g_ck': gain(MEM_DH),
        'w_co': nrm((L, MEM_HEADS * MEM_DH, D_MODEL), (MEM_HEADS * MEM_DH) ** -0.5),
        'g_ffn': gain(D_MODEL),
        'w_gu': nrm((L, D_MODEL, 2 * D_FF), D_MODEL ** -0.5),
        'w_down': nrm((L, D_FF, D_MODEL), D_FF ** -0.5),
    }

def second_block(x, mem, g_mix, w_in, b_nsa_gate, g_q, g_kc, g_ks, g_kw, pe_k, pe_v,
              w_ck1, w_ck2, w_cv1, w_cv2, g_nsa_out, w_gk2, b_gk, g_gla_out, w_out,
              g_cross, g_mem, w_cq, w_ck, w_cv, g_cq, g_ck, w_co, g_ffn, w_gu, w_down):
    for l in range(DEPTH):
        x = hybrid_layer_2(x, mem, g_mix[l], w_in[l], b_nsa_gate[l], g_q[l], g_kc[l], g_ks[l],
                         g_kw[l], pe_k[l], pe_v[l], w_ck1[l], w_ck2[l], w_cv1[l], w_cv2[l],
                         g_nsa_out[l], w_gk2[l], b_gk[l], g_gla_out[l], w_out[l],
                         g_cross[l], g_mem[l], w_cq[l], w_ck[l], w_cv[l], g_cq[l], g_ck[l],
                         w_co[l], g_ffn[l], w_gu[l], w_down[l])
    return x


def setup_inputs(seed=0):
    out = dict(first_inputs(seed))
    for name, value in second_inputs(seed + 1).items():
        if name != "x":
            out[name + "_2"] = value
    return out


def reference(
    x, w_in, b_in, conv_w, conv_b, conv_ln_g, conv_ln_b, sinks, w_out, b_out, ln_g, ln_b, mem_2,
    g_mix_2, w_in_2, b_nsa_gate_2, g_q_2, g_kc_2, g_ks_2, g_kw_2, pe_k_2, pe_v_2, w_ck1_2,
    w_ck2_2, w_cv1_2, w_cv2_2, g_nsa_out_2, w_gk2_2, b_gk_2, g_gla_out_2, w_out_2, g_cross_2,
    g_mem_2, w_cq_2, w_ck_2, w_cv_2, g_cq_2, g_ck_2, w_co_2, g_ffn_2, w_gu_2, w_down_2,
):
    x = first_block(
        x, w_in, b_in, conv_w, conv_b, conv_ln_g, conv_ln_b, sinks, w_out, b_out, ln_g, ln_b,
    )
    return second_block(
        x, mem_2, g_mix_2, w_in_2, b_nsa_gate_2, g_q_2, g_kc_2, g_ks_2, g_kw_2, pe_k_2, pe_v_2,
        w_ck1_2, w_ck2_2, w_cv1_2, w_cv2_2, g_nsa_out_2, w_gk2_2, b_gk_2, g_gla_out_2, w_out_2,
        g_cross_2, g_mem_2, w_cq_2, w_ck_2, w_cv_2, g_cq_2, g_ck_2, w_co_2, g_ffn_2, w_gu_2,
        w_down_2,
    )


_drawn_inputs = setup_inputs


def setup_inputs(seed=0):
    import zlib

    import numpy as np

    out = dict(_drawn_inputs(seed))
    spreads = {}
    factors = {'b_in': 7.48,
     'conv_b': 6.968,
     'conv_ln_g': 2.712,
     'conv_ln_b': 8.0,
     'sinks': 8.0,
     'g_q_2': 2.92,
     'g_kc_2': 7.798,
     'g_ks_2': 5.559,
     'g_kw_2': 5.297,
     'b_gk_2': 3.714,
     'g_gla_out_2': 3.132,
     'g_cross_2': 8.0,
     'g_mem_2': 8.0,
     'g_cq_2': 8.0,
     'g_ck_2': 8.0,
     'g_ffn_2': 8.0}
    for name, (base, spread) in spreads.items():
        noise = np.random.default_rng([zlib.crc32(name.encode()), seed]).standard_normal(out[name].shape)
        drawn = base * np.exp(spread * noise) if base else spread * noise
        out[name] = jnp.asarray(drawn.astype(out[name].dtype))
    for name, factor in factors.items():
        out[name] = (out[name] * factor).astype(out[name].dtype)
    return out
```

```python
from contextlib import ExitStack

import concourse.bass as bass
from concourse import mybir

P = 128
ALU = mybir.AluOpType
ACT = mybir.ActivationFunctionType
F32 = mybir.dt.float32
F32R = mybir.dt.float32r
I32 = mybir.dt.int32
U8 = mybir.dt.uint8
AX_X = mybir.AxisListType.X

T = 256
TT = T // P
D = 2048
KT = D // P
NG = 512
STEP = 2
CHUNK = 4
LEAD = 3
NSLOT = 4
NRAW = 4

C = 1024
TAPS = 31
HEADS = 16
HD = 64
KVH = 2
ALPHA = 2.0 ** 0.25
LN_EPS = 1e-5
NEG = -1e30
EPS = 1e-6
QH = 8
DK = 128
NCMP = (T - 32) // 16 + 1
CMP_LEN = 32
GH = 4
DV = 256
MH = 4
FF = 5632
LEVELS = 7

KIB = 1024


def stack_kernel(nc, a, out, stop=None, dbg=None):
    w_in, w_out, w_in2, w_out2 = a["w_in"][0], a["w_out"][0], a["w_in_2"][0], a["w_out_2"][0]

    groups = []

    def group(name, w, col, n, kt=KT, k0=0):
        groups.append(dict(name=name, w=w, col=col, n=n, kt=kt, k0=k0))

    for name, col, n in (("cv0", 0, 512), ("cg0", C, 512), ("cv1", 512, 512), ("cg1", C + 512, 512),
                         ("q0", 3 * C, 512), ("q1", 3 * C + 512, 512), ("kv", 4 * C, 256),
                         ("ga0", 2 * C, 512), ("ga1", 2 * C + 512, 512),
                         ("ag0", 4 * C + 256, 512), ("ag1", 4 * C + 768, 512)):
        group(name, w_in, col, n)
    for j in range(4):
        group(f"wo{j}", w_out, NG * j, NG)
    for name, col, n in (("nq0", 0, 512), ("nq1", 512, 512), ("ncmp", 1024, 512), ("nslc", 1536, 512),
                         ("nwin", 2048, 512), ("glq0", 2560, 280), ("lq1", 2840, 256),
                         ("lar0", 4632, 272), ("lk", 3096, 512), ("lv0", 3608, 512), ("lv1", 4120, 512),
                         ("lr1", 4904, 512), ("lr2", 5416, 256)):
        group(name, w_in2, col, n)
    for j in range(4):
        group(f"w2o{j}", w_out2, NG * j, NG)
    group("mk", a["w_ck_2"][0], 0, NG)
    group("mq", a["w_cq_2"][0], 0, NG)
    group("mv", a["w_cv_2"][0], 0, NG)
    for j in range(4):
        group(f"co{j}", a["w_co_2"][0], NG * j, NG, kt=4)
    PARTS = ((0, 6), (6, 5))
    for part, (g0, n) in enumerate(PARTS):
        for j in range(g0, g0 + n):
            group(f"fg{j}", a["w_gu_2"][0], NG * j, NG)
            group(f"fu{j}", a["w_gu_2"][0], FF + NG * j, NG)
        for j in range(4):
            group(f"fd{part}{j}", a["w_down_2"][0], NG * j, NG, kt=4 * n, k0=4 * g0)
    at_step = 0
    for i, g in enumerate(groups):
        g["i"], g["s0"], g["ns"] = i, at_step, g["kt"] // STEP
        at_step += g["ns"]
    G = {g["name"]: g for g in groups}
    chunks = []
    for g in groups:
        for c in range(g["kt"] // CHUNK):
            src = g["w"].rearrange("(k p) n -> p k n", p=P)[
                :, g["k0"] + CHUNK * c:g["k0"] + CHUNK * (c + 1), g["col"]:g["col"] + g["n"]]
            chunks.append(dict(src=src, n=g["n"], k=CHUNK, step=g["s0"] + 2 * c, group=g))
            g.setdefault("c0", len(chunks) - 1)
        if g["name"] == "nslc":
            for w in ("w_ck1_2", "w_cv1_2"):
                for c in range(4):
                    src = a[w][0].rearrange("(k p) n -> p k n", p=P)[:, 8 * c:8 * c + 8, :]
                    chunks.append(dict(src=src, n=256, k=8, step=None, direct=len([0 for x in chunks if x["step"] is None]), group=None))
    direct_chunks = [i for i, c in enumerate(chunks) if c["step"] is None]
    chunk_of_step = {}
    for i, c in enumerate(chunks):
        if c["step"] is not None:
            chunk_of_step[c["step"]] = chunk_of_step[c["step"] + 1] = i
    n_steps = at_step
    step_cols = [g["n"] for g in groups for _ in range(g["ns"])]
    if stop:
        stop_group = G[stop[1]]
        n_steps = stop_group["s0"] + stop_group["ns"]
        chunks = [c for c in chunks if c["step"] is not None and c["step"] < n_steps or
                  c["step"] is None and stop_group["i"] > G["nslc"]["i"]]

    with ExitStack() as ctx:
        def sem(name):
            return ctx.enter_context(nc.semaphore(name))

        def place(name, kib, shape, dt=F32):
            return nc.alloc_sbuf_tensor_at(name, shape, dt, offset=int(kib * KIB))

        BASE = -(-nc.sbuf_base // 64) * 64
        ctx.enter_context(nc.sbuf_tensor("fence", [P, (nc.sbuf_usable_end - BASE) // 4 - 16], F32))
        at0 = BASE / KIB

        def put(name, kib, shape, dt=F32):
            return place(name, at0 + kib, shape, dt)

        raw = put("raw", 0, [P, NRAW, CHUNK * NG])
        hi = put("hi", 32, [P, NSLOT, STEP * NG], F32R)
        lo = put("lo", 48, [P, NSLOT, STEP * NG], F32R)
        x = put("x", 64, [P, TT, D])
        aH = put("aH", 80, [P, KT, T], F32R)
        aL = put("aL", 96, [P, KT, T], F32R)

        small, small_at = [168 * KIB], {}

        def const(name, shape, dt=F32):
            n = 1
            for s in shape[1:]:
                n *= s
            off = small[0]
            small_at[name] = off / KIB
            small[0] += -(-n * (1 if dt == U8 else 4) // 32) * 32
            return put(name, off / KIB, shape, dt)

        ident = const("ident", [P, P])
        ones = const("ones", [P, T])
        NCOL = 101
        cols = const("cols", [P, 165])
        convw = const("convw", [P, 8, 32])
        sinks = const("sinks", [P, HEADS])
        bias = const("bias", [P, 2, NG])
        mask1 = const("mask1", [P, 3 * P])
        dist2 = const("dist2", [P, 3 * P])
        distc = const("distc", [P, TT, 16])
        visc = const("visc", [P, TT])
        lmask = const("lmask", [P, LEVELS + 1, P], U8)
        bgate = const("bgate", [P, 24])
        stat = const("stat", [P, 64])
        bnst = const("bnst", [P, TT, 4, 6])
        mv = const("mv", [P, TT, 2])
        assert small[0] <= nc.sbuf_usable_end - BASE, (small[0], nc.sbuf_usable_end - BASE)

        ps_g = [[ctx.enter_context(nc.psum_tensor(f"ps_g{p}{t}", [P, NG], F32)) for t in range(TT)]
                for p in range(2)]
        ps_m = [ctx.enter_context(nc.psum_tensor(f"ps_m{i}", [P, NG], F32)) for i in range(4)]

        s_raw = [sem(f"raw_landed{i}") for i in range(NRAW)]
        s_hi = sem("hi_ready")
        s_lo = sem("lo_ready")
        s_used = sem("steps_multiplied")
        s_direct = sem("direct_chunks_multiplied")
        s_free = [sem(f"pair{p}_evacuated") for p in range(2)]

        s_x = sem("x_landed")
        s_par = sem("params_landed")
        s_bias = [sem(f"bias_landed{i}") for i in range(2)]
        s_pool = sem("pool_steps")
        s_xt = sem("transposed")
        s_xh = sem("operand_hi")
        s_xl = sem("operand_lo")
        s_dve = sem("dve_steps")
        s_act = sem("act_steps")

        block = ctx.enter_context(nc.Block())

        def wait_raw(e, chunk):
            e.wait_ge(s_raw[chunk % NRAW], 16 * (chunk // NRAW + 1))

        def step_view(buf, s):
            n = step_cols[s]
            return buf[:, s % NSLOT, :STEP * n]

        def raw_view(s):
            c, n = chunk_of_step[s], step_cols[s]
            half = (s - chunks[c]["step"]) * STEP * n
            return raw[:, c % NRAW, half:half + STEP * n]

        def pair_of(g):
            return g["i"] % 2

        def evacuated(e, g):
            e.wait_ge(s_free[pair_of(g)], TT * (g["i"] // 2 + 1))

        def psum_ready(e, g):
            e.wait_ge(s_used, g["s0"] + g["ns"])

        builds = {}
        unit_at = 0
        for name, n in (("x", 8), ("yattn", 4), ("h", 8), ("y2", 16 // 2), ("mem", 8), ("hq", 8), ("oc", 2), ("hf", 8)):
            builds[name] = (unit_at, n)
            unit_at += n
        for j in range(FF // NG):
            builds[f"gu{j}"] = (unit_at, 2)
            unit_at += 2

        def build_pe(pe, name, src, before=None, only=None):
            u0, n = builds[name]
            for u in (range(n) if only is None else only):
                if u0 + u >= 4:
                    pe.wait_ge(s_xl, u0 + u - 3)
                    if before is not None:
                        before(u)
                elif before is not None:
                    before(u)
                for k in range(2):
                    for t in range(TT):
                        last = pe.transpose(ps_m[(u0 + u) % 4][:, (2 * k + t) * P:(2 * k + t + 1) * P],
                                            src(2 * u + k, t), ident[:])
                last.then_inc(s_xt, 1)

        def build_act(act, name, dst, gain=None, before=None, only=None):
            u0, n = builds[name]
            for u in (range(n) if only is None else only):
                act.wait_ge(s_xt, u0 + u + 1)
                if before is not None:
                    before(u)
                bank = ps_m[(u0 + u) % 4]
                if gain is None:
                    act.copy(dst(2 * u, 2).rearrange("p k t -> p (k t)"), bank[:]).then_inc(s_xh, 1)
                else:
                    for k in range(2):
                        last = act.activation(dst(2 * u + k, 1).rearrange("p k t -> p (k t)"), bank[:, k * T:(k + 1) * T], ACT.Copy,
                                              scale=gain(2 * u + k))
                    last.then_inc(s_xh, 1)

        def build_dve(dve, name, dst_hi, dst_lo, gain=None, only=None):
            u0, n = builds[name]
            for u in (range(n) if only is None else only):
                dve.wait_ge(s_xh, u0 + u + 1)
                bank = ps_m[(u0 + u) % 4]
                if gain is None:
                    dve.tensor_tensor(dst_lo(2 * u, 2).rearrange("p k t -> p (k t)"), bank[:],
                                      dst_hi(2 * u, 2).rearrange("p k t -> p (k t)").bitcast(F32),
                                      ALU.subtract).then_inc(s_xl, 1)
                else:
                    for k in range(2):
                        last = dve.scalar_tensor_tensor(
                            out=dst_lo(2 * u + k, 1).rearrange("p k t -> p (k t)"), in0=bank[:, k * T:(k + 1) * T],
                            scalar=gain(2 * u + k), in1=dst_hi(2 * u + k, 1).rearrange("p k t -> p (k t)").bitcast(F32),
                            op0=ALU.mult, op1=ALU.subtract)
                    last.then_inc(s_xl, 1)

        def built(name, k_tiles_done):
            return builds[name][0] + k_tiles_done // 2

        def A(buf, k0=0):
            return lambda k, n: buf[:, k0 + k:k0 + k + n, :]

        def gemm(pe, g, j, opH, opL, before=None):
            s = g["s0"] + j
            if j == 0 and g["i"] >= 2:
                pe.wait_ge(s_free[pair_of(g)], TT * (g["i"] // 2))
            if before is not None:
                before(j)
            pe.wait_ge(s_hi, s + 1)
            pe.wait_ge(s_lo, s + 1)
            n = g["n"]
            for k in range(STEP):
                wh = step_view(hi, s)[:, k * n:(k + 1) * n]
                wl = step_view(lo, s)[:, k * n:(k + 1) * n]
                kk = STEP * j + k
                first, final = kk == 0, kk == g["kt"] - 1
                for t in range(TT):
                    dst = ps_g[pair_of(g)][t][:, :n]
                    xh = opH(kk, 1)[:, 0, t * P:(t + 1) * P]
                    xl = opL(kk, 1)[:, 0, t * P:(t + 1) * P]
                    pe.matmul(dst, xh, wh, start=first, stop=False)
                    pe.matmul(dst, xh, wl, start=False, stop=False)
                    last = pe.matmul(dst, xl, wh, start=False, stop=final)
            last.then_inc(s_used, 1)

        def split_hi(act, s):
            if s >= n_steps:
                return
            wait_raw(act, chunk_of_step[s])
            if s >= NSLOT:
                act.wait_ge(s_used, s - NSLOT + 1)
            act.copy(step_view(hi, s), raw_view(s)).then_inc(s_hi, 1)

        def split_lo(pool, s):
            pool.wait_ge(s_hi, s + 1)
            if s >= NSLOT:
                pool.wait_ge(s_used, s - NSLOT + 1)
            pool.tensor_tensor(step_view(lo, s), raw_view(s), step_view(hi, s).bitcast(F32),
                               ALU.subtract).then_inc(s_lo, 1)

        bias_groups = ["cv0", "cg0", "cv1", "cg1", "q0", "q1", "kv", "ga0", "ga1", "ag0", "ag1",
                       "wo0", "wo1", "wo2", "wo3"]
        bias_used = sem("output_bias_added")

        def bias_slot(e, name):
            i = bias_groups.index(name)
            e.wait_ge(s_bias[i % 2], 16 * (i // 2 + 1))
            return bias[:, i % 2, :G[name]["n"]]

        q_sb = put("q_sb", 112, [P, TT, C])
        qT = put("qT", 120, [P, 8, T])
        c_h = put("c_h", 128, [P, TT, C])
        gT = put("gT", 128, [P, 8, T])
        hT = put("hT", 136, [P, 8, T + TAPS - 1])
        cT = put("cT", 145.25, [P, 8, T])
        stg = put("stg", 153.25, [P, TT, NG])
        kT = put("kT", 157.25, [P, KVH, T])
        v_sb = put("v_sb", 159.25, [P, TT, P])
        sS = put("sS", 160.25, [P, 2, 3 * P])
        pT = put("pT", 163.25, [P, 2, 3 * P])
        k_dup = put("k_dup", 163.25, [P, TT, KVH, 2, HD])
        mx = put("mx", 166.25, [P, HEADS, 2])
        den = put("den", 166.375, [P, HEADS, 2])
        esk = put("esk", 166.5, [P, HEADS, 2])
        rden = put("rden", 166.625, [P, HEADS, 2])
        mean_sb = put("mean_sb", 166.75, [P, T])
        rstd_sb = put("rstd_sb", 144, [P, T])
        sq_sb = put("sq_sb", 136, [P, 8, T])
        param_rows = put("param_rows", 112, [P, P])
        pe_rows = put("pe_rows", 112.5, [64, P])
        cw_rows = put("cw_rows", 113, [TAPS, C])

        CB, CLG, CLB, GM, GC, GME, GF, BGK, GQ, GKC, GKS, GKW, GCQ, GCK = (
            0, 8, 16, 24, 40, 56, 72, 88, 92, 93, 94, 95, 96, 97)
        GNS, GGL = 98, 99
        PEK, PEV = 101, 133
        row_loads = [("conv_b", CB, 8), ("conv_ln_g", CLG, 8), ("conv_ln_b", CLB, 8), ("g_mix_2", GM, 16),
                     ("g_cross_2", GC, 16), ("g_mem_2", GME, 16), ("g_ffn_2", GF, 16), ("b_gk_2", BGK, 4),
                     ("g_q_2", GQ, 1), ("g_kc_2", GKC, 1), ("g_ks_2", GKS, 1), ("g_kw_2", GKW, 1),
                     ("g_cq_2", GCQ, 1), ("g_ck_2", GCK, 1), ("g_nsa_out_2", GNS, 1), ("g_gla_out_2", GGL, 2)]
        N_PAR = 16 * (len(row_loads) + 2 + 1 + 1 + 1 + 2)

        s_cols = sem("param_columns_in_psum")
        s_colsb = sem("param_columns_ready")
        s_stga = sem("staged_through_act")
        s_ch = sem("conv_input_ready")
        s_cht = sem("conv_input_transposed")
        s_hT = sem("conv_input_T_ready")
        s_conv = sem("conv_taps")
        s_qt = sem("qk_transposed")
        s_qT = sem("qk_T_ready")
        s_sc = sem("scores")
        s_sm = sem("scores_shifted")
        s_exp = sem("exp_done")
        s_pt = sem("probs_transposed")
        s_pTc = sem("probs_T_ready")
        s_pv = sem("pv_done")
        s_yn = sem("pv_normalized")
        s_yat = sem("attn_gated")
        s_gat = sem("gate_transposed")
        s_gT = sem("gate_T_ready")
        s_lns = sem("conv_ln_sums")
        s_lnc = sem("conv_ln_steps")
        s_lna = sem("conv_ln_act")
        s_ych = sem("y_conv_hi")
        s_ycl = sem("y_conv_lo")
        s_x1 = sem("x_updated")
        s_out = sem("out_stored")

        ln_rows = put("ln_rows", 190, [P, 2, D])

        yn = put("yn", 112, [P, TT, QH, DK])
        yg = put("yg", 120, [P, TT, GH, DV])
        pc = put("pc", 120, [P, TT, QH, 32])
        pTc = put("pTc", 122, [P, TT, KVH, P])
        hid = put("hid", 124, [2 * NCMP, 512])
        kcn = put("kcn", 126, [2 * NCMP, DK])
        kcT15 = put("kcT15", 126.5, [P, 2 * NCMP])
        aT = put("aT", 127, [16, T])
        nqT = put("nqT", 128, [P, QH, T])
        ksT = put("ksT", 136, [P, KVH, T])
        kwT = put("kwT", 138, [P, KVH, T])
        vs = put("vs", 140, [P, TT, KVH * DK])
        vw = put("vw", 142, [P, TT, KVH * DK])
        kcT = put("kcT", 144, [P, KVH, T])
        vcT = put("vcT", 146, [P, KVH, T])
        kp = put("kp", 148, [P, 2, 32, KVH, NCMP])
        qlT = put("qlT", 156, [P, GH, T])
        klT = put("klT", 160, [P, GH, T])
        vc_bd = put("vc_bd", 160, [P, KVH, 4, DK])
        hidTk = put("hidTk", 164, [P, 2, 32])
        hidTv = put("hidTv", 165, [P, 2, KVH, 4, 32])
        gb = put("gb", 164, [P, GH, T])
        nq = put("nq", 181.75, [P, TT, QH, DK])
        rl = put("rl", 181.75, [P, TT, 1024])
        vl = put("vl", 189.75, [P, TT, GH, DV])
        sS2 = put("sS2", 197.75, [P, 2, 3 * P])
        pT2 = put("pT2", 200.75, [P, 2, 3 * P])
        sT = put("sT", 197.75, [P, 3, GH, P])
        stg2 = put("stg2", 203.75, [P, TT, NG])
        E = [put(f"E{i}", 128 + 4 * i, [P, GH * T]) for i in range(2)]
        QK = [put(f"QK{i}", 148 + 4 * i, [P, GH * T]) for i in range(2)]
        off_bias = small_at["bias"]
        w_gk2 = put("w_gk2", off_bias, [16, 512])
        w_c2 = put("w_c2", off_bias + 2, [P, 2, 2, DK])
        gates = const("gates", [P, TT, 24])
        st2 = const("st2", [P, 160])

        HIDTV_CLEARED = 1
        gz = put("gz", 144, [P, GH * T])
        sq_row = put("sq_row", 181.75, [P, D])
        sq_c = put("sq_c", 127, [2 * NCMP, DK])
        sc8 = put("sc8", 128, [P, TT, GH, DV])
        mx2, den2 = st2[:, 0:32].rearrange("p (u t) -> p u t", t=2), st2[:, 32:64].rearrange("p (u t) -> p u t", t=2)
        rden2 = st2[:, 64:96].rearrange("p (u t) -> p u t", t=2)
        ss_n = st2[:, 96:112]
        mxc = st2[:, 112:128]
        rc = st2[:, 128:144]
        denc = st2[:, 144:160]
        var_ln = stat[:, 0:2]
        ss = stat[:, 2:4]
        ss_q = stat[:, 4:20].rearrange("p (a b) -> p a b", a=2)
        ss_k = stat[:, 20:28].rearrange("p (a b) -> p a b", a=2)
        ss_c = stat[0:2 * NCMP, 28:29]
        ss_g = stat[:, 29:37]
        colq = stat[:, 37:38]
        mean_ln = stat[:, 38:40]

        memn = put("memn", 128, [P, TT, D])
        mH = put("mH", 144, [P, KT, T], F32R)
        mL = put("mL", 181.75, [P, KT, T], F32R)
        sq_m = put("sq_m", 112, [P, D])
        ckn = put("ckn", 197.75, [P, TT, MH, DK])
        cvn = put("cvn", 201.75, [P, TT, MH * DK])
        cqn = put("cqn", 112, [P, TT, MH, DK])
        scr4 = put("scr4", 116, [P, TT, MH, DK])
        ocn = put("ocn", 116, [P, TT, MH, DK])
        ckT = put("ckT", 120, [P, MH, T])
        cqT = put("cqT", 124, [P, MH, T])
        sS3 = put("sS3", 128, [P, MH, TT, T])
        pT3 = put("pT3", 136, [P, MH, TT, TT, P])
        ocH = put("ocH", 144, [P, 4, T], F32R)
        ocL = put("ocL", 148, [P, 4, T], F32R)
        guH = put("guH", 112, [P, 24, T], F32R)
        guL = put("guL", 136, [P, 24, T], F32R)
        sg = put("sg", 160, [P, TT, NG])
        hn = put("hn", 164, [P, TT, NG])
        st3 = stat[:, 40:64]
        ss_m, ss_x2, ss_x3, colcq = st3[:, 0:2], st3[:, 2:4], st3[:, 4:6], st3[:, 6:7]
        ss_ck, ss_cq = st3[:, 8:16], st3[:, 16:24]
        mx3, den3 = st2[:, 0:8].rearrange("p (u t) -> p u t", t=2), st2[:, 8:16].rearrange("p (u t) -> p u t", t=2)
        s_ckr = sem("cross_rows_ready")
        s_sc3 = sem("cross_scores")
        s_sm3 = sem("cross_maxima")
        s_exp3 = sem("cross_exp")
        s_pt3 = sem("cross_probs_transposed")
        s_pTc3 = sem("cross_probs_T_ready")
        s_pv3 = sem("cross_pv")
        s_on = sem("cross_normalized")
        s_sqs = sem("squares_scratch")
        s_ffs = sem("ffn_scale_ready")
        sq_f = put("sq_f", 136, [P, D])

        s_var = sem("variances")
        s_sqrt = sem("square_roots")
        s_ss = sem("row_squares_summed")
        s_p2 = sem("layer_two_small_weights_landed")
        s_t2 = sem("bank0_written")
        s_t2c = sem("bank0_copied")
        s_t2s = sem("bank0_source_ready")
        s_kp = sem("compress_operands")
        s_hid = sem("compress_hidden")
        s_c2 = sem("compressed_in_psum")
        s_c2v = sem("compressed_values_ready")
        s_csc = sem("cmp_scores")
        s_csm = sem("cmp_scores_shifted")
        s_cexp = sem("cmp_exp")
        s_cpv = sem("cmp_pv")
        s_cyn = sem("cmp_normalized")
        s_gsig = sem("gates_ready")
        s_sc2 = sem("scores2")
        s_sm2 = sem("scores2_shifted")
        s_exp2 = sem("exp2_done")
        s_pt2 = sem("probs2_transposed")
        s_pTc2 = sem("probs2_T_ready")
        s_pv2 = sem("pv2_done")
        s_yn2 = sem("pv2_normalized")
        s_z = sem("gate_z_parts")
        s_la = sem("log_decay")
        s_gE = sem("level_exponents")
        s_gX = sem("level_decays")
        s_gQ = sem("level_operands")
        s_gP = sem("level_products")
        s_gS = sem("level_scores_taken")
        s_go = sem("gla_out")
        s_goc = sem("gla_out_copied")
        s_y2n = sem("nsa_rows_ready")
        s_y2g = sem("gla_rows_ready")
        s_rl = sem("gla_gate_ready")
        s_mem = sem("mem_landed")

        conv_units = 8 * TAPS
        LNC_READ_SUMS = 3
        n_dve = [0]

        @block.sync
        def _(sp):
            sp.dma_start(x[:, 0, :], a["x"][0, 0:P, :]).then_inc(s_x, 16)
            sp.dma_start(x[:, 1, :], a["x"][0, P:T, :]).then_inc(s_x, 16)
            for name, r0, n in row_loads:
                sp.dma_start(param_rows[r0:r0 + n, :], a[name][0].rearrange("(r c) -> r c", c=P)).then_inc(s_par, 16)
            sp.dma_start(pe_rows[0:32, :], a["pe_k_2"][0]).then_inc(s_par, 16)
            sp.dma_start(pe_rows[32:64, :], a["pe_v_2"][0]).then_inc(s_par, 16)
            sp.dma_start(cw_rows[:, :], a["conv_w"][0]).then_inc(s_par, 16)
            sp.dma_start(sinks[:], a["sinks"][0].partition_broadcast(P)).then_inc(s_par, 16)
            sp.dma_start(ln_rows[:, 0, :], a["ln_g"][0].partition_broadcast(P)).then_inc(s_par, 16)
            sp.dma_start(ln_rows[:, 1, :], a["ln_b"][0].partition_broadcast(P)).then_inc(s_par, 16)
            sp.dma_start(bgate[:], a["b_nsa_gate_2"][0].partition_broadcast(P)).then_inc(s_par, 16)
            for c, ch in enumerate(chunks):
                g = ch["group"]
                if g is not None and g["name"] == "w2o2" and c == g["c0"]:
                    sp.wait_ge(s_xl, built("y2", KT))
                    sp.dma_start(memn[:], a["mem_2"][0].rearrange("(t p) d -> p t d", p=P)).then_inc(s_mem, 16)
                if g is not None and g["name"] == "nq0" and c == g["c0"]:
                    sp.wait_ge(bias_used, 4)
                    sp.dma_start(w_gk2[:], a["w_gk2_2"][0]).then_inc(s_p2, 16)
                    for i, w in enumerate(("w_ck2_2", "w_cv2_2")):
                        sp.dma_start(w_c2[:, i], a[w][0].rearrange("(k p) n -> p k n", p=P)).then_inc(s_p2, 16)
                if g is not None and g["name"] in bias_groups and c == g["c0"]:
                    i = bias_groups.index(g["name"])
                    if i >= 2 and i < 13:
                        evacuated(sp, G[bias_groups[i - 2]])
                    if i >= 13:
                        sp.wait_ge(bias_used, i - 12)
                    b = a["b_in"][0] if g["w"] is w_in else a["b_out"][0]
                    sp.dma_start(bias[:, i % 2, :g["n"]], b[g["col"]:g["col"] + g["n"]].partition_broadcast(P)
                                 ).then_inc(s_bias[i % 2], 16)
                if c >= NRAW:
                    old = chunks[c - NRAW]
                    if old["step"] is None:
                        sp.wait_ge(s_direct, old["direct"] + 1)
                    else:
                        sp.wait_ge(s_lo, old["step"] + 2)
                sp.dma_start(raw[:, c % NRAW, :ch["k"] * ch["n"]].rearrange("p (k n) -> p k n", k=ch["k"]),
                             ch["src"]).then_inc(s_raw[c % NRAW], 16)
            if not stop:
                for j in range(4):
                    evacuated(sp, G[f"fd1{j}"])
                    sp.dma_start(out[0].rearrange("(t p) d -> p t d", p=P)[:, :, j * NG:(j + 1) * NG],
                                 x[:, :, j * NG:(j + 1) * NG]).then_inc(s_out, 16)
                sp.wait_ge(s_out, 64)
            if stop:
                if stop[0] == "one":
                    sp.wait_ge(s_x1, stop[2])
                else:
                    evacuated(sp, G[stop[1]])
                    evacuated(sp, groups[G[stop[1]]["i"] - 1])
                sp.dma_start(out.rearrange("a (t p) d -> p (a t) d", p=P), x[:]).then_inc(s_out, 16)
                sp.wait_ge(s_out, 16)

        iot = put("iot", 120, [P, 2, P], I32)
        xorf = put("xorf", 121, [P, P])
        ge = put("ge", 121.5, [P, LEVELS + 1, P])
        tri = put("tri", 125.5, [P, P])
        n_pool = 0

        @block.gpsimd
        def _(pool):
            k = [0]

            def own(ins):
                k[0] += 1
                ins.then_inc(s_pool, 1)
                pool.wait_ge(s_pool, k[0])

            own(pool.memset(ident[:], 0.0))
            own(pool.affine_select(out=ident[:], in_=ident[:], compare_op=ALU.not_equal, fill=1.0, base=0,
                                   pattern=[[-1, P]], channel_multiplier=1))
            pool.memset(ones[:], 1.0)
            pool.memset(hT[:, :, 0:TAPS - 1], 0.0)
            own(pool.memset(mask1[:], 0.0))
            own(pool.affine_select(out=mask1[:, 0:P], in_=mask1[:, 0:P], compare_op=ALU.is_ge, fill=NEG, base=0,
                                   pattern=[[-1, P]], channel_multiplier=1))
            own(pool.affine_select(out=mask1[:, P:], in_=mask1[:, P:], compare_op=ALU.is_gt, fill=NEG, base=0,
                                   pattern=[[1, 2 * P]], channel_multiplier=-1))
            own(pool.affine_select(out=mask1[:, P:], in_=mask1[:, P:], compare_op=ALU.is_ge, fill=NEG, base=P,
                                   pattern=[[-1, 2 * P]], channel_multiplier=1))
            own(pool.iota(dist2[:, 0:P], [[1, P]], base=0, channel_multiplier=-1,
                          allow_small_or_imprecise_dtypes=True))
            own(pool.iota(dist2[:, P:], [[1, 2 * P]], base=-P, channel_multiplier=-1,
                          allow_small_or_imprecise_dtypes=True))
            own(pool.affine_select(out=dist2[:, 0:P], in_=dist2[:, 0:P], compare_op=ALU.is_ge, fill=-1e33, base=0,
                                   pattern=[[-1, P]], channel_multiplier=1))
            own(pool.affine_select(out=dist2[:, P:], in_=dist2[:, P:], compare_op=ALU.is_ge, fill=-1e33, base=P,
                                   pattern=[[-1, 2 * P]], channel_multiplier=1))
            pool.iota(iot[:, 0, :], [[1, P]], base=0, channel_multiplier=0)
            own(pool.iota(iot[:, 1, :], [[0, P]], base=0, channel_multiplier=1))
            own(pool.iota(distc[:], [[-P, TT], [16, 16]], base=0, channel_multiplier=-1,
                          allow_small_or_imprecise_dtypes=True))
            own(pool.tensor_scalar(distc[:], distc[:], 15.5, 1.0, ALU.add, ALU.mult))
            own(pool.affine_select(out=distc[:], in_=distc[:], compare_op=ALU.is_ge, fill=-1e33, base=-31,
                                   pattern=[[P, TT], [-16, 16]], channel_multiplier=1))
            own(pool.memset(visc[:], 1.0))
            own(pool.affine_select(out=visc[:], in_=visc[:], compare_op=ALU.is_ge, fill=0.0, base=-31,
                                   pattern=[[P, TT]], channel_multiplier=1))
            own(pool.memset(tri[:], 1.0))
            own(pool.affine_select(out=tri[:], in_=tri[:], compare_op=ALU.is_gt, fill=0.0, base=0,
                                   pattern=[[1, P]], channel_multiplier=-1))
            for s in range(n_steps):
                split_lo(pool, s)

        POOL_CONSTS = 18

        ga = G["ga0"]["s0"]
        score_slot = {2 + 7 * u // 4: u for u in range(HEADS)}

        @block.tensor
        def _(pe):
            pe.wait_ge(s_pool, 2)
            pe.wait_ge(s_par, N_PAR)
            pe.transpose(ps_m[2][:, 0:NCOL], param_rows[0:NCOL, :], ident[0:NCOL, 0:NCOL])
            pe.transpose(ps_m[2][:, NCOL:165], pe_rows[:, :], ident[0:64, 0:64]).then_inc(s_cols, 1)
            for c in range(8):
                last = pe.transpose(ps_m[3][:, 32 * c:32 * c + TAPS], cw_rows[:, c * P:(c + 1) * P],
                                    ident[0:TAPS, 0:TAPS])
            last.then_inc(s_cols, 1)
            pe.wait_ge(s_x, 32)

            def before_x(u):
                if u == 2:
                    pe.wait_ge(s_colsb, 2)
            build_pe(pe, "x", lambda k, t: x[:, t, k * P:(k + 1) * P], before_x)

            def conv_in_T(j):
                pe.wait_ge(s_ch, j + 1)
                for c in range(4):
                    if c % 2 == 0 and j == 1:
                        pe.wait_ge(s_hT, c // 2 + 1)
                    for t in range(TT):
                        last = pe.transpose(ps_m[c // 2][:, (c % 2) * T + t * P:(c % 2) * T + (t + 1) * P],
                                            c_h[:, t, (4 * j + c) * P:(4 * j + c + 1) * P], ident[:])
                    if c % 2:
                        last.then_inc(s_cht, 1)

            def q_T(j):
                evacuated(pe, G[("q0", "q1")[j]])
                for c in range(4):
                    if c % 2 == 0 and j == 1:
                        pe.wait_ge(s_qT, c // 2 + 1)
                    for t in range(TT):
                        last = pe.transpose(ps_m[2 + c // 2][:, (c % 2) * T + t * P:(c % 2) * T + (t + 1) * P],
                                            q_sb[:, t, (4 * j + c) * P:(4 * j + c + 1) * P], ident[:])
                    if c % 2:
                        last.then_inc(s_qt, 1)

            def k_T():
                evacuated(pe, G["kv"])
                pe.wait_ge(s_qT, 3)
                for h in range(KVH):
                    for t in range(TT):
                        last = pe.transpose(ps_m[2][:, h * T + t * P:h * T + (t + 1) * P],
                                            k_dup[:, t, h].rearrange("p a b -> p (a b)"), ident[:])
                last.then_inc(s_qt, 1)

            def scores(u):
                if u == 0:
                    pe.wait_ge(s_qT, 5)
                    pe.wait_ge(s_hT, 4)
                if u >= 1:
                    pe.wait_ge(s_sm, u)
                r = (u % 2) * HD
                k = u // (HEADS // KVH)
                pe.matmul(ps_m[0][:, 0:P], qT[r:r + HD, u // 2, 0:P], kT[r:r + HD, k, 0:P], start=True, stop=True)
                pe.matmul(ps_m[0][:, P:3 * P], qT[r:r + HD, u // 2, P:T], kT[r:r + HD, k, :],
                          start=True, stop=True).then_inc(s_sc, 1)

            def probs_T(u):
                pe.wait_ge(s_exp, u + 1)
                if u >= 1:
                    pe.wait_ge(s_pTc, u)
                for j in range(3):
                    last = pe.transpose(ps_m[2][:, j * P:(j + 1) * P], sS[:, u % 2, j * P:(j + 1) * P], ident[:])
                last.then_inc(s_pt, 1)

            def pv(u):
                pe.wait_ge(s_pTc, u + 1)
                if u == 0:
                    pe.wait_ge(s_qT, 4)
                if u >= 1:
                    pe.wait_ge(s_yn, u)
                k = u // (HEADS // KVH) * HD
                o = (u % 2) * 2 * HD
                pe.matmul(ps_m[3][:, o:o + HD], pT[:, u % 2, 0:P], v_sb[:, 0, k:k + HD], start=True, stop=True)
                pe.matmul(ps_m[3][:, o + HD:o + 2 * HD], pT[:, u % 2, P:2 * P], v_sb[:, 0, k:k + HD], start=True, stop=False)
                pe.matmul(ps_m[3][:, o + HD:o + 2 * HD], pT[:, u % 2, 2 * P:], v_sb[:, 1, k:k + HD],
                          start=False, stop=True).then_inc(s_pv, 1)

            def attn_slot(i):
                if i in score_slot:
                    scores(score_slot[i])
                if i - 2 in score_slot:
                    probs_T(score_slot[i - 2])
                if i - 4 in score_slot:
                    pv(score_slot[i - 4])

            def gate_T(c):
                if c == 0:
                    pe.wait_ge(s_lnc, LNC_READ_SUMS)
                if c % 4 == 0:
                    pe.wait_ge(s_stga, 3 + c // 4)
                if c >= 1:
                    pe.wait_ge(s_gT, c)
                for t in range(TT):
                    last = pe.transpose(ps_m[1][:, t * P:(t + 1) * P],
                                        stg[:, t, (c % 4) * P:(c % 4 + 1) * P], ident[:])
                last.then_inc(s_gat, 1)

            def channel_sum(i, src):
                if i == 0:
                    pe.wait_ge(s_conv, conv_units)
                else:
                    pe.wait_ge(s_lna, 1)
                for c in range(8):
                    last = pe.matmul(ps_m[1][:, 0:T], ones[:, 0:P], src[:, c, :], start=(c == 0), stop=(c == 7))
                last.then_inc(s_lns, 1)

            for g in groups[:11]:
                for j in range(g["ns"]):
                    gemm(pe, g, j, A(aH), A(aL),
                         (lambda j: pe.wait_ge(s_xl, built("x", 2 * j + 2))) if g["i"] == 0 else None)
                    if g["name"] == "cv1" and j == 2:
                        conv_in_T(0)
                    if g["name"] == "q0" and j == 2:
                        conv_in_T(1)
                    if g["name"] == "q1" and j == 1:
                        q_T(0)
                    if g["name"] == "kv" and j == 2:
                        q_T(1)
                    if g["name"] == "ga0" and j == 1:
                        k_T()
                    if (g["name"], j) == ("ga0", 4):
                        channel_sum(0, cT)
                    if (g["name"], j) == ("ga1", 0):
                        channel_sum(1, sq_sb)
                    if g["name"] == "ga1" and j in (4, 5, 6, 7):
                        gate_T(j - 4)
                    if g["name"] == "ag0" and j in (2, 3, 4, 5):
                        gate_T(4 + j - 2)
                    i = g["s0"] + j - ga
                    if i >= 2:
                        attn_slot(i)
            attn_slot(32)
            def before_y(u):
                if u == 0:
                    pe.wait_ge(s_yat, 2)
                    pe.wait_ge(s_yn, HEADS)
                    pe.wait_ge(s_lnc, LNC_READ_SUMS)
            build_pe(pe, "yattn", lambda k, t: q_sb[:, t, k * P:(k + 1) * P], before_y)

            def before_wo(g):
                def wait(j):
                    if g["name"] == "wo0":
                        if j == 0:
                            pe.wait_ge(s_ycl, 1)
                        if j >= 4:
                            pe.wait_ge(s_xl, built("yattn", 2 * (j - 4) + 2))
                return wait
            for g in groups[11:15]:
                for j in range(g["ns"]):
                    gemm(pe, g, j, A(aH), A(aL), before_wo(g))
            if stop and stop[0] == "one":
                return

            build_pe(pe, "h", lambda k, t: x[:, t, k * P:(k + 1) * P],
                     lambda u: pe.wait_ge(s_x1, u // 2 + 1))

            t2 = [0]

            def unit_begin(ready=None):
                if t2[0] >= 1:
                    pe.wait_ge(s_t2c, t2[0])
                if isinstance(ready, str):
                    evacuated(pe, G[ready])
                elif ready is not None:
                    pe.wait_ge(s_t2s, ready)

            def unit_end(last):
                last.then_inc(s_t2, 1)
                t2[0] += 1

            def rows_T(srcs, ready, rows=P, width=T):
                unit_begin(ready)
                for i, s in enumerate(srcs):
                    last = pe.transpose(ps_m[0][0:s.shape[1], i * P:i * P + s.shape[0]], s, ident[0:s.shape[0], 0:s.shape[0]])
                unit_end(last)

            def heads_T(buf, h, ready):
                rows_T([buf[:, t, hh * DK:(hh + 1) * DK] for hh in (h, h + 1) for t in range(TT)], ready)

            def nq_T(h):
                rows_T([nq[:, t, hh, :] for hh in (h, h + 1) for t in range(TT)], 1 + h // 4)

            def direct(i, w):
                if i == 0:
                    pe.wait_ge(s_xl, built("h", KT))
                pe.wait_ge(s_kp, i + 1)
                for c in range(4):
                    n = direct_chunks[4 * i + c]
                    wait_raw(pe, n)
                    for l in range(8):
                        last = pe.matmul(ps_m[3][0:2 * NCMP, i * T:(i + 1) * T],
                                         kp[:, i, 8 * c + l].rearrange("p k n -> p (k n)"),
                                         raw[:, n % NRAW, l * T:(l + 1) * T], start=(c == 0 and l == 0),
                                         stop=(c == 3 and l == 7))
                    last.then_inc(s_direct, 1)

            def hid_T(i):
                unit_begin()
                if i == 0:
                    pe.wait_ge(s_hid, 1)
                for hk in range(2):
                    last = pe.transpose(ps_m[0][:, hk * 32:hk * 32 + 2 * NCMP],
                                        hid[:, i * T + hk * P:i * T + (hk + 1) * P], ident[0:2 * NCMP, 0:2 * NCMP])
                unit_end(last)

            def compressed():
                pe.wait_ge(s_p2, 48)
                pe.wait_ge(s_t2c, t2[0])
                for hk in range(2):
                    pe.matmul(ps_m[1][0:2 * NCMP, 0:P], hidTk[:, hk, 0:2 * NCMP], w_c2[:, 0, hk, :],
                              start=(hk == 0), stop=(hk == 1))
                for kv in range(KVH):
                    for hk in range(2):
                        last = pe.matmul(ps_m[1][:, (1 + kv) * P:(2 + kv) * P],
                                         hidTv[:, hk, kv].rearrange("p r n -> p (r n)"), w_c2[:, 1, hk, :],
                                         start=(hk == 0), stop=(hk == 1))
                last.then_inc(s_c2, 1)

            def cmp_scores():
                for t in range(TT):
                    for h in range(QH):
                        kv = h // 4
                        last = pe.matmul(ps_m[2][:, (t * QH + h) * 16:(t * QH + h) * 16 + NCMP],
                                         nqT[:, h, t * P:(t + 1) * P], kcT15[:, kv * NCMP:(kv + 1) * NCMP],
                                         start=True, stop=True)
                last.then_inc(s_csc, 1)

            def cmp_pv(i):
                t, kv = i // KVH, i % KVH
                if i == 0:
                    pe.wait_ge(s_c2v, 2)
                    pe.wait_ge(s_t2c, t2[0])
                else:
                    pe.wait_ge(s_cyn, i)
                pe.matmul(ps_m[1][:], pTc[:, t, kv, :], vc_bd[:, kv].rearrange("p r d -> p (r d)"), start=True,
                          stop=True).then_inc(s_cpv, 1)

            def scores2(u):
                br, h = divmod(u, QH)
                kT_ = (ksT, kwT)[br]
                if u == 0:
                    pe.wait_ge(s_t2c, t2[0])
                    pe.wait_ge(s_csm, 1)
                else:
                    pe.wait_ge(s_sm2, u)
                pe.matmul(ps_m[2][:, 0:P], nqT[:, h, 0:P], kT_[:, h // 4, 0:P], start=True, stop=True)
                pe.matmul(ps_m[2][:, P:3 * P], nqT[:, h, P:T], kT_[:, h // 4, :], start=True, stop=True
                          ).then_inc(s_sc2, 1)

            def probs2_T(u):
                pe.wait_ge(s_exp2, u + 1)
                if u >= 1:
                    pe.wait_ge(s_pTc2, u)
                for j in range(3):
                    last = pe.transpose(ps_m[3][:, j * P:(j + 1) * P], sS2[:, u % 2, j * P:(j + 1) * P], ident[:])
                last.then_inc(s_pt2, 1)

            def pv2(u):
                br, h = divmod(u, QH)
                v_, kv = (vs, vw)[br], h // 4 * DK
                pe.wait_ge(s_pTc2, u + 1)
                if u == 0:
                    pe.wait_ge(s_cyn, 4)
                else:
                    pe.wait_ge(s_yn2, u)
                pe.matmul(ps_m[1][:, 0:DK], pT2[:, u % 2, 0:P], v_[:, 0, kv:kv + DK], start=True, stop=True)
                pe.matmul(ps_m[1][:, DK:2 * DK], pT2[:, u % 2, P:2 * P], v_[:, 0, kv:kv + DK], start=True, stop=False)
                pe.matmul(ps_m[1][:, DK:2 * DK], pT2[:, u % 2, 2 * P:], v_[:, 1, kv:kv + DK], start=False, stop=True
                          ).then_inc(s_pv2, 1)

            def nsa_slot(i):
                if i >= 3 and (i - 3) % 2 == 0 and (i - 3) // 2 < 2 * QH:
                    scores2((i - 3) // 2)
                if i >= 5 and (i - 5) % 2 == 0 and (i - 5) // 2 < 2 * QH:
                    probs2_T((i - 5) // 2)
                if i >= 7 and (i - 7) % 2 == 0 and (i - 7) // 2 < 2 * QH:
                    pv2((i - 7) // 2)

            def gk(i):
                unit_begin()
                for h in (2 * i, 2 * i + 1):
                    last = pe.matmul(ps_m[0][:, (h % 2) * T:(h % 2 + 1) * T], w_gk2[:, h * DK:(h + 1) * DK], aT[:],
                                     start=True, stop=True)
                unit_end(last)

            def level_products(i):
                if i == 0:
                    pe.wait_ge(s_t2c, t2[0])
                    pe.wait_ge(s_yn2, 2 * QH)
                    pe.wait_ge(s_pTc2, 2 * QH)
                else:
                    pe.wait_ge(s_gQ, i)
                for h in range(TT if i < 8 else 1):
                    if i >= 1:
                        pe.wait_ge(s_gS, 2 * i + h)
                    for g_ in range(GH):
                        o = g_ * T + h * P
                        if i == 0:
                            l_, r_ = klT[:, g_, h * P:(h + 1) * P], qlT[:, g_, h * P:(h + 1) * P]
                        elif i < 8:
                            l_ = r_ = QK[i % 2][:, o:o + P]
                        else:
                            l_, r_ = QK[i % 2][:, g_ * T:g_ * T + P], QK[i % 2][:, g_ * T + P:(g_ + 1) * T]
                        last = pe.matmul(ps_m[2 + h][:, g_ * P:(g_ + 1) * P], l_, r_, start=True, stop=True)
                    last.then_inc(s_gP, 1)

            def gla_out(i):
                t, hp = divmod(i, 2)
                pe.wait_ge(s_gS, 18)
                if i >= 2:
                    pe.wait_ge(s_goc, i - 1)
                for h in (2 * hp, 2 * hp + 1):
                    dst = ps_m[2 + i % 2][:, (h % 2) * DV:(h % 2 + 1) * DV]
                    if t == 0:
                        last = pe.matmul(dst, sT[:, 0, h, :], vl[:, 0, h, :], start=True, stop=True)
                    else:
                        pe.matmul(dst, sT[:, 2, h, :], vl[:, 0, h, :], start=True, stop=False)
                        last = pe.matmul(dst, sT[:, 1, h, :], vl[:, 1, h, :], start=False, stop=True)
                last.then_inc(s_go, 1)

            def stg_heads(h, ready):
                rows_T([stg2[:, t, hh * DK:(hh + 1) * DK] for hh in (h, h + 1) for t in range(TT)], ready)

            lq1 = G["lq1"]["s0"]
            for g in groups[15:28]:
                for j in range(g["ns"]):
                    gemm(pe, g, j, A(aH), A(aL),
                         (lambda j: pe.wait_ge(s_xl, built("h", 2 * j + 2))) if g["name"] == "nq0" else None)
                    here = (g["name"], j)
                    if here == ("nq1", 4):
                        nq_T(0)
                        nq_T(2)
                    if here == ("ncmp", 4):
                        nq_T(4)
                        nq_T(6)
                    if here == ("nslc", 2):
                        stg_heads(0, 3)
                        stg_heads(2, 3)
                    if here == ("nslc", 7):
                        direct(0, "k")
                        direct(1, "v")
                    if here == ("nwin", 1):
                        stg_heads(0, 4)
                    if here == ("nwin", 2):
                        hid_T(0)
                        hid_T(1)
                    if here == ("nwin", 3):
                        compressed()
                    if here == ("nwin", 5):
                        rows_T([kcn[:, :]], 5)
                    if here == ("glq0", 1):
                        stg_heads(0, 6)
                    if here == ("glq0", 2):
                        cmp_scores()
                    if here == ("glq0", 5):
                        rows_T([pc[:, t, 4 * kv:4 * kv + 4, :].rearrange("p h n -> p (h n)") for t in range(TT) for kv in range(KVH)], 7)
                    if g["name"] == "lq1" and j in (1, 2, 3, 4):
                        cmp_pv(j - 1)
                    if here == ("lq1", 2):
                        stg_heads(0, "glq0")
                    if here == ("lar0", 2):
                        stg_heads(0, "lq1")
                    if here == ("lk", 1):
                        rows_T([stg2[:, t, 0:16] for t in range(TT)], "lar0")
                    if here == ("lk", 2):
                        gk(0)
                        gk(1)
                    if here == ("lv0", 1):
                        stg_heads(0, "lk")
                        stg_heads(2, "lk")
                    if g["s0"] + j >= lq1:
                        nsa_slot(g["s0"] + j - lq1)
                    if here == ("lv1", 6):
                        level_products(0)
                    if g["name"] == "lr1":
                        level_products(1 + j)
                    if g["name"] == "lr2" and 1 <= j <= 4:
                        gla_out(j - 1)

            def y2_src(k, t):
                return yn[:, t, k, :] if k < 8 else yg[:, t, (k - 8) // 2, (k % 2) * P:(k % 2 + 1) * P]

            def before_y2(u):
                if u == 0:
                    pe.wait_ge(s_goc, 4)
                    pe.wait_ge(s_y2n, 1)
                if u == 4:
                    pe.wait_ge(s_y2g, 1)
            build_pe(pe, "y2", y2_src, before_y2)
            for g in groups[28:32]:
                for j in range(g["ns"]):
                    gemm(pe, g, j, A(aH), A(aL),
                         (lambda j: pe.wait_ge(s_xl, built("y2", 2 * j + 2))) if g["name"] == "w2o0" else None)
                    u = g["s0"] + j - G["w2o2"]["s0"] - 4
                    if 0 <= u < 8:
                        build_pe(pe, "mem", lambda k, t: memn[:, t, k * P:(k + 1) * P],
                                 lambda u: pe.wait_ge(s_mem, 16), only=[u])
            if stop and stop[0] == "two":
                return

            def scores3(u):
                if u == 0:
                    pe.wait_ge(s_t2c, t2[0])
                else:
                    pe.wait_ge(s_exp3, u)
                for t in range(TT):
                    last = pe.matmul(ps_m[2][:, t * T:(t + 1) * T], cqT[:, u, t * P:(t + 1) * P], ckT[:, u, :],
                                     start=True, stop=True)
                last.then_inc(s_sc3, 1)

            def probs3_T(u):
                pe.wait_ge(s_exp3, u + 1)
                if u >= 1:
                    pe.wait_ge(s_pTc3, u)
                for t in range(TT):
                    for m in range(TT):
                        i = t * TT + m
                        last = pe.transpose(ps_m[3][:, i * P:(i + 1) * P], sS3[:, u, t, m * P:(m + 1) * P], ident[:])
                last.then_inc(s_pt3, 1)

            def pv3(u):
                pe.wait_ge(s_pTc3, u + 1)
                if u >= 1:
                    pe.wait_ge(s_on, u)
                else:
                    evacuated(pe, G["mv"])
                for t in range(TT):
                    for m in range(TT):
                        last = pe.matmul(ps_m[1][:, t * P:(t + 1) * P], pT3[:, u, t, m, :],
                                         cvn[:, m, u * DK:(u + 1) * DK], start=(m == 0), stop=(m == TT - 1))
                last.then_inc(s_pv3, 1)

            def cross_T(buf, h, ready):
                unit_begin()
                pe.wait_ge(s_ckr, ready)
                for i, (hh, t) in enumerate([(hh, t) for hh in (h, h + 1) for t in range(TT)]):
                    last = pe.transpose(ps_m[0][:, i * P:(i + 1) * P], buf[:, t, hh, :], ident[:])
                unit_end(last)

            for g in groups[32:35]:
                for j in range(g["ns"]):
                    op = (aH, aL) if g["name"] == "mq" else (mH, mL)
                    before = None
                    if g["name"] == "mk":
                        before = lambda j: pe.wait_ge(s_xl, built("mem", 2 * j + 2))
                    if g["name"] == "mq":
                        before = lambda j: pe.wait_ge(s_xl, built("hq", 2 * j + 2))
                    gemm(pe, g, j, A(op[0]), A(op[1]), before)
                    here = (g["name"], j)
                    if g["name"] == "mk":
                        def before_hq(u):
                            if u == 0:
                                evacuated(pe, G["w2o3"])
                                evacuated(pe, G["w2o2"])
                        build_pe(pe, "hq", lambda k, t: x[:, t, k * P:(k + 1) * P], before_hq, only=[j])
                    if here == ("mq", 4):
                        pe.wait_ge(s_xl, built("hq", KT))
                        cross_T(ckn, 0, 1)
                        cross_T(ckn, 2, 1)
                    if here == ("mv", 2):
                        cross_T(cqn, 0, 2)
                        cross_T(cqn, 2, 2)
                    if g["name"] == "mv" and 4 <= j:
                        scores3(j - 4)
                    if g["name"] == "mv" and 6 <= j:
                        probs3_T(j - 6)
            probs3_T(2)
            probs3_T(3)
            for u in range(MH):
                pv3(u)

            def before_oc(u):
                if u == 0:
                    pe.wait_ge(s_on, MH)
                    pe.wait_ge(s_pTc3, MH)
            build_pe(pe, "oc", lambda k, t: ocn[:, t, k, :], before_oc)
            for g in groups[35:39]:
                for j in range(g["ns"]):
                    gemm(pe, g, j, A(ocH), A(ocL),
                         (lambda j: pe.wait_ge(s_xl, built("oc", 2 * j + 2))) if g["name"] == "co0" else None)
            if stop and stop[0] == "three":
                return

            build_pe(pe, "hf", lambda k, t: x[:, t, k * P:(k + 1) * P],
                     lambda u: evacuated(pe, G[f"co{u // 2}"]))

            def hidden_T(j):
                def before(u):
                    evacuated(pe, G[f"fu{j}"])
                build_pe(pe, f"gu{j}", lambda k, t: hn[:, t, k * P:(k + 1) * P], before)

            for part, (g0, n) in enumerate(PARTS):
                for i in range(g0, g0 + n):
                    for g in (G[f"fg{i}"], G[f"fu{i}"]):
                        for j in range(g["ns"]):
                            gemm(pe, g, j, A(aH), A(aL),
                                 (lambda j: pe.wait_ge(s_xl, built("hf", 2 * j + 2))) if g["name"] == "fg0" else None)
                            if g["name"] == f"fg{i}" and j == 2 and i > g0:
                                hidden_T(i - 1)
                hidden_T(g0 + n - 1)
                for i in range(4):
                    g = G[f"fd{part}{i}"]
                    for j in range(g["ns"]):
                        gemm(pe, g, j, A(guH), A(guL),
                             (lambda j: pe.wait_ge(s_xl, built(f"gu{g0}", 2 * j + 2))) if i == 0 else None)

        @block.scalar
        def _(act):
            for s in range(LEAD):
                split_hi(act, s)
            build_act(act, "x", A(aH))

            def sigmoid(i, func):
                evacuated(act, G[("cg0", "cg1", "ga0", "ga1", "ag0", "ag1")[i]])
                act.activation(stg[:], stg[:], func).then_inc(s_stga, 1)

            def conv_in(j):
                for c in range(2):
                    act.wait_ge(s_cht, 2 * j + c + 1)
                    act.copy(hT[:, 4 * j + 2 * c:4 * j + 2 * c + 2, TAPS - 1:],
                             ps_m[c][:].rearrange("p (c t) -> p c t", c=2)).then_inc(s_hT, 1)

            def q_T(j):
                for c in range(2):
                    act.wait_ge(s_qt, 2 * j + c + 1)
                    act.copy(qT[:, 4 * j + 2 * c:4 * j + 2 * c + 2, :].rearrange("p c t -> p (c t)"),
                             ps_m[2 + c][:]).then_inc(s_qT, 1)

            def k_T():
                act.wait_ge(s_qt, 5)
                act.copy(kT[:].rearrange("p k t -> p (k t)"), ps_m[2][:]).then_inc(s_qT, 1)

            def exps(u):
                act.wait_ge(s_sm, u + 1)
                act.activation(sS[:, u % 2, 0:P], sS[:, u % 2, 0:P], ACT.Exp, bias=mx[:, u, 0:1],
                               accum_out=den[:, u, 0:1])
                act.activation(sS[:, u % 2, P:], sS[:, u % 2, P:], ACT.Exp, bias=mx[:, u, 1:2],
                               accum_out=den[:, u, 1:2])
                act.activation(esk[:, u, :], mx[:, u, :], ACT.Exp, bias=sinks[:, u:u + 1]).then_inc(s_exp, 1)

            def probs_copy(u):
                act.wait_ge(s_pt, u + 1)
                if u >= 2:
                    act.wait_ge(s_pv, u - 1)
                act.copy(pT[:, u % 2, :], ps_m[2][:, 0:3 * P]).then_inc(s_pTc, 1)

            def gate_copy(c):
                act.wait_ge(s_gat, c + 1)
                act.copy(gT[:, c, :], ps_m[1][:, 0:T]).then_inc(s_gT, 1)

            def attn_slot(i):
                if i - 1 in score_slot:
                    exps(score_slot[i - 1])
                if i - 3 in score_slot:
                    probs_copy(score_slot[i - 3])

            for g in groups[:11]:
                for j in range(g["ns"]):
                    split_hi(act, g["s0"] + j + LEAD)
                    here = (g["name"], j)
                    if here == ("cv1", 1):
                        sigmoid(0, ACT.Sigmoid)
                    if here == ("cv1", 3):
                        conv_in(0)
                    if here == ("q0", 1):
                        sigmoid(1, ACT.Sigmoid)
                    if here == ("q0", 3):
                        conv_in(1)
                    if here == ("q1", 2):
                        q_T(0)
                    if here == ("kv", 3):
                        q_T(1)
                    if here == ("ga0", 2):
                        k_T()
                    if here == ("ga0", 6):
                        act.wait_ge(s_lnc, 2)
                        act.wait_ge(s_conv, conv_units)
                        act.activation(sq_sb[:], cT[:], ACT.Square).then_inc(s_lna, 1)
                    if here == ("ga1", 1):
                        act.wait_ge(s_lnc, LNC_READ_SUMS)
                        act.activation(rstd_sb[:], rstd_sb[:], ACT.Sqrt).then_inc(s_lna, 1)
                    if here == ("ga1", 2):
                        sigmoid(2, ACT.Silu)
                    if g["name"] == "ga1" and j in (5, 6, 7):
                        gate_copy(j - 5)
                    if here == ("ag0", 0):
                        gate_copy(3)
                    if here == ("ag0", 1):
                        sigmoid(3, ACT.Silu)
                        act.wait_ge(s_lnc, LNC_READ_SUMS + 2)
                        for c in range(8):
                            last = act.activation(cT[:, c, :], cT[:, c, :], ACT.Silu,
                                                  scale=cols[:, CLG + c:CLG + c + 1],
                                                  bias=cols[:, CLB + c:CLB + c + 1])
                        last.then_inc(s_lna, 1)
                    if g["name"] == "ag0" and j in (3, 4, 5, 6):
                        gate_copy(4 + j - 3)
                    if here == ("ag1", 1):
                        sigmoid(4, ACT.Silu)
                    i = g["s0"] + j - ga
                    if i >= 3:
                        attn_slot(i)
            sigmoid(5, ACT.Silu)
            attn_slot(32)
            act.wait_ge(s_lnc, LNC_READ_SUMS + 3)
            act.wait_ge(s_used, G["wo0"]["s0"])
            act.copy(aH[:, 0:8, :], cT[:]).then_inc(s_ych, 1)
            build_act(act, "yattn", A(aH, 8))
            for g in groups[11:15]:
                for j in range(g["ns"]):
                    split_hi(act, g["s0"] + j + LEAD)
            if stop and stop[0] == "one":
                return

            roots = [0]

            def root(ap):
                act.wait_ge(s_var, roots[0] + 1)
                act.activation(ap, ap, ACT.Sqrt).then_inc(s_sqrt, 1)
                roots[0] += 1

            t2 = [0]

            def bank0(*copies):
                act.wait_ge(s_t2, t2[0] + 1)
                for out_, in_, scale in copies:
                    last = act.copy(out_, in_) if scale is None else act.activation(out_, in_, ACT.Copy, scale=scale)
                last.then_inc(s_t2c, 1)
                t2[0] += 1

            def col(c):
                return cols[:, c:c + 1]

            root(var_ln)
            build_act(act, "h", A(aH), lambda k: col(GM + k))
            for t in range(TT):
                last = act.activation(sq_row[:], x[:, t, :], ACT.Square, accum_out=ss[:, t:t + 1])
                if t == 0:
                    last.then_inc(s_act, 1)
                    act.wait_ge(s_act, 1)
            last.then_inc(s_ss, 1)
            root(ss)

            def heads2(dst, h, scale):
                bank0((dst[:, h:h + 2, :].rearrange("p h t -> p (h t)"), ps_m[0][:], scale))

            def cmp_exp():
                act.wait_ge(s_csm, 2)
                act.activation(pc[:, :, :, 0:NCMP].rearrange("p t h n -> p (t h) n"),
                               pc[:, :, :, 0:NCMP].rearrange("p t h n -> p (t h) n"), ACT.Exp).then_inc(s_cexp, 1)

            def exps2(u):
                act.wait_ge(s_sm2, u + 1)
                act.activation(sS2[:, u % 2, 0:P], sS2[:, u % 2, 0:P], ACT.Exp, bias=mx2[:, u, 0:1],
                               accum_out=den2[:, u, 0:1])
                act.activation(sS2[:, u % 2, P:], sS2[:, u % 2, P:], ACT.Exp, bias=mx2[:, u, 1:2],
                               accum_out=den2[:, u, 1:2]).then_inc(s_exp2, 1)

            def probs2_copy(u):
                act.wait_ge(s_pt2, u + 1)
                if u >= 2:
                    act.wait_ge(s_pv2, u - 1)
                act.copy(pT2[:, u % 2, :], ps_m[3][:, 0:3 * P]).then_inc(s_pTc2, 1)

            def nsa_slot(i):
                if i >= 4 and (i - 4) % 2 == 0 and (i - 4) // 2 < 2 * QH:
                    exps2((i - 4) // 2)
                if i >= 6 and (i - 6) % 2 == 0 and (i - 6) // 2 < 2 * QH:
                    probs2_copy((i - 6) // 2)

            def level_exp(i):
                act.wait_ge(s_gE, i)
                act.activation(E[i % 2][:], E[i % 2][:], ACT.Exp, scale=1.0 / 16.0).then_inc(s_gX, 1)

            def log_sigmoid():
                act.wait_ge(s_t2c, t2[0])
                act.wait_ge(s_yn2, 2 * QH)
                act.activation(E[1][:], gz[:], ACT.Abs).then_inc(s_z, 1)
                act.wait_ge(s_z, 1)
                act.activation(E[1][:], E[1][:], ACT.Exp, scale=-1.0).then_inc(s_z, 1)
                act.wait_ge(s_z, 2)
                act.activation(E[1][:], E[1][:], ACT.Ln, bias=1.0).then_inc(s_z, 1)

            lq1 = G["lq1"]["s0"]
            for g in groups[15:28]:
                for j in range(g["ns"]):
                    split_hi(act, g["s0"] + j + LEAD)
                    here = (g["name"], j)
                    if here == ("nq1", 1):
                        root(ss_q[:, 0])
                    if here == ("nq1", 5):
                        heads2(nqT, 0, colq)
                        heads2(nqT, 2, colq)
                    if here == ("ncmp", 1):
                        root(ss_q[:, 1])
                    if here == ("ncmp", 5):
                        heads2(nqT, 4, colq)
                        heads2(nqT, 6, colq)
                    if here == ("nslc", 3):
                        heads2(kcT, 0, None)
                        heads2(vcT, 0, None)
                    if here == ("nwin", 0):
                        root(ss_k[:, 0])
                    if here == ("nwin", 1):
                        act.wait_ge(s_direct, 8)
                        act.activation(hid[:], ps_m[3][0:2 * NCMP, :], ACT.Silu).then_inc(s_hid, 1)
                    if here == ("nwin", 2):
                        heads2(ksT, 0, col(GKS))
                        bank0((hidTk[:, :, 0:2 * NCMP],
                               ps_m[0][:, 0:64].rearrange("p (a b) -> p a b", a=2)[:, :, 0:2 * NCMP], None))
                        act.wait_ge(s_c2v, HIDTV_CLEARED)
                        bank0(*[(hidTv[:, hk, kv, :, 0:NCMP],
                                 ps_m[0][:, hk * 32 + kv * NCMP:hk * 32 + (kv + 1) * NCMP].unsqueeze(1).to_broadcast([P, 4, NCMP]),
                                 None) for hk in range(2) for kv in range(KVH)])
                    if here == ("nwin", 4):
                        root(ss_c)
                    if here == ("nwin", 6):
                        bank0((kcT15[:], ps_m[0][:, 0:2 * NCMP], col(GKC)))
                    if here == ("glq0", 1):
                        root(ss_k[:, 1])
                    if here == ("glq0", 2):
                        heads2(kwT, 0, col(GKW))
                    if here == ("glq0", 4):
                        cmp_exp()
                    if here == ("glq0", 6):
                        bank0((pTc[:].rearrange("p t k q -> p (t k q)"), ps_m[0][:], None))
                    if here == ("lq1", 1):
                        evacuated(act, G["glq0"])
                        act.activation(gates[:], gates[:], ACT.Sigmoid).then_inc(s_gsig, 1)
                    if here == ("lq1", 3):
                        heads2(qlT, 0, float(DK) ** -0.5)
                    if here == ("lar0", 3):
                        heads2(qlT, 2, float(DK) ** -0.5)
                    if here == ("lk", 2):
                        bank0((aT[:], ps_m[0][0:16, 0:T], None))
                    if here == ("lk", 3):
                        for i in range(2):
                            act.wait_ge(s_t2, t2[0] + 1)
                            for h in (2 * i, 2 * i + 1):
                                last = act.activation(gz[:, h * T:(h + 1) * T], ps_m[0][:, (h % 2) * T:(h % 2 + 1) * T],
                                                      ACT.Identity, bias=col(BGK + h))
                            last.then_inc(s_t2c, 1)
                            t2[0] += 1
                    if here == ("lv0", 2):
                        heads2(klT, 0, None)
                        heads2(klT, 2, None)
                    if g["s0"] + j >= lq1:
                        nsa_slot(g["s0"] + j - lq1)
                    if here == ("lv1", 6):
                        log_sigmoid()
                    if g["name"] == "lr1":
                        if j == 0:
                            level_exp(1)
                        if j < 7:
                            level_exp(j + 2)
                    if here == ("lr2", 0):
                        evacuated(act, G["lr1"])
                        evacuated(act, G["lar0"])
                        act.activation(rl[:, :, 0:768], rl[:, :, 0:768], ACT.Silu)
                    if here == ("lr2", 1):
                        root(ss_n)
            evacuated(act, G["lr2"])
            act.activation(rl[:, :, 768:], rl[:, :, 768:], ACT.Silu).then_inc(s_rl, 1)
            root(ss_g)
            act.wait_ge(s_used, G["w2o0"]["s0"])
            build_act(act, "y2", A(aH), lambda k: col(GNS) if k < 8 else col(GGL + k % 2))

            def squares(src, sums, scratch, count):
                for t in range(TT):
                    act.activation(scratch, src[:, t, :], ACT.Square, accum_out=sums[:, t:t + 1]).then_inc(s_sqs, 1)
                    act.wait_ge(s_sqs, count + t + 1)

            for g in groups[28:32]:
                for j in range(g["ns"]):
                    split_hi(act, g["s0"] + j + LEAD)
                    u = g["s0"] + j - G["w2o2"]["s0"] - 5
                    if 0 <= u < 8:
                        build_act(act, "mem", A(mH), lambda k: col(GME + k), only=[u])
                    if u == 0:
                        squares(memn, ss_m, sq_m[:], 0)
            build_act(act, "mem", A(mH), lambda k: col(GME + k), only=list(range(g["s0"] + 7 - G["w2o2"]["s0"] - 4, 8)))
            if stop and stop[0] == "two":
                return

            root(ss_m)
            evacuated(act, G["w2o3"])
            evacuated(act, G["w2o2"])

            def exps3(u):
                act.wait_ge(s_sm3, u + 1)
                for t in range(TT):
                    last = act.activation(sS3[:, u, t, :], ps_m[2][:, t * T:(t + 1) * T], ACT.Exp,
                                          bias=mx3[:, u, t:t + 1], accum_out=den3[:, u, t:t + 1])
                last.then_inc(s_exp3, 1)

            def probs3_copy(u):
                act.wait_ge(s_pt3, u + 1)
                act.copy(pT3[:, u].rearrange("p t m q -> p (t m q)"), ps_m[3][:]).then_inc(s_pTc3, 1)

            for g in groups[32:35]:
                for j in range(g["ns"]):
                    split_hi(act, g["s0"] + j + LEAD)
                    here = (g["name"], j)
                    if g["name"] == "mk" and j >= 1:
                        build_act(act, "hq", A(aH), lambda k: col(GC + k), only=[j - 1])
                    if here == ("mq", 0):
                        build_act(act, "hq", A(aH), lambda k: col(GC + k), only=[7])
                        squares(x, ss_x2, sq_m[:], 2)
                    if here == ("mq", 1):
                        root(ss_x2)
                    if here == ("mq", 3):
                        root(ss_ck)
                    if here == ("mq", 5):
                        heads2(ckT, 0, col(GCK))
                        heads2(ckT, 2, col(GCK))
                    if here == ("mv", 1):
                        root(ss_cq)
                    if here == ("mv", 3):
                        heads2(cqT, 0, colcq)
                        heads2(cqT, 2, colcq)
                    if g["name"] == "mv" and j >= 5:
                        exps3(j - 5)
                    if here == ("mv", 7):
                        probs3_copy(0)
            exps3(3)
            for u in range(1, MH):
                probs3_copy(u)
            build_act(act, "oc", A(ocH))
            for g in groups[35:39]:
                for j in range(g["ns"]):
                    split_hi(act, g["s0"] + j + LEAD)
            if stop and stop[0] == "three":
                return

            build_act(act, "hf", A(aH), lambda k: col(GF + k))
            squares(x, ss_x3, sq_f[:], 4)
            root(ss_x3)
            for part, (g0, n) in enumerate(PARTS):
                for i in range(g0, g0 + n):
                    def hidden(u):
                        build_act(act, f"gu{u}", A(guH, 4 * (u - g0)))
                    for j in range(8):
                        split_hi(act, G[f"fg{i}"]["s0"] + j + LEAD)
                        if j == 3 and i > g0:
                            hidden(i - 1)
                    for j in range(8):
                        split_hi(act, G[f"fu{i}"]["s0"] + j + LEAD)
                        if j == 0:
                            g = G[f"fg{i}"]
                            psum_ready(act, g)
                            act.wait_ge(s_ffs, 1)
                            if i >= 1:
                                evacuated(act, G[f"fu{i - 1}"])
                            for t in range(TT):
                                act.activation(sg[:, t, :], ps_g[pair_of(g)][t][:], ACT.Silu, scale=ss_x3[:, t:t + 1]
                                               ).then_inc(s_free[pair_of(g)], 1)
                hidden(g0 + n - 1)
                for i in range(4):
                    g = G[f"fd{part}{i}"]
                    for j in range(g["ns"]):
                        split_hi(act, g["s0"] + j + LEAD)

        @block.vector
        def _(dve):
            def link(ins):
                n_dve[0] += 1
                ins.then_inc(s_dve, 1)
                dve.wait_ge(s_dve, n_dve[0])

            def mark(ins):
                n_dve[0] += 1
                ins.then_inc(s_dve, 1)
                return n_dve[0]

            dve.wait_ge(s_cols, 1)
            dve.tensor_copy(cols[:], ps_m[2][:, 0:165]).then_inc(s_colsb, 1)
            dve.wait_ge(s_cols, 2)
            dve.tensor_copy(convw[:, :, 0:TAPS], ps_m[3][:, 0:256].rearrange("p (c k) -> p c k", c=8)[:, :, 0:TAPS]
                            ).then_inc(s_colsb, 1)
            dve.wait_ge(s_pool, POOL_CONSTS)
            link(dve.tensor_tensor(iot[:, 0, :], iot[:, 0, :], iot[:, 1, :], ALU.bitwise_xor))
            link(dve.tensor_copy(xorf[:], iot[:, 0, :]))
            link(dve.tensor_tensor(xorf[:], xorf[:], tri[:], ALU.mult))
            for l in range(LEVELS + 1):
                last = dve.tensor_scalar(ge[:, l, :], xorf[:], float(2 ** l), None, ALU.is_ge)
            link(last)
            for l in range(LEVELS):
                dve.tensor_tensor(lmask[:, l, :], ge[:, l, :], ge[:, l + 1, :], ALU.subtract)
            link(dve.tensor_copy(lmask[:, LEVELS, :], ident[:]))
            build_dve(dve, "x", A(aH), A(aL))

            def evac(g, dst, t0=0):
                psum_ready(dve, g)
                b = bias_slot(dve, g["name"])
                for t in range(TT):
                    dve.tensor_tensor(dst(t), ps_g[pair_of(g)][t][:, :g["n"]], b, ALU.add
                                      ).then_inc(s_free[pair_of(g)], 1)

            def evac_stage(i, name):
                g = G[name]
                psum_ready(dve, g)
                b = bias_slot(dve, name)
                if i == 3:
                    dve.wait_ge(s_gat, 4)
                if i == 4:
                    dve.wait_ge(s_gat, 8)
                for t in range(TT):
                    dve.tensor_tensor(stg[:, t, :], ps_g[pair_of(g)][t][:], b, ALU.add).then_inc(s_free[pair_of(g)], 1)

            def glu(j):
                dve.wait_ge(s_stga, j + 1)
                dve.tensor_tensor(c_h[:, :, j * NG:(j + 1) * NG], c_h[:, :, j * NG:(j + 1) * NG], stg[:],
                                  ALU.mult).then_inc(s_ch, 1)

            conv_order = [(half, k, c) for half in range(2) for k in range(TAPS) for c in range(4)]
            conv_at = [0]

            def conv(n):
                for half, k, c in conv_order[conv_at[0]:conv_at[0] + n]:
                    i = conv_at[0]
                    conv_at[0] += 1
                    ct = 4 * half + c
                    if k == 0 and c == 0:
                        dve.wait_ge(s_hT, 2 * half + 2)
                    src = hT[:, ct, k:k + T]
                    w = convw[:, ct, k:k + 1]
                    if k == 0:
                        dve.tensor_scalar(cT[:, ct, :], src, w, cols[:, CB + ct:CB + ct + 1], ALU.mult,
                                          ALU.add).then_inc(s_conv, 1)
                    else:
                        dve.wait_ge(s_conv, i - 3)
                        dve.scalar_tensor_tensor(out=cT[:, ct, :], in0=src, scalar=w, in1=cT[:, ct, :],
                                                 op0=ALU.mult, op1=ALU.add).then_inc(s_conv, 1)

            def softmax(u):
                dve.wait_ge(s_sc, u + 1)
                if u >= 2:
                    dve.wait_ge(s_pt, u - 1)
                link(dve.scalar_tensor_tensor(out=sS[:, u % 2, :], in0=ps_m[0][:, 0:3 * P], scalar=HD ** -0.5,
                                              in1=mask1[:], op0=ALU.mult, op1=ALU.add))
                dve.tensor_reduce(mx[:, u, 0:1], sS[:, u % 2, 0:P], AX_X, ALU.max)
                link(dve.tensor_reduce(mx[:, u, 1:2], sS[:, u % 2, P:], AX_X, ALU.max))
                dve.tensor_scalar(mx[:, u, :], mx[:, u, :], sinks[:, u:u + 1], -1.0, ALU.max,
                                  ALU.mult).then_inc(s_sm, 1)

            def normalize(u):
                dve.wait_ge(s_pv, u + 1)
                link(dve.tensor_tensor(den[:, u, :], den[:, u, :], esk[:, u, :], ALU.add))
                link(dve.reciprocal(rden[:, u, :], den[:, u, :]))
                o = (u % 2) * 2 * HD
                for t in range(TT):
                    last = dve.tensor_scalar(q_sb[:, t, u * HD:(u + 1) * HD],
                                             ps_m[3][:, o + t * HD:o + (t + 1) * HD], rden[:, u, t:t + 1], None,
                                             ALU.mult)
                last.then_inc(s_yn, 1)

            def gate_attn(j):
                dve.wait_ge(s_stga, 5 + j)
                dve.wait_ge(s_yn, 8 * (j + 1))
                dve.tensor_tensor(q_sb[:, :, j * NG:(j + 1) * NG], q_sb[:, :, j * NG:(j + 1) * NG], stg[:],
                                  ALU.mult).then_inc(s_yat, 1)

            def layer_norm_sum(i):
                dve.wait_ge(s_lns, i + 1)
                if i == 0:
                    dve.tensor_scalar(mean_sb[:], ps_m[1][:, 0:T], 1.0 / C, None, ALU.mult).then_inc(s_lnc, 1)
                    dve.wait_ge(s_lnc, 1)
                    dve.tensor_tensor(cT[:], cT[:], mean_sb[:].unsqueeze(1).to_broadcast([P, 8, T]),
                                      ALU.subtract).then_inc(s_lnc, 1)
                else:
                    dve.tensor_scalar(rstd_sb[:], ps_m[1][:, 0:T], 1.0 / C, LN_EPS, ALU.mult,
                                      ALU.add).then_inc(s_lnc, 1)
                    dve.wait_ge(s_lna, 2)
                    dve.reciprocal(rstd_sb[:], rstd_sb[:]).then_inc(s_lnc, 1)
                    dve.wait_ge(s_lnc, LNC_READ_SUMS + 1)
                    dve.tensor_tensor(cT[:], cT[:], rstd_sb[:].unsqueeze(1).to_broadcast([P, 8, T]),
                                      ALU.mult).then_inc(s_lnc, 1)

            def half(j):
                return lambda t: c_h[:, t, j * NG:(j + 1) * NG]

            evac(G["cv0"], half(0))
            evac_stage(0, "cg0")
            glu(0)
            conv(40)
            evac(G["cv1"], half(1))
            conv(40)
            dve.wait_ge(s_ch, 1)
            evac_stage(1, "cg1")
            glu(1)
            conv(44)
            evac(G["q0"], lambda t: q_sb[:, t, 0:NG])
            conv(45)
            evac(G["q1"], lambda t: q_sb[:, t, NG:])
            conv(40)
            g = G["kv"]
            psum_ready(dve, g)
            b = bias_slot(dve, "kv")
            for t in range(TT):
                src = ps_g[pair_of(g)][t]
                for d in range(2):
                    dve.tensor_tensor(k_dup[:, t, :, d, :], src[:, 0:P].rearrange("p (k d) -> p k d", k=KVH),
                                      b[:, 0:P].rearrange("p (k d) -> p k d", k=KVH), ALU.add)
                dve.tensor_tensor(v_sb[:, t, :], src[:, P:2 * P], b[:, P:2 * P], ALU.add
                                  ).then_inc(s_free[pair_of(g)], 1)
            conv(conv_units - 209)
            dve.wait_ge(s_conv, conv_units)
            for i in range(2, 39):
                if i in score_slot:
                    softmax(score_slot[i])
                if i - 5 in score_slot:
                    normalize(score_slot[i - 5])
                if i == 6:
                    layer_norm_sum(0)
                if i == 8:
                    dve.wait_ge(s_ch, 2)
                    evac_stage(2, "ga0")
                if i == 9:
                    layer_norm_sum(1)
                if i == 16:
                    evac_stage(3, "ga1")
                if i == 22:
                    dve.wait_ge(s_gT, 8)
                    dve.wait_ge(s_lna, 3)
                    dve.tensor_tensor(cT[:], cT[:], gT[:], ALU.mult).then_inc(s_lnc, 1)
                if i == 24:
                    evac_stage(4, "ag0")
                if i == 25:
                    gate_attn(0)
                if i == 32:
                    dve.wait_ge(s_yat, 1)
                    evac_stage(5, "ag1")
            gate_attn(1)
            dve.wait_ge(s_ych, 1)
            dve.tensor_tensor(aL[:, 0:8, :], cT[:], aH[:, 0:8, :].bitcast(F32), ALU.subtract).then_inc(s_ycl, 1)
            build_dve(dve, "yattn", A(aH, 8), A(aL, 8))

            for j in range(4):
                g = G[f"wo{j}"]
                psum_ready(dve, g)
                b = bias_slot(dve, g["name"])
                for t in range(TT):
                    last = dve.scalar_tensor_tensor(out=x[:, t, j * NG:(j + 1) * NG], in0=x[:, t, j * NG:(j + 1) * NG],
                                                    scalar=ALPHA, in1=ps_g[pair_of(g)][t][:], op0=ALU.mult,
                                                    op1=ALU.add).then_inc(s_free[pair_of(g)], 1)
                evacuated(dve, g)
                for t in range(TT):
                    last = dve.tensor_tensor(x[:, t, j * NG:(j + 1) * NG], x[:, t, j * NG:(j + 1) * NG], b, ALU.add)
                last.then_inc(bias_used, 1)
                dve.wait_ge(bias_used, j + 1)
                for t in range(TT):
                    last = dve.bn_stats(bnst[:, t, j, :], x[:, t, j * NG:(j + 1) * NG])
            link(last)
            for t in range(TT):
                link(dve.bn_aggr(mv[:, t, :], bnst[:, t].rearrange("p a b -> p (a b)")))
            link(dve.tensor_scalar(var_ln, mv[:, :, 1], LN_EPS, None, ALU.add))
            dve.tensor_copy(mean_ln, mv[:, :, 0]).then_inc(s_var, 1)
            roots = [0]

            def rooted(ap):
                roots[0] += 1
                dve.wait_ge(s_sqrt, roots[0])
                link(dve.reciprocal(ap, ap))

            def variance(ap, n, eps=EPS):
                dve.tensor_scalar(ap, ap, 1.0 / n, eps, ALU.mult, ALU.add).then_inc(s_var, 1)

            rooted(var_ln)
            for q in range(4):
                c = slice(q * NG, (q + 1) * NG)
                for t in range(TT):
                    last = dve.tensor_scalar(x[:, t, c], x[:, t, c], mean_ln[:, t:t + 1], var_ln[:, t:t + 1],
                                             ALU.subtract, ALU.mult)
                link(last)
                for i, op in ((0, ALU.mult), (1, ALU.add)):
                    last = dve.tensor_tensor(x[:, :, c], x[:, :, c],
                                             ln_rows[:, i, c].unsqueeze(1).to_broadcast([P, TT, NG]), op)
                    if i == 0:
                        link(last)
                last.then_inc(s_x1, 1)
            if stop and stop[0] == "one":
                return

            build_dve(dve, "h", A(aH), A(aL), lambda k: cols[:, GM + k:GM + k + 1])
            link(dve.tensor_scalar(colq, cols[:, GQ:GQ + 1], float(DK) ** -0.5, None, ALU.mult))
            dve.wait_ge(s_ss, 1)
            variance(ss, D)
            rooted(ss)
            r2 = ss

            def take(g, t, dst, a0, a1):
                return dve.tensor_scalar(dst, ps_g[pair_of(g)][t][:, a0:a1], r2[:, t:t + 1], None, ALU.mult)

            def evac_rows(name, dst, a0=0, a1=None):
                g = G[name]
                psum_ready(dve, g)
                for t in range(TT):
                    take(g, t, dst(t), a0, a1 or g["n"]).then_inc(s_free[pair_of(g)], 1)
                evacuated(dve, g)

            def head_squares(rows, scratch, sums):
                link(dve.tensor_tensor(scratch, rows, rows, ALU.mult))
                link(dve.tensor_reduce(sums, scratch, AX_X, ALU.add))

            def q_rows(i):
                evac_rows(f"nq{i}", lambda t: nq[:, t, 4 * i:4 * i + 4, :].rearrange("p h d -> p (h d)"))
                rows = nq[:, :, 4 * i:4 * i + 4, :]
                sums = ss_q[:, i].rearrange("p (t h) -> p t h", t=TT)
                head_squares(rows, stg2[:].rearrange("p t (h d) -> p t h d", h=4), sums)
                variance(ss_q[:, i], DK)
                rooted(ss_q[:, i])
                dve.tensor_tensor(rows, rows, sums.unsqueeze(3).to_broadcast([P, TT, 4, DK]),
                                  ALU.mult).then_inc(s_t2s, 1)

            def kv_rows(i, name, v_):
                g = G[name]
                psum_ready(dve, g)
                for t in range(TT):
                    take(g, t, stg2[:, t, 0:T], 0, T)
                    take(g, t, v_[:, t, :], T, 2 * T).then_inc(s_free[pair_of(g)], 1)
                evacuated(dve, g)
                rows = stg2[:, :, 0:T].rearrange("p t (h d) -> p t h d", h=KVH)
                sums = ss_k[:, i].rearrange("p (t h) -> p t h", t=TT)
                head_squares(rows, stg2[:, :, T:2 * T].rearrange("p t (h d) -> p t h d", h=KVH), sums)
                variance(ss_k[:, i], DK)
                rooted(ss_k[:, i])
                dve.tensor_tensor(rows, rows, sums.unsqueeze(3).to_broadcast([P, TT, KVH, DK]),
                                  ALU.mult).then_inc(s_t2s, 1)

            q_rows(0)
            q_rows(1)
            evac_rows("ncmp", lambda t: stg2[:, t, :])
            dve.memset(hidTv[:], 0.0).then_inc(s_c2v, 1)
            dve.memset(vc_bd[:], 0.0)
            dve.memset(pc[:], 0.0).then_inc(s_t2s, 1)
            dve.wait_ge(s_t2c, 6)
            for i, (src, pe0) in enumerate(((kcT, PEK), (vcT, PEV))):
                for h in range(2):
                    for kv in range(KVH):
                        last = dve.tensor_tensor(
                            kp[:, i, 16 * h:16 * h + 16, kv, :],
                            src[:, kv, 16 * h:16 * h + 16 * NCMP].rearrange("p (n b) -> p b n", b=16),
                            cols[:, pe0 + 16 * h:pe0 + 16 * h + 16].unsqueeze(2).to_broadcast([P, 16, NCMP]), ALU.add)
                last.then_inc(s_kp, 1)
            kv_rows(0, "nslc", vs)
            dve.wait_ge(s_c2, 1)
            link(dve.tensor_copy(kcn[:], ps_m[1][0:2 * NCMP, 0:P]))
            dve.wait_ge(s_t2s, 3)
            for kv in range(KVH):
                for r in range(4):
                    last = dve.tensor_copy(vc_bd[32 * r:32 * r + 32, kv, r, :],
                                           ps_m[1][32 * r:32 * r + 32, (1 + kv) * P:(2 + kv) * P])
            last.then_inc(s_c2v, 1)
            link(dve.tensor_tensor(sq_c[:], kcn[:], kcn[:], ALU.mult))
            link(dve.tensor_reduce(ss_c, sq_c[:], AX_X, ALU.add))
            variance(ss_c, DK)
            rooted(ss_c)
            dve.tensor_scalar(kcn[:], kcn[:], ss_c, None, ALU.mult).then_inc(s_t2s, 1)
            dve.wait_ge(s_t2c, 7)
            kv_rows(1, "nwin", vw)
            dve.wait_ge(s_csc, 1)
            src = ps_m[2][:, 0:256].rearrange("p (t h n) -> p t h n", t=TT, h=QH)
            for h in range(QH):
                last = dve.scalar_tensor_tensor(out=pc[:, :, h, 0:NCMP], in0=distc[:, :, 0:NCMP],
                                                scalar=2.0 ** -(h + 1), in1=src[:, :, h, 0:NCMP], op0=ALU.mult,
                                                op1=ALU.add)
            last.then_inc(s_csm, 1)
            dve.wait_ge(s_csm, 1)
            pcv = pc[:, :, :, 0:NCMP].rearrange("p t h n -> p (t h) n")
            link(dve.tensor_reduce(mxc, pcv, AX_X, ALU.max))
            dve.tensor_tensor(pcv, pcv, mxc.unsqueeze(2).to_broadcast([P, TT * QH, NCMP]), ALU.subtract).then_inc(s_csm, 1)
            dve.wait_ge(s_cexp, 1)
            link(dve.tensor_reduce(denc, pcv, AX_X, ALU.add))
            link(dve.reciprocal(rc, denc))
            link(dve.tensor_tensor(rc.rearrange("p (t h) -> p t h", t=TT), rc.rearrange("p (t h) -> p t h", t=TT),
                                   visc[:].unsqueeze(2).to_broadcast([P, TT, QH]), ALU.mult))
            dve.tensor_tensor(pcv, pcv, rc.unsqueeze(2).to_broadcast([P, TT * QH, NCMP]), ALU.mult).then_inc(s_t2s, 1)
            g = G["glq0"]
            psum_ready(dve, g)
            dve.wait_ge(s_t2c, 11)
            for t in range(TT):
                dve.scalar_tensor_tensor(out=gates[:, t, :], in0=ps_g[pair_of(g)][t][:, 0:24], scalar=r2[:, t:t + 1],
                                         in1=bgate[:], op0=ALU.mult, op1=ALU.add)
                last = take(g, t, stg2[:, t, 0:T], 24, 24 + T)
                last.then_inc(s_free[pair_of(g)], 1)
            evacuated(dve, g)
            for i in range(4):
                t, kv = i // KVH, i % KVH
                if i == 0:
                    dve.wait_ge(s_gsig, 1)
                dve.wait_ge(s_cpv, i + 1)
                gt = gates[:, t, :].rearrange("p (h b) -> p h b", b=3)[:, 4 * kv:4 * kv + 4, 0:1]
                dve.tensor_tensor(yn[:, t, 4 * kv:4 * kv + 4, :], ps_m[1][:].rearrange("p (h d) -> p h d", h=4),
                                  gt.to_broadcast([P, 4, DK]), ALU.mult).then_inc(s_cyn, 1)
            dve.wait_ge(s_cyn, 4)

            def softmax2(u):
                br, h = divmod(u, QH)
                dve.wait_ge(s_sc2, u + 1)
                if u >= 2:
                    dve.wait_ge(s_pt2, u - 1)
                link(dve.scalar_tensor_tensor(out=sS2[:, u % 2, :], in0=dist2[:], scalar=2.0 ** -(h + 1),
                                              in1=ps_m[2][:, 0:3 * P], op0=ALU.mult, op1=ALU.add))
                dve.tensor_reduce(mx2[:, u, 0:1], sS2[:, u % 2, 0:P], AX_X, ALU.max, negate=True)
                dve.tensor_reduce(mx2[:, u, 1:2], sS2[:, u % 2, P:], AX_X, ALU.max, negate=True).then_inc(s_sm2, 1)

            def normalize2(u):
                br, h = divmod(u, QH)
                dve.wait_ge(s_pv2, u + 1)
                link(dve.reciprocal(rden2[:, u, :], den2[:, u, :]))
                link(dve.tensor_tensor(rden2[:, u, :], rden2[:, u, :], gates[:, :, 3 * h + 1 + br], ALU.mult))
                if br == 1:
                    dve.wait_ge(s_yn2, u - QH + 1)
                for t in range(TT):
                    last = dve.scalar_tensor_tensor(out=yn[:, t, h, :], in0=ps_m[1][:, t * DK:(t + 1) * DK],
                                                    scalar=rden2[:, u, t:t + 1], in1=yn[:, t, h, :], op0=ALU.mult,
                                                    op1=ALU.add)
                last.then_inc(s_yn2, 1)

            lq1 = G["lq1"]["s0"]
            for i in range(3, 40):
                if (i - 3) % 2 == 0 and (i - 3) // 2 < 2 * QH:
                    softmax2((i - 3) // 2)
                if i == 8:
                    dve.wait_ge(s_t2c, 13)
                    evac_rows("lq1", lambda t: stg2[:, t, 0:T])
                if i == 16:
                    dve.wait_ge(s_t2c, 14)
                    g = G["lar0"]
                    psum_ready(dve, g)
                    for t in range(TT):
                        take(g, t, stg2[:, t, 0:16], 0, 16)
                        take(g, t, rl[:, t, 0:T], 16, 16 + T).then_inc(s_free[pair_of(g)], 1)
                    evacuated(dve, g)
                if i == 24:
                    dve.wait_ge(s_t2c, 15)
                    evac_rows("lk", lambda t: stg2[:, t, :])
                if i == 32:
                    evac_rows("lv0", lambda t: vl[:, t, 0:2, :].rearrange("p h v -> p (h v)"))
                if (i - 8) % 2 == 0 and 0 <= (i - 8) // 2 < 2 * QH:
                    normalize2((i - 8) // 2)
            dve.wait_ge(s_yn2, 2 * QH)
            link(dve.tensor_tensor(E[0][:], yn[:, 0].rearrange("p h d -> p (h d)"), yn[:, 0].rearrange("p h d -> p (h d)"), ALU.mult))
            link(dve.tensor_reduce(ss_n[:, 0:8], E[0][:].rearrange("p (h d) -> p h d", h=QH), AX_X, ALU.add))
            link(dve.tensor_tensor(E[0][:], yn[:, 1].rearrange("p h d -> p (h d)"), yn[:, 1].rearrange("p h d -> p (h d)"), ALU.mult))
            link(dve.tensor_reduce(ss_n[:, 8:16], E[0][:].rearrange("p (h d) -> p h d", h=QH), AX_X, ALU.add))
            variance(ss_n, DK)
            dve.wait_ge(s_z, 3)
            link(dve.scalar_tensor_tensor(out=gz[:], in0=gz[:], scalar=0.0, in1=E[1][:], op0=ALU.min, op1=ALU.subtract))
            for h in range(GH):
                last = dve.tensor_tensor_scan(gb[:, h, :], ones[:], gz[:, h * T:(h + 1) * T], 0.0, ALU.mult, ALU.add)
            link(last)
            dve.memset(sT[:], 0.0).then_inc(s_gS, 1)
            evac_rows("lv1", lambda t: vl[:, t, 2:4, :].rearrange("p h v -> p (h v)"))
            gbf = gb[:].rearrange("p h t -> p (h t)")
            qf, kf = qlT[:].rearrange("p h t -> p (h t)"), klT[:].rearrange("p h t -> p (h t)")

            def halves(ap, L):
                return ap.rearrange("p (m two l) -> p m two l", two=2, l=L)

            def level_size(i):
                return 2 ** (LEVELS - i) if i < 8 else 128

            def level_diff(i):
                L = level_size(i)
                b_, e_ = halves(gbf, L), halves(E[i % 2][:], L)
                m = GH * T // (2 * L)
                ref = b_[:, :, 0, L - 1:L].to_broadcast([P, m, L])
                dve.tensor_tensor(e_[:, :, 0, :], ref, b_[:, :, 0, :], ALU.subtract)
                dve.tensor_tensor(e_[:, :, 1, :], b_[:, :, 1, :], ref, ALU.subtract).then_inc(s_gE, 1)

            def level_operand(i):
                L = level_size(i)
                dve.wait_ge(s_gX, i)
                if i >= 3:
                    dve.wait_ge(s_gP, 2 * (i - 1))
                e_, o_ = halves(E[i % 2][:], L), halves(QK[i % 2][:], L)
                dve.tensor_tensor(o_[:, :, 0, :], e_[:, :, 0, :], halves(kf, L)[:, :, 0, :], ALU.mult)
                dve.tensor_tensor(o_[:, :, 1, :], e_[:, :, 1, :], halves(qf, L)[:, :, 1, :], ALU.mult).then_inc(s_gQ, 1)

            def level_take(i):
                for h in range(TT if i < 8 else 1):
                    dve.wait_ge(s_gP, 2 * i + h + 1)
                    src = ps_m[2 + h][:].rearrange("p (g q) -> p g q", g=GH)
                    if i == 8:
                        dve.tensor_copy(sT[:, 2], src).then_inc(s_gS, 1)
                    else:
                        l = LEVELS if i == 0 else LEVELS - i
                        dve.wait_ge(s_gS, 2 * i + h + 1)
                        dve.copy_predicated(sT[:, h], lmask[:, l, :].unsqueeze(1).to_broadcast([P, GH, P]), src
                                            ).then_inc(s_gS, 1)

            dve.wait_ge(s_t2c, 19)
            level_diff(1)
            level_take(0)
            level_diff(2)
            for i in range(1, 9):
                level_operand(i)
                if i + 2 <= 8:
                    dve.wait_ge(s_gQ, i)
                    level_diff(i + 2)
                level_take(i)
                if i == 8:
                    g = G["lr1"]
                    psum_ready(dve, g)
                    for t in range(TT):
                        take(g, t, rl[:, t, T:T + NG], 0, NG).then_inc(s_free[pair_of(g)], 1)
                    evacuated(dve, g)
            rooted(ss_n)
            dve.tensor_tensor(yn[:], yn[:], ss_n.rearrange("p (t h) -> p t h", t=TT).unsqueeze(3).to_broadcast(
                [P, TT, QH, DK]), ALU.mult).then_inc(s_y2n, 1)
            for i in range(4):
                t, hp = divmod(i, 2)
                dve.wait_ge(s_go, i + 1)
                dve.tensor_copy(yg[:, t, 2 * hp:2 * hp + 2, :].rearrange("p h v -> p (h v)"), ps_m[2 + i % 2][:]
                                ).then_inc(s_goc, 1)
            evac_rows("lr2", lambda t: rl[:, t, 768:])
            dve.wait_ge(s_goc, 4)
            head_squares(yg[:], sc8[:], ss_g.rearrange("p (t h) -> p t h", t=TT))
            variance(ss_g, DV)
            dve.wait_ge(s_rl, 1)
            link(dve.tensor_tensor(yg[:].rearrange("p t h v -> p t (h v)"), yg[:].rearrange("p t h v -> p t (h v)"),
                                   rl[:], ALU.mult))
            rooted(ss_g)
            dve.tensor_tensor(yg[:], yg[:], ss_g.rearrange("p (t h) -> p t h", t=TT).unsqueeze(3).to_broadcast(
                [P, TT, GH, DV]), ALU.mult).then_inc(s_y2g, 1)
            build_dve(dve, "y2", A(aH), A(aL),
                      lambda k: cols[:, GNS:GNS + 1] if k < 8 else cols[:, GGL + k % 2:GGL + k % 2 + 1])

            def residual(name):
                g = G[name]
                j = int(name[-1])
                psum_ready(dve, g)
                for t in range(TT):
                    c = x[:, t, j * NG:(j + 1) * NG]
                    dve.tensor_tensor(c, c, ps_g[pair_of(g)][t][:], ALU.add).then_inc(s_free[pair_of(g)], 1)

            def mem_units(us):
                build_dve(dve, "mem", A(mH), A(mL), lambda k: cols[:, GME + k:GME + k + 1], only=us)

            residual("w2o0")
            residual("w2o1")
            mem_units(range(0, 3))
            residual("w2o2")
            mem_units(range(3, 8))
            residual("w2o3")
            if stop and stop[0] == "two":
                return

            dve.wait_ge(s_sqs, 2)
            variance(ss_m, D)
            rooted(ss_m)
            build_dve(dve, "hq", A(aH), A(aL), lambda k: cols[:, GC + k:GC + k + 1])
            dve.wait_ge(s_sqs, 4)
            variance(ss_x2, D)
            rooted(ss_x2)
            link(dve.tensor_scalar(colcq, cols[:, GCQ:GCQ + 1], float(DK) ** -0.5, None, ALU.mult))

            def cross_rows(name, scale, dst, sums, scratch):
                g = G[name]
                psum_ready(dve, g)
                for t in range(TT):
                    dve.tensor_scalar(dst[:, t].rearrange("p h d -> p (h d)"), ps_g[pair_of(g)][t][:], scale[:, t:t + 1],
                                      None, ALU.mult).then_inc(s_free[pair_of(g)], 1)
                evacuated(dve, g)
                head_squares(dst[:], scratch[:], sums.rearrange("p (t h) -> p t h", t=TT))
                variance(sums, DK)
                rooted(sums)
                dve.tensor_tensor(dst[:], dst[:], sums.rearrange("p (t h) -> p t h", t=TT).unsqueeze(3).to_broadcast(
                    [P, TT, MH, DK]), ALU.mult).then_inc(s_ckr, 1)

            cross_rows("mk", ss_m, ckn, ss_ck, scr4)
            cross_rows("mq", ss_x2, cqn, ss_cq, scr4)
            for u in range(MH):
                dve.wait_ge(s_sc3, u + 1)
                dve.tensor_reduce(mx3[:, u, :], ps_m[2][:].rearrange("p (t m) -> p t m", t=TT), AX_X, ALU.max,
                                  negate=True).then_inc(s_sm3, 1)
            g = G["mv"]
            psum_ready(dve, g)
            for t in range(TT):
                dve.tensor_scalar(cvn[:, t, :], ps_g[pair_of(g)][t][:], ss_m[:, t:t + 1], None,
                                  ALU.mult).then_inc(s_free[pair_of(g)], 1)
            for u in range(MH):
                dve.wait_ge(s_pv3, u + 1)
                link(dve.reciprocal(den3[:, u, :], den3[:, u, :]))
                for t in range(TT):
                    last = dve.tensor_scalar(ocn[:, t, u, :], ps_m[1][:, t * P:(t + 1) * P], den3[:, u, t:t + 1], None,
                                             ALU.mult)
                last.then_inc(s_on, 1)
            build_dve(dve, "oc", A(ocH), A(ocL))
            for i in range(4):
                residual(f"co{i}")
            if stop and stop[0] == "three":
                return

            build_dve(dve, "hf", A(aH), A(aL), lambda k: cols[:, GF + k:GF + k + 1])
            dve.wait_ge(s_sqs, 6)
            variance(ss_x3, D)
            roots[0] += 1
            dve.wait_ge(s_sqrt, roots[0])
            dve.reciprocal(ss_x3, ss_x3).then_inc(s_ffs, 1)
            dve.wait_ge(s_ffs, 1)
            for part, (g0, n) in enumerate(PARTS):
                def hidden(i):
                    build_dve(dve, f"gu{i}", A(guH, 4 * (i - g0)), A(guL, 4 * (i - g0)))
                for i in range(g0, g0 + n):
                    if i > g0:
                        hidden(i - 1)
                    g = G[f"fu{i}"]
                    evacuated(dve, G[f"fg{i}"])
                    psum_ready(dve, g)
                    if i >= 1:
                        dve.wait_ge(s_xt, built(f"gu{i - 1}", 4))
                    for t in range(TT):
                        dve.scalar_tensor_tensor(out=hn[:, t, :], in0=ps_g[pair_of(g)][t][:], scalar=ss_x3[:, t:t + 1],
                                                 in1=sg[:, t, :], op0=ALU.mult, op1=ALU.mult
                                                 ).then_inc(s_free[pair_of(g)], 1)
                hidden(g0 + n - 1)
                for i in range(4):
                    residual(f"fd{part}{i}")


_INS = ["x", "w_in", "b_in", "conv_w", "conv_b", "conv_ln_g", "conv_ln_b", "sinks", "w_out", "b_out", "ln_g", "ln_b",
        "mem_2", "g_mix_2", "w_in_2", "b_nsa_gate_2", "g_q_2", "g_kc_2", "g_ks_2", "g_kw_2", "pe_k_2", "pe_v_2",
        "w_ck1_2", "w_ck2_2", "w_cv1_2", "w_cv2_2", "g_nsa_out_2", "w_gk2_2", "b_gk_2", "g_gla_out_2", "w_out_2",
        "g_cross_2", "g_mem_2", "w_cq_2", "w_ck_2", "w_cv_2", "g_cq_2", "g_ck_2", "w_co_2", "g_ffn_2", "w_gu_2",
        "w_down_2"]


def kernel(**inputs):
    import numpy as _np
    import concourse.bacc as _bacc
    from concourse import mybir as _mybir
    from concourse.bass_utils import run_bass_kernel_spmd as _run

    nc = _bacc.Bacc("TRN2", target_bir_lowering=False, num_devices=1)
    arrays, args = {}, {}
    for name in _INS:
        v = _np.ascontiguousarray(inputs[name])
        arrays[f"in_{name}_dram"] = v
        args[name] = nc.dram_tensor(f"in_{name}_dram", v.shape, _mybir.dt.from_np(v.dtype), kind="ExternalInput").ap()
    out = nc.dram_tensor("out_0_dram", (1, T, D), F32, kind="ExternalOutput").ap()
    stack_kernel(nc, args, out)
    r = _run(nc, [arrays], core_ids=[0])
    return r.results[0]["out_0_dram"]
```

```python
from contextlib import ExitStack

import concourse.bass as bass
from concourse import mybir

P = 128
ALU = mybir.AluOpType
ACT = mybir.ActivationFunctionType
F32 = mybir.dt.float32
F32R = mybir.dt.float32r
I32 = mybir.dt.int32
U8 = mybir.dt.uint8
AX_X = mybir.AxisListType.X

T = 256
TT = T // P
D = 2048
KT = D // P
NG = 512
STEP = 2
CHUNK = 4
LEAD = 3
NSLOT = 4
NRAW = 4

C = 1024
TAPS = 31
HEADS = 16
HD = 64
KVH = 2
ALPHA = 2.0 ** 0.25
LN_EPS = 1e-5
NEG = -1e30
EPS = 1e-6
QH = 8
DK = 128
NCMP = (T - 32) // 16 + 1
CMP_LEN = 32
GH = 4
DV = 256
MH = 4
FF = 5632
SEL_BLOCK, SEL_TOP, NSA_WINDOW = 64, 16, 512
assert T // SEL_BLOCK <= SEL_TOP and T <= NSA_WINDOW
LEVELS = 7

KIB = 1024


def stack_kernel(nc, a, out):
    w_in, w_out, w_in2, w_out2 = a["w_in"][0], a["w_out"][0], a["w_in_2"][0], a["w_out_2"][0]

    groups = []

    def group(name, w, col, n, kt=KT, k0=0):
        groups.append(dict(name=name, w=w, col=col, n=n, kt=kt, k0=k0))

    for name, col, n in (("cv0", 0, 512), ("cg0", C, 512), ("cv1", 512, 512), ("cg1", C + 512, 512),
                         ("q0", 3 * C, 512), ("q1", 3 * C + 512, 512), ("kv", 4 * C, 256),
                         ("ga0", 2 * C, 512), ("ga1", 2 * C + 512, 512),
                         ("ag0", 4 * C + 256, 512), ("ag1", 4 * C + 768, 512)):
        group(name, w_in, col, n)
    for j in range(4):
        group(f"wo{j}", w_out, NG * j, NG)
    for name, col, n in (("nq0", 0, 512), ("nq1", 512, 512), ("ncmp", 1024, 512), ("nslc", 1536, 512),
                         ("nwin", 2048, 512), ("glq0", 2560, 280), ("lq1", 2840, 256),
                         ("lar0", 4632, 272), ("lk", 3096, 512), ("lv0", 3608, 512), ("lv1", 4120, 512),
                         ("lr1", 4904, 512), ("lr2", 5416, 256)):
        group(name, w_in2, col, n)
    for j in range(4):
        group(f"w2o{j}", w_out2, NG * j, NG)
    group("mk", a["w_ck_2"][0], 0, NG)
    group("mq", a["w_cq_2"][0], 0, NG)
    group("mv", a["w_cv_2"][0], 0, NG)
    for j in range(4):
        group(f"co{j}", a["w_co_2"][0], NG * j, NG, kt=4)
    PARTS = ((0, 6), (6, 5))
    for part, (g0, n) in enumerate(PARTS):
        for j in range(g0, g0 + n):
            group(f"fg{j}", a["w_gu_2"][0], NG * j, NG)
            group(f"fu{j}", a["w_gu_2"][0], FF + NG * j, NG)
        for j in range(4):
            group(f"fd{part}{j}", a["w_down_2"][0], NG * j, NG, kt=4 * n, k0=4 * g0)
    at_step = 0
    for i, g in enumerate(groups):
        g["i"], g["s0"], g["ns"] = i, at_step, g["kt"] // STEP
        at_step += g["ns"]
    G = {g["name"]: g for g in groups}
    chunks = []
    for g in groups:
        for c in range(g["kt"] // CHUNK):
            src = g["w"].rearrange("(k p) n -> p k n", p=P)[
                :, g["k0"] + CHUNK * c:g["k0"] + CHUNK * (c + 1), g["col"]:g["col"] + g["n"]]
            chunks.append(dict(src=src, n=g["n"], k=CHUNK, step=g["s0"] + 2 * c, group=g))
            g.setdefault("c0", len(chunks) - 1)
        if g["name"] == "nslc":
            for w in ("w_ck1_2", "w_cv1_2"):
                for c in range(4):
                    src = a[w][0].rearrange("(k p) n -> p k n", p=P)[:, 8 * c:8 * c + 8, :]
                    chunks.append(dict(src=src, n=256, k=8, step=None, group=None,
                                       direct=sum(x["step"] is None for x in chunks)))
    direct_chunks = [i for i, c in enumerate(chunks) if c["step"] is None]
    chunk_of_step = {}
    for i, c in enumerate(chunks):
        if c["step"] is not None:
            chunk_of_step[c["step"]] = chunk_of_step[c["step"] + 1] = i
    n_steps = at_step
    step_cols = [g["n"] for g in groups for _ in range(g["ns"])]

    with ExitStack() as ctx:
        def sem(name):
            return ctx.enter_context(nc.semaphore(name))

        def place(name, kib, shape, dt=F32):
            return nc.alloc_sbuf_tensor_at(name, shape, dt, offset=int(kib * KIB))

        BASE = -(-nc.sbuf_base // 64) * 64
        ctx.enter_context(nc.sbuf_tensor("fence", [P, (nc.sbuf_usable_end - BASE) // 4 - 16], F32))
        at0 = BASE / KIB

        def put(name, kib, shape, dt=F32):
            return place(name, at0 + kib, shape, dt)

        raw = put("raw", 0, [P, NRAW, CHUNK * NG])
        hi = put("hi", 32, [P, NSLOT, STEP * NG], F32R)
        lo = put("lo", 48, [P, NSLOT, STEP * NG], F32R)
        x = put("x", 64, [P, TT, D])
        aH = put("aH", 80, [P, KT, T], F32R)
        aL = put("aL", 96, [P, KT, T], F32R)

        small, small_at = [168 * KIB], {}

        def const(name, shape, dt=F32):
            n = 1
            for s in shape[1:]:
                n *= s
            off = small[0]
            small_at[name] = off / KIB
            small[0] += -(-n * (1 if dt == U8 else 4) // 32) * 32
            return put(name, off / KIB, shape, dt)

        ident = const("ident", [P, P])
        ones = const("ones", [P, T])
        NCOL = 101
        cols = const("cols", [P, 229])
        convw = const("convw", [P, 8, 32])
        sinks = const("sinks", [P, HEADS])
        bias = const("bias", [P, 2, NG])
        mask1 = const("mask1", [P, 3 * P])
        dist2 = const("dist2", [P, 3 * P])
        distc = const("distc", [P, TT, 16])
        visc = const("visc", [P, TT])
        lmask = const("lmask", [P, LEVELS + 1, P], U8)
        bgate = const("bgate", [P, 24])
        stat = const("stat", [P, 64])
        bnst = const("bnst", [P, TT, 4, 6])
        mv = const("mv", [P, TT, 2])
        assert small[0] <= nc.sbuf_usable_end - BASE, (small[0], nc.sbuf_usable_end - BASE)

        ps_g = [[ctx.enter_context(nc.psum_tensor(f"ps_g{p}{t}", [P, NG], F32)) for t in range(TT)]
                for p in range(2)]
        ps_m = [ctx.enter_context(nc.psum_tensor(f"ps_m{i}", [P, NG], F32)) for i in range(4)]

        s_raw = [sem(f"raw_landed{i}") for i in range(NRAW)]
        s_hi = sem("hi_ready")
        s_lo = sem("lo_ready")
        s_used = sem("steps_multiplied")
        s_direct = sem("direct_chunks_multiplied")
        s_free = [sem(f"pair{p}_evacuated") for p in range(2)]

        s_x = sem("x_landed")
        s_par = sem("params_landed")
        s_bias = [sem(f"bias_landed{i}") for i in range(2)]
        s_pool = sem("constants_made")
        s_xt = sem("transposed")
        s_xh = sem("operand_hi")
        s_xl = sem("operand_lo")
        s_dve = sem("dve_own_results")
        s_act = sem("act_own_scratch")

        block = ctx.enter_context(nc.Block())

        def plus(later, per_iteration):
            return 0 if later is None else later[0] * per_iteration

        def plus_steps(later):
            return 0 if later is None else later[0] * later[1]

        def wait_raw(e, chunk, later=None):
            turns = 0 if later is None else plus(later, 16 * later[1] // (CHUNK // STEP * NRAW))
            e.wait_ge(s_raw[chunk % NRAW], 16 * (chunk // NRAW + 1) + turns)

        def step_view(buf, s):
            n = step_cols[s]
            return buf[:, s % NSLOT, :STEP * n]

        def raw_view(s):
            c, n = chunk_of_step[s], step_cols[s]
            half = (s - chunks[c]["step"]) * STEP * n
            return raw[:, c % NRAW, half:half + STEP * n]

        def pair_of(g):
            return g["i"] % 2

        def evacuated(e, g, later=None):
            e.wait_ge(s_free[pair_of(g)], TT * (g["i"] // 2 + 1) + plus(later, TT))

        def psum_ready(e, g, later=None):
            e.wait_ge(s_used, g["s0"] + g["ns"] + plus_steps(later))

        builds = {}
        unit_at = 0
        for name, n in (("x", 8), ("yattn", 4), ("h", 8), ("y2", 16 // 2), ("mem", 8), ("hq", 8), ("oc", 2), ("hf", 8)):
            builds[name] = (unit_at, n)
            unit_at += n
        for j in range(FF // NG):
            builds[f"gu{j}"] = (unit_at, 2)
            unit_at += 2

        UNITS_GU = NG // P // 2

        def build_bank(name, u):
            return ps_m[u if name.startswith("gu") else (builds[name][0] + u) % 4]

        def build_pe(pe, name, src, before=None, only=None, later=None):
            u0, n = builds[name]
            turn = UNITS_GU if name.startswith("gu") else 4
            for u in (range(n) if only is None else only):
                if u0 + u >= turn:
                    pe.wait_ge(s_xl, u0 + u - turn + 1 + plus(later, UNITS_GU))
                    if before is not None:
                        before(u)
                elif before is not None:
                    before(u)
                for k in range(2):
                    for t in range(TT):
                        last = pe.transpose(build_bank(name, u)[:, (2 * k + t) * P:(2 * k + t + 1) * P],
                                            src(2 * u + k, t), ident[:])
                last.then_inc(s_xt, 1)

        def build_act(act, name, dst, gain=None, before=None, only=None, later=None, offset=None):
            u0, n = builds[name]
            for u in (range(n) if only is None else only):
                act.wait_ge(s_xt, u0 + u + 1 + plus(later, UNITS_GU))
                if before is not None:
                    before(u)
                bank = build_bank(name, u)
                if gain is None:
                    act.copy(dst(2 * u, 2).rearrange("p k t -> p (k t)"), bank[:]).then_inc(s_xh, 1)
                else:
                    for k in range(2):
                        dst_k, src_k = dst(2 * u + k, 1).rearrange("p k t -> p (k t)"), bank[:, k * T:(k + 1) * T]
                        if offset is None:
                            last = act.activation(dst_k, src_k, ACT.Copy, scale=gain(2 * u + k))
                        else:
                            last = act.activation(dst_k, src_k, ACT.Identity, scale=gain(2 * u + k),
                                                  bias=offset(2 * u + k))
                    last.then_inc(s_xh, 1)

        def build_dve(dve, name, dst_hi, dst_lo, gain=None, only=None, later=None):
            u0, n = builds[name]
            for u in (range(n) if only is None else only):
                dve.wait_ge(s_xh, u0 + u + 1 + plus(later, UNITS_GU))
                bank = build_bank(name, u)
                if gain is None:
                    dve.tensor_tensor(dst_lo(2 * u, 2).rearrange("p k t -> p (k t)"), bank[:],
                                      dst_hi(2 * u, 2).rearrange("p k t -> p (k t)").bitcast(F32),
                                      ALU.subtract).then_inc(s_xl, 1)
                else:
                    for k in range(2):
                        last = dve.scalar_tensor_tensor(
                            out=dst_lo(2 * u + k, 1).rearrange("p k t -> p (k t)"), in0=bank[:, k * T:(k + 1) * T],
                            scalar=gain(2 * u + k), in1=dst_hi(2 * u + k, 1).rearrange("p k t -> p (k t)").bitcast(F32),
                            op0=ALU.mult, op1=ALU.subtract)
                    last.then_inc(s_xl, 1)

        def built(name, k_tiles_done):
            return builds[name][0] + k_tiles_done // 2

        def A(buf, k0=0):
            return lambda k, n: buf[:, k0 + k:k0 + k + n, :]

        def A_at(buf, k0):
            return lambda k, n: buf[:, bass.ds(k0 + k, n), :]

        def gemm(pe, g, j, opH, opL, before=None, later=None):
            s = g["s0"] + j
            if j == 0 and g["i"] >= 2:
                pe.wait_ge(s_free[pair_of(g)], TT * (g["i"] // 2) + plus(later, TT))
            if before is not None:
                before(j)
            pe.wait_ge(s_hi, s + 1 + plus_steps(later))
            pe.wait_ge(s_lo, s + 1 + plus_steps(later))
            n = g["n"]
            for k in range(STEP):
                wh = step_view(hi, s)[:, k * n:(k + 1) * n]
                wl = step_view(lo, s)[:, k * n:(k + 1) * n]
                kk = STEP * j + k
                first, final = kk == 0, kk == g["kt"] - 1
                for t in range(TT):
                    dst = ps_g[pair_of(g)][t][:, :n]
                    xh = opH(kk, 1)[:, 0, t * P:(t + 1) * P]
                    xl = opL(kk, 1)[:, 0, t * P:(t + 1) * P]
                    pe.matmul(dst, xh, wh, start=first, stop=False)
                    pe.matmul(dst, xh, wl, start=False, stop=False)
                    last = pe.matmul(dst, xl, wh, start=False, stop=final)
            last.then_inc(s_used, 1)

        def split_hi(act, s, later=None):
            if s >= n_steps:
                return
            wait_raw(act, chunk_of_step[s], later)
            if s >= NSLOT:
                act.wait_ge(s_used, s - NSLOT + 1 + plus_steps(later))
            act.copy(step_view(hi, s), raw_view(s)).then_inc(s_hi, 1)

        def split_lo(pool, s, later=None):
            pool.wait_ge(s_hi, s + 1 + plus_steps(later))
            if s >= NSLOT:
                pool.wait_ge(s_used, s - NSLOT + 1 + plus_steps(later))
            pool.tensor_tensor(step_view(lo, s), raw_view(s), step_view(hi, s).bitcast(F32),
                               ALU.subtract).then_inc(s_lo, 1)

        bias_groups = ["cv0", "cg0", "cv1", "cg1", "q0", "q1", "kv", "ga0", "ga1", "ag0", "ag1",
                       "wo0", "wo1", "wo2", "wo3"]
        bias_used = sem("output_bias_added")

        def bias_slot(e, name):
            i = bias_groups.index(name)
            e.wait_ge(s_bias[i % 2], 16 * (i // 2 + 1))
            return bias[:, i % 2, :G[name]["n"]]

        q_sb = put("q_sb", 112, [P, TT, C])
        qT = put("qT", 120, [P, 8, T])
        c_h = put("c_h", 128, [P, TT, C])
        gT = put("gT", 128, [P, 8, T])
        hT = put("hT", 136, [P, 8, T + TAPS - 1])
        cT = put("cT", 145.25, [P, 8, T])
        stg = put("stg", 153.25, [P, TT, NG])
        h_lin = put("h_lin", 153.25, [P, NG])
        kT = put("kT", 157.25, [P, KVH, T])
        v_sb = put("v_sb", 159.25, [P, TT, P])
        sS = put("sS", 160.25, [P, 2, 3 * P])
        pT = put("pT", 163.25, [P, 2, 3 * P])
        k_dup = put("k_dup", 163.25, [P, TT, KVH, 2, HD])
        mx = put("mx", 166.25, [P, HEADS, 2])
        den = put("den", 166.375, [P, HEADS, 2])
        esk = put("esk", 166.5, [P, HEADS, 2])
        rden = put("rden", 166.625, [P, HEADS, 2])
        mean_sb = put("mean_sb", 166.75, [P, T])
        rstd_sb = put("rstd_sb", 144, [P, T])
        sq_sb = put("sq_sb", 136, [P, 8, T])
        ycH = put("ycH", 136, [P, 8, T], F32R)
        ycL = put("ycL", 181.75, [P, 8, T], F32R)
        param_rows = put("param_rows", 112, [P, P])
        pe_rows = put("pe_rows", 112.5, [96, P])
        cw_rows = put("cw_rows", 113, [TAPS, C])

        CB, CLG, CLB, GM, GC, GME, GF, BGK, GQ, GKC, GKS, GKW, GCQ, GCK = (
            0, 8, 16, 24, 40, 56, 72, 88, 92, 93, 94, 95, 96, 97)
        GNS, GGL = 98, 99
        PEK, PEV, LNG, LNB, HG, HB = 101, 133, 165, 181, 197, 213
        row_loads = [("conv_b", CB, 8), ("conv_ln_g", CLG, 8), ("conv_ln_b", CLB, 8), ("g_mix_2", GM, 16),
                     ("g_cross_2", GC, 16), ("g_mem_2", GME, 16), ("g_ffn_2", GF, 16), ("b_gk_2", BGK, 4),
                     ("g_q_2", GQ, 1), ("g_kc_2", GKC, 1), ("g_ks_2", GKS, 1), ("g_kw_2", GKW, 1),
                     ("g_cq_2", GCQ, 1), ("g_ck_2", GCK, 1), ("g_nsa_out_2", GNS, 1), ("g_gla_out_2", GGL, 2)]
        N_PAR = 16 * (len(row_loads) + 4 + 1 + 1 + 1 + 2)

        s_cols = sem("param_columns_in_psum")
        s_colsb = sem("param_columns_ready")
        s_stga = sem("staged_through_act")
        s_ch = sem("conv_input_ready")
        s_cht = sem("conv_input_transposed")
        s_pad = sem("conv_input_padded")
        s_hT = sem("conv_input_T_ready")
        s_conv = sem("conv_taps")
        s_qt = sem("qk_transposed")
        s_qT = sem("qk_T_ready")
        s_sc = sem("scores")
        s_sm = sem("scores_shifted")
        s_exp = sem("exp_done")
        s_pt = sem("probs_transposed")
        s_pTc = sem("probs_T_ready")
        s_pv = sem("pv_done")
        s_yn = sem("pv_normalized")
        s_yat = sem("attn_gated")
        s_gat = sem("gate_transposed")
        s_gT = sem("gate_T_ready")
        s_lns = sem("conv_ln_sums")
        s_lnc = sem("conv_ln_steps")
        s_lna = sem("conv_ln_act")
        s_ych = sem("y_conv_hi")
        s_ycl = sem("y_conv_lo")
        s_xn = sem("rows_normalized")
        s_x1 = sem("x_updated")
        s_out = sem("out_stored")

        ln_rows = put("ln_rows", 190, [P, 2, D])

        yn = put("yn", 112, [P, TT, QH, DK])
        yg = put("yg", 120, [P, TT, GH, DV])
        pc = put("pc", 120, [P, TT, QH, 32])
        pTc = put("pTc", 122, [P, TT, KVH, P])
        hid = put("hid", 124, [2 * NCMP, 512])
        kcn = put("kcn", 126, [2 * NCMP, DK])
        kcT15 = put("kcT15", 126.5, [P, 2 * NCMP])
        aT = put("aT", 127, [16, T])
        nqT = put("nqT", 128, [P, QH, T])
        ksT = put("ksT", 136, [P, KVH, T])
        kwT = put("kwT", 138, [P, KVH, T])
        vs = put("vs", 140, [P, TT, KVH * DK])
        vw = put("vw", 142, [P, TT, KVH * DK])
        kcT = put("kcT", 144, [P, KVH, T])
        vcT = put("vcT", 146, [P, KVH, T])
        kp = put("kp", 148, [P, 2, 32, KVH, NCMP])
        qlT = put("qlT", 156, [P, GH, T])
        klT = put("klT", 160, [P, GH, T])
        vc_bd = put("vc_bd", 160, [P, KVH, 4, DK])
        hidTk = put("hidTk", 164, [P, 2, 32])
        hidTv = put("hidTv", 165, [P, 2, KVH, 4, 32])
        gb = put("gb", 164, [P, GH, T])
        nq = put("nq", 181.75, [P, TT, QH, DK])
        rl = put("rl", 181.75, [P, TT, 1024])
        vl = put("vl", 189.75, [P, TT, GH, DV])
        sS2 = put("sS2", 197.75, [P, 2, 3 * P])
        pT2 = put("pT2", 200.75, [P, 2, 3 * P])
        sT = put("sT", 197.75, [P, 3, GH, P])
        stg2 = put("stg2", 203.75, [P, TT, NG])
        E = [put(f"E{i}", 128 + 4 * i, [P, GH * T]) for i in range(2)]
        QK = [put(f"QK{i}", 148 + 4 * i, [P, GH * T]) for i in range(2)]
        off_bias = small_at["bias"]
        w_gk2 = put("w_gk2", off_bias, [16, 512])
        w_c2 = put("w_c2", off_bias + 2, [P, 2, 2, DK])
        gates = const("gates", [P, TT, 24])
        st2 = const("st2", [P, 160])

        HIDTV_CLEARED = 1
        gz = put("gz", 144, [P, GH * T])
        sq_row = put("sq_row", 181.75, [P, D])
        sq_c = put("sq_c", 127, [2 * NCMP, DK])
        sc8 = put("sc8", 128, [P, TT, GH, DV])
        mx2, den2 = st2[:, 0:32].rearrange("p (u t) -> p u t", t=2), st2[:, 32:64].rearrange("p (u t) -> p u t", t=2)
        rden2 = st2[:, 64:96].rearrange("p (u t) -> p u t", t=2)
        ss_n = st2[:, 96:112]
        mxc = st2[:, 112:128]
        rc = st2[:, 128:144]
        denc = st2[:, 144:160]
        var_ln = stat[:, 0:2]
        ss = stat[:, 2:4]
        ss_q = stat[:, 4:20].rearrange("p (a b) -> p a b", a=2)
        ss_k = stat[:, 20:28].rearrange("p (a b) -> p a b", a=2)
        ss_c = stat[0:2 * NCMP, 28:29]
        ss_g = stat[:, 29:37]
        colq = stat[:, 37:38]
        mean_ln = stat[:, 38:40]

        memn = put("memn", 128, [P, TT, D])
        mH = put("mH", 144, [P, KT, T], F32R)
        mL = put("mL", 181.75, [P, KT, T], F32R)
        sq_m = put("sq_m", 112, [P, D])
        ckn = put("ckn", 197.75, [P, TT, MH, DK])
        cvn = put("cvn", 201.75, [P, TT, MH * DK])
        cqn = put("cqn", 112, [P, TT, MH, DK])
        scr4 = put("scr4", 116, [P, TT, MH, DK])
        ocn = put("ocn", 116, [P, TT, MH, DK])
        ckT = put("ckT", 120, [P, MH, T])
        cqT = put("cqT", 124, [P, MH, T])
        sS3 = put("sS3", 128, [P, MH, TT, T])
        pT3 = put("pT3", 136, [P, MH, TT, TT, P])
        ocH = put("ocH", 144, [P, 4, T], F32R)
        ocL = put("ocL", 148, [P, 4, T], F32R)
        guH = put("guH", 112, [P, 24, T], F32R)
        guL = put("guL", 136, [P, 24, T], F32R)
        sg = put("sg", 160, [P, TT, NG])
        hn = put("hn", 164, [P, TT, NG])
        st3 = stat[:, 40:64]
        ss_m, ss_x2, ss_x3, colcq = st3[:, 0:2], st3[:, 2:4], st3[:, 4:6], st3[:, 6:7]
        ss_ck, ss_cq = st3[:, 8:16], st3[:, 16:24]
        mx3, den3 = st2[:, 0:8].rearrange("p (u t) -> p u t", t=2), st2[:, 8:16].rearrange("p (u t) -> p u t", t=2)
        s_ckr = sem("cross_rows_ready")
        s_sc3 = sem("cross_scores")
        s_sm3 = sem("cross_maxima")
        s_exp3 = sem("cross_exp")
        s_pt3 = sem("cross_probs_transposed")
        s_pTc3 = sem("cross_probs_T_ready")
        s_pv3 = sem("cross_pv")
        s_on = sem("cross_normalized")
        s_sqs = sem("squares_scratch")
        s_ffs = sem("ffn_scale_ready")
        sq_f = put("sq_f", 136, [P, D])

        s_var = sem("variances")
        s_sqrt = sem("square_roots")
        s_ss = sem("row_squares_summed")
        s_p2 = sem("layer_two_small_weights_landed")
        s_t2 = sem("bank0_written")
        s_t2c = sem("bank0_copied")
        s_t2s = sem("bank0_source_ready")
        s_kp = sem("compress_operands")
        s_hid = sem("compress_hidden")
        s_c2 = sem("compressed_in_psum")
        s_c2v = sem("compressed_values_ready")
        s_csc = sem("cmp_scores")
        s_csm = sem("cmp_scores_shifted")
        s_cexp = sem("cmp_exp")
        s_cpv = sem("cmp_pv")
        s_cyn = sem("cmp_normalized")
        s_gsig = sem("gates_ready")
        s_sc2 = sem("scores2")
        s_sm2 = sem("scores2_shifted")
        s_exp2 = sem("exp2_done")
        s_pt2 = sem("probs2_transposed")
        s_pTc2 = sem("probs2_T_ready")
        s_pv2 = sem("pv2_done")
        s_yn2 = sem("pv2_normalized")
        s_z = sem("gate_z_parts")
        s_gE = sem("level_exponents")
        s_gX = sem("level_decays")
        s_gQ = sem("level_operands")
        s_gP = sem("level_products")
        s_gS = sem("level_scores_taken")
        s_go = sem("gla_out")
        s_goc = sem("gla_out_copied")
        s_y2n = sem("nsa_rows_ready")
        s_y2g = sem("gla_rows_ready")
        s_rl = sem("gla_gate_ready")
        s_mem = sem("mem_landed")

        conv_units = 8 * TAPS
        LNC_READ_SUMS = 3
        n_dve = [0]

        @block.sync
        def _(sp):
            sp.dma_start(x[:, 0, :], a["x"][0, 0:P, :]).then_inc(s_x, 16)
            sp.dma_start(x[:, 1, :], a["x"][0, P:T, :]).then_inc(s_x, 16)
            params = [(param_rows[r0:r0 + n, :], a[name][0].rearrange("(r c) -> r c", c=P))
                      for name, r0, n in row_loads]
            params += [(pe_rows[0:32, :], a["pe_k_2"][0]), (pe_rows[32:64, :], a["pe_v_2"][0]),
                       (pe_rows[64:80, :], a["ln_g"][0].rearrange("(r c) -> r c", c=P)),
                       (pe_rows[80:96, :], a["ln_b"][0].rearrange("(r c) -> r c", c=P)),
                       (cw_rows[:, :], a["conv_w"][0]), (sinks[:], a["sinks"][0].partition_broadcast(P)),
                       (ln_rows[:, 0, :], a["ln_g"][0].partition_broadcast(P)),
                       (ln_rows[:, 1, :], a["ln_b"][0].partition_broadcast(P)),
                       (bgate[:], a["b_nsa_gate_2"][0].partition_broadcast(P))]

            def load(c, src=None, later=None):
                ch = chunks[c]
                if c >= NRAW:
                    old = chunks[c - NRAW]
                    if old["step"] is None:
                        sp.wait_ge(s_direct, old["direct"] + 1)
                    else:
                        sp.wait_ge(s_lo, old["step"] + 2 + plus_steps(later))
                sp.dma_start(raw[:, c % NRAW, :ch["k"] * ch["n"]].rearrange("p (k n) -> p k n", k=ch["k"]),
                             ch["src"] if src is None else src).then_inc(s_raw[c % NRAW], 16)

            for c, ch in enumerate(chunks[:G["fg0"]["c0"]]):
                g = ch["group"]
                if g is not None and g["name"] == "w2o2" and c == g["c0"]:
                    sp.wait_ge(s_xl, built("y2", KT))
                    sp.dma_start(memn[:], a["mem_2"][0].rearrange("(t p) d -> p t d", p=P)).then_inc(s_mem, 16)
                if g is not None and g["name"] == "nq1" and c == g["c0"]:
                    sp.wait_ge(bias_used, 4)
                    sp.dma_start(w_gk2[:], a["w_gk2_2"][0]).then_inc(s_p2, 16)
                    for i, w in enumerate(("w_ck2_2", "w_cv2_2")):
                        sp.dma_start(w_c2[:, i], a[w][0].rearrange("(k p) n -> p k n", p=P)).then_inc(s_p2, 16)
                if g is not None and g["name"] in bias_groups and c == g["c0"]:
                    i = bias_groups.index(g["name"])
                    if i >= 2 and i < 13:
                        evacuated(sp, G[bias_groups[i - 2]])
                    if i >= 13:
                        sp.wait_ge(bias_used, i - 12)
                    b = a["b_in"][0] if g["w"] is w_in else a["b_out"][0]
                    sp.dma_start(bias[:, i % 2, :g["n"]], b[g["col"]:g["col"] + g["n"]].partition_broadcast(P)
                                 ).then_inc(s_bias[i % 2], 16)
                load(c)
                if c < 5:
                    for dst, src in params[6 * c:6 * c + 6]:
                        sp.dma_start(dst, src).then_inc(s_par, 16)

            def load_groups(names, it):
                two = [G[name] for name in names]
                steps = sum(g["ns"] for g in two)
                for g in two:
                    w = g["w"].rearrange("(k p) n -> p k n", p=P)
                    for c in range(g["kt"] // CHUNK):
                        k = g["k0"] + CHUNK * c
                        further = NG if names[0].startswith("fg") else 2 * NG
                        load(g["c0"] + c, w[:, k:k + CHUNK, bass.ds(g["col"] + it * further, NG)], (it, steps))

            for part, (g0, n) in enumerate(PARTS):
                with sp.Fori(0, n) as it:
                    load_groups((f"fg{g0}", f"fu{g0}"), it)
                if n * 2 % NRAW == 0:
                    with sp.Fori(0, 2) as it:
                        load_groups((f"fd{part}0", f"fd{part}1"), it)
                else:
                    for c in range(G[f"fd{part}0"]["c0"], G[f"fd{part}3"]["c0"] + n):
                        load(c)
            for j in range(4):
                evacuated(sp, G[f"fd1{j}"])
                sp.dma_start(out[0].rearrange("(t p) d -> p t d", p=P)[:, :, j * NG:(j + 1) * NG],
                             x[:, :, j * NG:(j + 1) * NG]).then_inc(s_out, 16)
            sp.wait_ge(s_out, 4 * 16)

        iot = put("iot", 189.75, [P, 2, P], I32)
        xorf = put("xorf", 190.75, [P, P])
        ge = put("ge", 191.25, [P, LEVELS + 1, P])
        tri = put("tri", 195.25, [P, P])
        @block.gpsimd
        def _(pool):
            k = [0]

            def own(ins):
                k[0] += 1
                ins.then_inc(s_pool, 1)
                pool.wait_ge(s_pool, k[0])

            own(pool.memset(ident[:], 0.0))
            own(pool.affine_select(out=ident[:], in_=ident[:], compare_op=ALU.not_equal, fill=1.0, base=0,
                                   pattern=[[-1, P]], channel_multiplier=1))

            def window_mask():
                pool.memset(ones[:], 1.0)
                own(pool.memset(mask1[:], 0.0))
                own(pool.affine_select(out=mask1[:, 0:P], in_=mask1[:, 0:P], compare_op=ALU.is_ge, fill=NEG, base=0,
                                       pattern=[[-1, P]], channel_multiplier=1))
                own(pool.affine_select(out=mask1[:, P:], in_=mask1[:, P:], compare_op=ALU.is_gt, fill=NEG, base=0,
                                       pattern=[[1, 2 * P]], channel_multiplier=-1))
                own(pool.affine_select(out=mask1[:, P:], in_=mask1[:, P:], compare_op=ALU.is_ge, fill=NEG, base=P,
                                       pattern=[[-1, 2 * P]], channel_multiplier=1))

            def layer_two_constants():
                pool.wait_ge(s_x1, 4)
                own(pool.iota(dist2[:, 0:P], [[1, P]], base=0, channel_multiplier=-1,
                              allow_small_or_imprecise_dtypes=True))
                own(pool.iota(dist2[:, P:], [[1, 2 * P]], base=-P, channel_multiplier=-1,
                              allow_small_or_imprecise_dtypes=True))
                own(pool.affine_select(out=dist2[:, 0:P], in_=dist2[:, 0:P], compare_op=ALU.is_ge, fill=-1e33, base=0,
                                       pattern=[[-1, P]], channel_multiplier=1))
                own(pool.affine_select(out=dist2[:, P:], in_=dist2[:, P:], compare_op=ALU.is_ge, fill=-1e33, base=P,
                                       pattern=[[-1, 2 * P]], channel_multiplier=1))
                pool.iota(iot[:, 0, :], [[1, P]], base=0, channel_multiplier=0)
                own(pool.iota(iot[:, 1, :], [[0, P]], base=0, channel_multiplier=1))
                own(pool.iota(distc[:], [[-P, TT], [16, 16]], base=0, channel_multiplier=-1,
                              allow_small_or_imprecise_dtypes=True))
                own(pool.tensor_scalar(distc[:], distc[:], 15.5, 1.0, ALU.add, ALU.mult))
                own(pool.affine_select(out=distc[:], in_=distc[:], compare_op=ALU.is_ge, fill=-1e33, base=-31,
                                       pattern=[[P, TT], [-16, 16]], channel_multiplier=1))
                own(pool.memset(visc[:], 1.0))
                own(pool.affine_select(out=visc[:], in_=visc[:], compare_op=ALU.is_ge, fill=0.0, base=-31,
                                       pattern=[[P, TT]], channel_multiplier=1))
                own(pool.memset(tri[:], 1.0))
                own(pool.affine_select(out=tri[:], in_=tri[:], compare_op=ALU.is_gt, fill=0.0, base=0,
                                       pattern=[[1, P]], channel_multiplier=-1))
            turn = NRAW * CHUNK // STEP
            s = 0
            while s < n_steps:
                run = 1
                while (s + run < n_steps and step_cols[s + run] == step_cols[s] and
                       chunk_of_step[s + run] - chunk_of_step[s + run - 1] <= 1):
                    run += 1
                if s == G["kv"]["s0"]:
                    window_mask()
                if s == G["nwin"]["s0"]:
                    layer_two_constants()
                peeled = turn if s < NSLOT else 0
                for i in range(peeled):
                    split_lo(pool, s + i)
                if s == 0:
                    pool.memset(hT[:, :, 0:TAPS - 1], 0.0).then_inc(s_pad, 1)
                n = (run - peeled) // turn
                if n > 1:
                    with pool.Fori(0, n) as it:
                        for i in range(turn):
                            split_lo(pool, s + peeled + i, (it, turn))
                else:
                    n = 0
                for i in range(peeled + n * turn, run):
                    split_lo(pool, s + i)
                s += run

        POOL_CONSTS = 18

        ga = G["ga0"]["s0"]
        nsa_units = {3 + 2 * u if u < 7 else 10 + u: u for u in range(2 * QH)}
        score_slot = {2 + 7 * u // 4: u for u in range(HEADS)}

        gla_units = {2: (4, 5), 3: (6,), 4: (7,)}

        @block.tensor
        def _(pe):
            pe.wait_ge(s_pool, 2)
            pe.wait_ge(s_x, 32)
            build_pe(pe, "x", lambda k, t: x[:, t, k * P:(k + 1) * P], only=range(0, 4))

            def param_columns():
                pe.wait_ge(s_par, N_PAR)
                pe.wait_ge(s_xl, built("x", KT))
                pe.transpose(ps_m[2][:, 0:NCOL], param_rows[0:NCOL, :], ident[0:NCOL, 0:NCOL])
                pe.transpose(ps_m[2][:, NCOL:197], pe_rows[:, :], ident[0:96, 0:96]).then_inc(s_cols, 1)
                for c in range(8):
                    last = pe.transpose(ps_m[3][:, 32 * c:32 * c + TAPS], cw_rows[:, c * P:(c + 1) * P],
                                        ident[0:TAPS, 0:TAPS])
                last.then_inc(s_cols, 1)

            def conv_in_T(j):
                pe.wait_ge(s_ch, j + 1)
                for c in range(4):
                    if c % 2 == 0 and j == 1:
                        pe.wait_ge(s_hT, c // 2 + 1)
                    for t in range(TT):
                        last = pe.transpose(ps_m[c // 2][:, (c % 2) * T + t * P:(c % 2) * T + (t + 1) * P],
                                            c_h[:, t, (4 * j + c) * P:(4 * j + c + 1) * P], ident[:])
                    if c % 2:
                        last.then_inc(s_cht, 1)

            def q_T(j):
                evacuated(pe, G[("q0", "q1")[j]])
                for c in range(4):
                    if c % 2 == 0 and j == 1:
                        pe.wait_ge(s_qT, c // 2 + 1)
                    for t in range(TT):
                        last = pe.transpose(ps_m[2 + c // 2][:, (c % 2) * T + t * P:(c % 2) * T + (t + 1) * P],
                                            q_sb[:, t, (4 * j + c) * P:(4 * j + c + 1) * P], ident[:])
                    if c % 2:
                        last.then_inc(s_qt, 1)

            def k_T():
                evacuated(pe, G["kv"])
                pe.wait_ge(s_qT, 3)
                for h in range(KVH):
                    for t in range(TT):
                        last = pe.transpose(ps_m[2][:, h * T + t * P:h * T + (t + 1) * P],
                                            k_dup[:, t, h].rearrange("p a b -> p (a b)"), ident[:])
                last.then_inc(s_qt, 1)

            def scores(u):
                if u == 0:
                    pe.wait_ge(s_qT, 5)
                    pe.wait_ge(s_hT, 4)
                if u >= 1:
                    pe.wait_ge(s_sm, u)
                r = (u % 2) * HD
                k = u // (HEADS // KVH)
                pe.matmul(ps_m[0][:, 0:P], qT[r:r + HD, u // 2, 0:P], kT[r:r + HD, k, 0:P], start=True, stop=True)
                pe.matmul(ps_m[0][:, P:3 * P], qT[r:r + HD, u // 2, P:T], kT[r:r + HD, k, :],
                          start=True, stop=True).then_inc(s_sc, 1)

            def probs_T(u):
                pe.wait_ge(s_exp, u + 1)
                if u >= 1:
                    pe.wait_ge(s_pTc, u)
                for j in range(3):
                    last = pe.transpose(ps_m[2][:, j * P:(j + 1) * P], sS[:, u % 2, j * P:(j + 1) * P], ident[:])
                last.then_inc(s_pt, 1)

            def pv(u):
                pe.wait_ge(s_pTc, u + 1)
                if u == 0:
                    pe.wait_ge(s_qT, 4)
                if u >= 1:
                    pe.wait_ge(s_yn, u)
                k = u // (HEADS // KVH) * HD
                o = (u % 2) * 2 * HD
                pe.matmul(ps_m[3][:, o:o + HD], pT[:, u % 2, 0:P], v_sb[:, 0, k:k + HD], start=True, stop=True)
                pe.matmul(ps_m[3][:, o + HD:o + 2 * HD], pT[:, u % 2, P:2 * P], v_sb[:, 0, k:k + HD], start=True, stop=False)
                pe.matmul(ps_m[3][:, o + HD:o + 2 * HD], pT[:, u % 2, 2 * P:], v_sb[:, 1, k:k + HD],
                          start=False, stop=True).then_inc(s_pv, 1)

            def attn_slot(i):
                if i in score_slot:
                    scores(score_slot[i])
                if i - 3 in score_slot:
                    probs_T(score_slot[i - 3])
                if i - 5 in score_slot:
                    pv(score_slot[i - 5])

            def gate_T(c):
                if c == 0:
                    pe.wait_ge(s_lnc, LNC_READ_SUMS)
                if c % 4 == 0:
                    pe.wait_ge(s_stga, 3 + c // 4)
                if c >= 1:
                    pe.wait_ge(s_gT, c)
                for t in range(TT):
                    last = pe.transpose(ps_m[1][:, t * P:(t + 1) * P],
                                        stg[:, t, (c % 4) * P:(c % 4 + 1) * P], ident[:])
                last.then_inc(s_gat, 1)

            def channel_sum(i, src):
                if i == 0:
                    pe.wait_ge(s_conv, conv_units)
                else:
                    pe.wait_ge(s_lna, 1)
                for c in range(8):
                    last = pe.matmul(ps_m[1][:, 0:T], ones[:, 0:P], src[:, c, :], start=(c == 0), stop=(c == 7))
                last.then_inc(s_lns, 1)

            for g in groups[:11]:
                for j in range(g["ns"]):
                    gemm(pe, g, j, A(aH), A(aL),
                         (lambda j: pe.wait_ge(s_xl, built("x", 2 * j + 2))) if g["i"] == 0 else None)
                    if g["i"] == 0 and j < 4:
                        build_pe(pe, "x", lambda k, t: x[:, t, k * P:(k + 1) * P], only=[j + 4])
                    if g["i"] == 0 and j == 7:
                        param_columns()
                    if g["name"] == "cv1" and j == 2:
                        conv_in_T(0)
                    if g["name"] == "q0" and j == 2:
                        conv_in_T(1)
                    if g["name"] == "q1" and j == 1:
                        q_T(0)
                    if g["name"] == "kv" and j == 2:
                        q_T(1)
                    if g["name"] == "ga0" and j == 1:
                        k_T()
                    i = g["s0"] + j - ga
                    if i == 7:
                        channel_sum(0, cT)
                    if i == 11:
                        channel_sum(1, sq_sb)
                    if 15 <= i < 19:
                        gate_T(i - 15)
                    if 22 <= i < 26:
                        gate_T(4 + i - 22)
                    if i >= 2:
                        attn_slot(i)
            def before_y(u):
                if u == 0:
                    pe.wait_ge(s_yat, 2)
                    pe.wait_ge(s_yn, HEADS)
                    pe.wait_ge(s_lnc, LNC_READ_SUMS)
            def before_wo(g):
                def wait(j):
                    if g["name"] == "wo0":
                        if j == 0:
                            pe.wait_ge(s_ycl, 1)
                        if j >= 4:
                            pe.wait_ge(s_xl, built("yattn", 2 * (j - 4) + 2))
                return wait
            def y_operand(conv, attn):
                return lambda k, n: conv[:, k:k + n, :] if k < 8 else attn[:, k:k + n, :]

            for g in groups[11:15]:
                for j in range(g["ns"]):
                    if (g["name"], j) == ("wo0", 4):
                        build_pe(pe, "yattn", lambda k, t: q_sb[:, t, k * P:(k + 1) * P], before_y)
                    gemm(pe, g, j, y_operand(ycH, aH), y_operand(ycL, aL), before_wo(g))
                    if g["name"] == "wo0" and j < 3:
                        attn_slot(32 + j)
            def h_T(us):
                build_pe(pe, "h", lambda k, t: x[:, t, k * P:(k + 1) * P],
                         lambda u: pe.wait_ge(s_xn, u // 2 + 1), only=us)
            h_T(range(0, 4))

            t2 = [0]

            def unit_begin(ready=None):
                if t2[0] >= 1:
                    pe.wait_ge(s_t2c, t2[0])
                if isinstance(ready, str):
                    evacuated(pe, G[ready])
                elif ready is not None:
                    pe.wait_ge(s_t2s, ready)

            def unit_end(last):
                last.then_inc(s_t2, 1)
                t2[0] += 1

            def rows_T(srcs, ready):
                unit_begin(ready)
                for i, s in enumerate(srcs):
                    last = pe.transpose(ps_m[0][0:s.shape[1], i * P:i * P + s.shape[0]], s, ident[0:s.shape[0], 0:s.shape[0]])
                unit_end(last)

            def heads_T(buf, h, ready):
                rows_T([buf[:, t, hh * DK:(hh + 1) * DK] for hh in (h, h + 1) for t in range(TT)], ready)

            def nq_T(h):
                rows_T([nq[:, t, hh, :] for hh in (h, h + 1) for t in range(TT)], 1 + h // 4)

            def direct(i):
                if i == 0:
                    pe.wait_ge(s_xl, built("h", KT))
                pe.wait_ge(s_kp, i + 1)
                for c in range(4):
                    n = direct_chunks[4 * i + c]
                    wait_raw(pe, n)
                    for l in range(8):
                        last = pe.matmul(ps_m[3][0:2 * NCMP, i * T:(i + 1) * T],
                                         kp[:, i, 8 * c + l].rearrange("p k n -> p (k n)"),
                                         raw[:, n % NRAW, l * T:(l + 1) * T], start=(c == 0 and l == 0),
                                         stop=(c == 3 and l == 7))
                    last.then_inc(s_direct, 1)

            def hid_T(i):
                unit_begin()
                if i == 0:
                    pe.wait_ge(s_hid, 1)
                for hk in range(2):
                    last = pe.transpose(ps_m[0][:, hk * 32:hk * 32 + 2 * NCMP],
                                        hid[:, i * T + hk * P:i * T + (hk + 1) * P], ident[0:2 * NCMP, 0:2 * NCMP])
                unit_end(last)

            def compressed():
                pe.wait_ge(s_p2, 48)
                pe.wait_ge(s_t2c, t2[0])
                for hk in range(2):
                    pe.matmul(ps_m[1][0:2 * NCMP, 0:P], hidTk[:, hk, 0:2 * NCMP], w_c2[:, 0, hk, :],
                              start=(hk == 0), stop=(hk == 1))
                for kv in range(KVH):
                    for hk in range(2):
                        last = pe.matmul(ps_m[1][:, (1 + kv) * P:(2 + kv) * P],
                                         hidTv[:, hk, kv].rearrange("p r n -> p (r n)"), w_c2[:, 1, hk, :],
                                         start=(hk == 0), stop=(hk == 1))
                last.then_inc(s_c2, 1)

            def cmp_scores():
                for t in range(TT):
                    for h in range(QH):
                        kv = h // 4
                        last = pe.matmul(ps_m[2][:, (t * QH + h) * 16:(t * QH + h) * 16 + NCMP],
                                         nqT[:, h, t * P:(t + 1) * P], kcT15[:, kv * NCMP:(kv + 1) * NCMP],
                                         start=True, stop=True)
                last.then_inc(s_csc, 1)

            def cmp_pv(i):
                t, kv = i // KVH, i % KVH
                if i == 0:
                    pe.wait_ge(s_c2v, 2)
                    pe.wait_ge(s_t2c, t2[0])
                else:
                    pe.wait_ge(s_cyn, i)
                pe.matmul(ps_m[1][:], pTc[:, t, kv, :], vc_bd[:, kv].rearrange("p r d -> p (r d)"), start=True,
                          stop=True).then_inc(s_cpv, 1)

            def scores2(u):
                br, h = divmod(u, QH)
                kT_ = (ksT, kwT)[br]
                if u == 0:
                    pe.wait_ge(s_t2c, t2[0])
                    pe.wait_ge(s_csm, 1)
                else:
                    pe.wait_ge(s_sm2, u)
                pe.matmul(ps_m[2][:, 0:P], nqT[:, h, 0:P], kT_[:, h // 4, 0:P], start=True, stop=True)
                pe.matmul(ps_m[2][:, P:3 * P], nqT[:, h, P:T], kT_[:, h // 4, :], start=True, stop=True
                          ).then_inc(s_sc2, 1)

            def probs2_T(u):
                pe.wait_ge(s_exp2, u + 1)
                if u >= 1:
                    pe.wait_ge(s_pTc2, u)
                for j in range(3):
                    last = pe.transpose(ps_m[3][:, j * P:(j + 1) * P], sS2[:, u % 2, j * P:(j + 1) * P], ident[:])
                last.then_inc(s_pt2, 1)

            def pv2(u):
                br, h = divmod(u, QH)
                v_, kv = (vs, vw)[br], h // 4 * DK
                pe.wait_ge(s_pTc2, u + 1)
                if u == 0:
                    pe.wait_ge(s_cyn, 4)
                else:
                    pe.wait_ge(s_yn2, u)
                pe.matmul(ps_m[1][:, 0:DK], pT2[:, u % 2, 0:P], v_[:, 0, kv:kv + DK], start=True, stop=True)
                pe.matmul(ps_m[1][:, DK:2 * DK], pT2[:, u % 2, P:2 * P], v_[:, 0, kv:kv + DK], start=True, stop=False)
                pe.matmul(ps_m[1][:, DK:2 * DK], pT2[:, u % 2, 2 * P:], v_[:, 1, kv:kv + DK], start=False, stop=True
                          ).then_inc(s_pv2, 1)

            def nsa_slot(i):
                if i in nsa_units:
                    scores2(nsa_units[i])
                if i - 2 in nsa_units:
                    probs2_T(nsa_units[i - 2])
                if i - 4 in nsa_units:
                    pv2(nsa_units[i - 4])

            def gk(i):
                unit_begin()
                for h in (2 * i, 2 * i + 1):
                    last = pe.matmul(ps_m[0][:, (h % 2) * T:(h % 2 + 1) * T], w_gk2[:, h * DK:(h + 1) * DK], aT[:],
                                     start=True, stop=True)
                unit_end(last)

            def level_products(i):
                if i == 0:
                    pe.wait_ge(s_t2c, t2[0])
                    pe.wait_ge(s_yn2, 2 * QH)
                    pe.wait_ge(s_pTc2, 2 * QH)
                else:
                    pe.wait_ge(s_gQ, i)
                for h in range(TT if i < 8 else 1):
                    if i >= 1:
                        pe.wait_ge(s_gS, 2 * i + h)
                    for g_ in range(GH):
                        o = g_ * T + h * P
                        if i == 0:
                            l_, r_ = klT[:, g_, h * P:(h + 1) * P], qlT[:, g_, h * P:(h + 1) * P]
                        elif i < 8:
                            l_ = r_ = QK[i % 2][:, o:o + P]
                        else:
                            l_, r_ = QK[i % 2][:, g_ * T:g_ * T + P], QK[i % 2][:, g_ * T + P:(g_ + 1) * T]
                        last = pe.matmul(ps_m[2 + h][:, g_ * P:(g_ + 1) * P], l_, r_, start=True, stop=True)
                    last.then_inc(s_gP, 1)

            def gla_out(i):
                t, hp = divmod(i, 2)
                pe.wait_ge(s_gS, 18)
                if i >= 2:
                    pe.wait_ge(s_goc, i - 1)
                for h in (2 * hp, 2 * hp + 1):
                    dst = ps_m[2 + i % 2][:, (h % 2) * DV:(h % 2 + 1) * DV]
                    if t == 0:
                        last = pe.matmul(dst, sT[:, 0, h, :], vl[:, 0, h, :], start=True, stop=True)
                    else:
                        pe.matmul(dst, sT[:, 2, h, :], vl[:, 0, h, :], start=True, stop=False)
                        last = pe.matmul(dst, sT[:, 1, h, :], vl[:, 1, h, :], start=False, stop=True)
                last.then_inc(s_go, 1)

            def stg_heads(h, ready):
                rows_T([stg2[:, t, hh * DK:(hh + 1) * DK] for hh in (h, h + 1) for t in range(TT)], ready)

            lq1 = G["lq1"]["s0"]
            for g in groups[15:28]:
                for j in range(g["ns"]):
                    gemm(pe, g, j, A(aH), A(aL),
                         (lambda j: pe.wait_ge(s_xl, built("h", 2 * j + 2))) if g["name"] == "nq0" else None)
                    here = (g["name"], j)
                    if g["name"] == "nq0" and j < 4:
                        h_T([j + 4])
                    if here == ("nq1", 4):
                        nq_T(0)
                        nq_T(2)
                    if here == ("ncmp", 4):
                        nq_T(4)
                        nq_T(6)
                    if here == ("nslc", 2):
                        stg_heads(0, 3)
                        stg_heads(2, 3)
                    if here == ("nslc", 7):
                        direct(0)
                        direct(1)
                    if here == ("nwin", 1):
                        stg_heads(0, 4)
                    if here == ("nwin", 2):
                        hid_T(0)
                        hid_T(1)
                    if here == ("nwin", 3):
                        compressed()
                    if here == ("nwin", 5):
                        rows_T([kcn[:, :]], 5)
                    if here == ("glq0", 1):
                        stg_heads(0, 6)
                    if here == ("glq0", 2):
                        cmp_scores()
                    if here == ("glq0", 5):
                        rows_T([pc[:, t, 4 * kv:4 * kv + 4, :].rearrange("p h n -> p (h n)") for t in range(TT) for kv in range(KVH)], 7)
                    if g["name"] == "lq1" and j in (1, 2, 3, 4):
                        cmp_pv(j - 1)
                    if here == ("lq1", 2):
                        stg_heads(0, "glq0")
                    if here == ("lar0", 2):
                        stg_heads(0, "lq1")
                    if here == ("lk", 1):
                        rows_T([stg2[:, t, 0:16] for t in range(TT)], "lar0")
                    if here == ("lk", 2):
                        gk(0)
                        gk(1)
                    if here == ("lv0", 1):
                        stg_heads(0, "lk")
                        stg_heads(2, "lk")
                    if g["s0"] + j >= lq1:
                        nsa_slot(g["s0"] + j - lq1)
                    i = g["s0"] + j - lq1
                    if i >= 31 and i < 49 and i % 2:
                        level_products((i - 31) // 2)
                    if g["name"] == "lr2" and 1 <= j <= 4:
                        gla_out(j - 1)

            def y2_src(k, t):
                return yn[:, t, k, :] if k < 8 else yg[:, t, (k - 8) // 2, (k % 2) * P:(k % 2 + 1) * P]

            def before_y2(u):
                if u == 0:
                    pe.wait_ge(s_goc, 4)
                    pe.wait_ge(s_y2n, 1)
                if u == 4:
                    pe.wait_ge(s_y2g, 1)
            build_pe(pe, "y2", y2_src, before_y2, only=range(0, 4))
            for g in groups[28:32]:
                for j in range(g["ns"]):
                    gemm(pe, g, j, A(aH), A(aL),
                         (lambda j: pe.wait_ge(s_xl, built("y2", 2 * j + 2))) if g["name"] == "w2o0" else None)
                    if g["name"] == "w2o0" and j in gla_units:
                        build_pe(pe, "y2", y2_src, before_y2, only=gla_units[j])
                    u = g["s0"] + j - G["w2o2"]["s0"] - 4
                    if 0 <= u < 8:
                        build_pe(pe, "mem", lambda k, t: memn[:, t, k * P:(k + 1) * P],
                                 lambda u: pe.wait_ge(s_mem, 16), only=[u])
            def scores3(u):
                if u == 0:
                    pe.wait_ge(s_t2c, t2[0])
                if u >= 2:
                    pe.wait_ge(s_exp3, u - 1)
                for t in range(TT):
                    last = pe.matmul(ps_m[2 * (u % 2)][:, t * T:(t + 1) * T], cqT[:, u, t * P:(t + 1) * P], ckT[:, u, :],
                                     start=True, stop=True)
                last.then_inc(s_sc3, 1)

            def probs3_T(u):
                pe.wait_ge(s_exp3, u + 1)
                if u >= 1:
                    pe.wait_ge(s_pTc3, u)
                for t in range(TT):
                    for m in range(TT):
                        i = t * TT + m
                        last = pe.transpose(ps_m[3][:, i * P:(i + 1) * P], sS3[:, u, t, m * P:(m + 1) * P], ident[:])
                last.then_inc(s_pt3, 1)

            def pv3(u):
                pe.wait_ge(s_pTc3, u + 1)
                if u >= 2:
                    pe.wait_ge(s_on, u - 1)
                elif u == 0:
                    evacuated(pe, G["mv"])
                for t in range(TT):
                    for m in range(TT):
                        last = pe.matmul(ps_m[1 + u % 2][:, t * P:(t + 1) * P], pT3[:, u, t, m, :],
                                         cvn[:, m, u * DK:(u + 1) * DK], start=(m == 0), stop=(m == TT - 1))
                last.then_inc(s_pv3, 1)

            def cross_T(buf, h, ready):
                unit_begin()
                pe.wait_ge(s_ckr, ready)
                for i, (hh, t) in enumerate([(hh, t) for hh in (h, h + 1) for t in range(TT)]):
                    last = pe.transpose(ps_m[0][:, i * P:(i + 1) * P], buf[:, t, hh, :], ident[:])
                unit_end(last)

            for g in groups[32:35]:
                for j in range(g["ns"]):
                    op = (aH, aL) if g["name"] == "mq" else (mH, mL)
                    before = None
                    if g["name"] == "mk":
                        before = lambda j: pe.wait_ge(s_xl, built("mem", 2 * j + 2))
                    if g["name"] == "mq":
                        before = lambda j: pe.wait_ge(s_xl, built("hq", 2 * j + 2))
                    gemm(pe, g, j, A(op[0]), A(op[1]), before)
                    here = (g["name"], j)
                    if g["name"] == "mk":
                        def before_hq(u):
                            if u == 0:
                                evacuated(pe, G["w2o3"])
                                evacuated(pe, G["w2o2"])
                        build_pe(pe, "hq", lambda k, t: x[:, t, k * P:(k + 1) * P], before_hq, only=[j])
                    if here == ("mq", 4):
                        pe.wait_ge(s_xl, built("hq", KT))
                        cross_T(ckn, 0, 1)
                        cross_T(ckn, 2, 1)
                    if here == ("mv", 2):
                        cross_T(cqn, 0, 2)
                        cross_T(cqn, 2, 2)
                    if g["name"] == "mv" and j in (4, 5):
                        scores3(2 * j - 8)
                        scores3(2 * j - 7)
                    if g["name"] == "mv" and 6 <= j:
                        probs3_T(j - 6)
            probs3_T(2)
            probs3_T(3)
            for u in range(MH):
                pv3(u)

            def before_oc(u):
                if u == 0:
                    pe.wait_ge(s_on, MH)
                    pe.wait_ge(s_pTc3, MH)
            build_pe(pe, "oc", lambda k, t: ocn[:, t, k, :], before_oc)
            for g in groups[35:39]:
                for j in range(g["ns"]):
                    gemm(pe, g, j, A(ocH), A(ocL),
                         (lambda j: pe.wait_ge(s_xl, built("oc", 2 * j + 2))) if g["name"] == "co0" else None)
            def hf_T(us):
                build_pe(pe, "hf", lambda k, t: x[:, t, k * P:(k + 1) * P],
                         lambda u: evacuated(pe, G[f"co{u // 2}"]), only=us)
            hf_T(range(0, 4))

            def hidden_T(j, later=None):
                def before(u):
                    evacuated(pe, G[f"fu{j}"], later)
                build_pe(pe, f"gu{j}", lambda k, t: hn[:, t, k * P:(k + 1) * P], before, later=later)

            def gate_up(i, hidden=None, later=None):
                for g in (G[f"fg{i}"], G[f"fu{i}"]):
                    for j in range(g["ns"]):
                        gemm(pe, g, j, A(aH), A(aL),
                             (lambda j: pe.wait_ge(s_xl, built("hf", 2 * j + 2))) if g["name"] == "fg0" else None,
                             later)
                        if g["name"] == "fg0" and j < 4:
                            hf_T([j + 4])
                        if hidden is not None and g["name"] == f"fg{i}" and j == 2:
                            hidden_T(hidden, later)

            for part, (g0, n) in enumerate(PARTS):
                gate_up(g0)
                with pe.Fori(0, n - 1) as it:
                    gate_up(g0 + 1, hidden=g0, later=(it, 2 * KT // STEP))
                hidden_T(g0 + n - 1)
                with pe.Fori(0, 2) as it:
                    for i in range(2):
                        g = G[f"fd{part}{i}"]
                        for j in range(g["ns"]):
                            gemm(pe, g, j, A(guH), A(guL),
                                 (lambda j: pe.wait_ge(s_xl, built(f"gu{g0}", 2 * j + 2))) if i == 0 else None,
                                 (it, 2 * g["ns"]))

        @block.scalar
        def _(act):
            for s in range(LEAD):
                split_hi(act, s)
            build_act(act, "x", A(aH), only=range(0, 4))

            def sigmoid(i, func):
                evacuated(act, G[("cg0", "cg1", "ga0", "ga1", "ag0", "ag1")[i]])
                act.activation(stg[:], stg[:], func).then_inc(s_stga, 1)

            def conv_in(j):
                for c in range(2):
                    act.wait_ge(s_cht, 2 * j + c + 1)
                    act.copy(hT[:, 4 * j + 2 * c:4 * j + 2 * c + 2, TAPS - 1:],
                             ps_m[c][:].rearrange("p (c t) -> p c t", c=2)).then_inc(s_hT, 1)

            def q_T(j):
                for c in range(2):
                    act.wait_ge(s_qt, 2 * j + c + 1)
                    act.copy(qT[:, 4 * j + 2 * c:4 * j + 2 * c + 2, :].rearrange("p c t -> p (c t)"),
                             ps_m[2 + c][:]).then_inc(s_qT, 1)

            def k_T():
                act.wait_ge(s_qt, 5)
                act.copy(kT[:].rearrange("p k t -> p (k t)"), ps_m[2][:]).then_inc(s_qT, 1)

            def exps(u):
                act.wait_ge(s_sm, u + 1)
                act.activation(sS[:, u % 2, 0:P], sS[:, u % 2, 0:P], ACT.Exp, bias=mx[:, u, 0:1],
                               accum_out=den[:, u, 0:1])
                act.activation(sS[:, u % 2, P:], sS[:, u % 2, P:], ACT.Exp, bias=mx[:, u, 1:2],
                               accum_out=den[:, u, 1:2])
                act.activation(esk[:, u, :], mx[:, u, :], ACT.Exp, bias=sinks[:, u:u + 1]).then_inc(s_exp, 1)

            def probs_copy(u):
                act.wait_ge(s_pt, u + 1)
                if u >= 2:
                    act.wait_ge(s_pv, u - 1)
                act.copy(pT[:, u % 2, :], ps_m[2][:, 0:3 * P]).then_inc(s_pTc, 1)

            def gate_copy(c):
                act.wait_ge(s_gat, c + 1)
                act.copy(gT[:, c, :], ps_m[1][:, 0:T]).then_inc(s_gT, 1)

            def attn_slot(i):
                if i - 1 in score_slot:
                    exps(score_slot[i - 1])
                if i - 4 in score_slot:
                    probs_copy(score_slot[i - 4])

            for g in groups[:11]:
                for j in range(g["ns"]):
                    split_hi(act, g["s0"] + j + LEAD)
                    if g["i"] == 0 and j < 4:
                        build_act(act, "x", A(aH), only=[j + 4])
                    here = (g["name"], j)
                    if here == ("cv1", 1):
                        sigmoid(0, ACT.Sigmoid)
                    if here == ("cv1", 3):
                        conv_in(0)
                    if here == ("q0", 1):
                        sigmoid(1, ACT.Sigmoid)
                    if here == ("q0", 3):
                        conv_in(1)
                    if here == ("q1", 2):
                        q_T(0)
                    if here == ("kv", 3):
                        q_T(1)
                    if here == ("ga0", 2):
                        k_T()
                    i = g["s0"] + j - ga
                    if i >= 3:
                        attn_slot(i)
                    if i == 9:
                        act.wait_ge(s_lnc, 2)
                        act.wait_ge(s_conv, conv_units)
                        act.activation(sq_sb[:], cT[:], ACT.Square).then_inc(s_lna, 1)
                    if i == 12:
                        act.wait_ge(s_lnc, LNC_READ_SUMS)
                        act.activation(rstd_sb[:], rstd_sb[:], ACT.Sqrt).then_inc(s_lna, 1)
                    if i == 14:
                        sigmoid(2, ACT.Silu)
                    if 16 <= i < 20:
                        gate_copy(i - 16)
                    if i == 16:
                        act.wait_ge(s_lnc, LNC_READ_SUMS + 2)
                        for c in range(8):
                            last = act.activation(cT[:, c, :], cT[:, c, :], ACT.Silu,
                                                  scale=cols[:, CLG + c:CLG + c + 1],
                                                  bias=cols[:, CLB + c:CLB + c + 1])
                        last.then_inc(s_lna, 1)
                    if i == 21:
                        sigmoid(3, ACT.Silu)
                    if 23 <= i < 27:
                        gate_copy(4 + i - 23)
                    if i == 29:
                        sigmoid(4, ACT.Silu)
                    if i == 28:
                        act.wait_ge(s_lnc, LNC_READ_SUMS + 3)
                        act.copy(ycH[:], cT[:]).then_inc(s_ych, 1)
                    i = g["s0"] + j - ga
            for g in groups[11:15]:
                for j in range(g["ns"]):
                    split_hi(act, g["s0"] + j + LEAD)
                    if g["name"] == "wo0" and j < 3:
                        attn_slot(32 + j)
                    if (g["name"], j) == ("wo0", 0):
                        sigmoid(5, ACT.Silu)
                    if (g["name"], j) == ("wo0", 3):
                        act.wait_ge(s_used, G["wo0"]["s0"])
                        build_act(act, "yattn", A(aH, 8))
            roots = [0]

            def root(ap):
                act.wait_ge(s_var, roots[0] + 1)
                act.activation(ap, ap, ACT.Sqrt).then_inc(s_sqrt, 1)
                roots[0] += 1

            t2 = [0]

            def bank0(*copies):
                act.wait_ge(s_t2, t2[0] + 1)
                for out_, in_, scale in copies:
                    last = act.copy(out_, in_) if scale is None else act.activation(out_, in_, ACT.Copy, scale=scale)
                last.then_inc(s_t2c, 1)
                t2[0] += 1

            def col(c):
                return cols[:, c:c + 1]

            root(var_ln)

            def h_hi(us):
                build_act(act, "h", A(aH), lambda k: col(HG + k), only=us, offset=lambda k: col(HB + k))

            def row_squares():
                act.wait_ge(s_x1, 4)
                for t in range(TT):
                    last = act.activation(sq_row[:], x[:, t, :], ACT.Square, accum_out=ss[:, t:t + 1])
                    if t == 0:
                        last.then_inc(s_act, 1)
                        act.wait_ge(s_act, 1)
                last.then_inc(s_ss, 1)
                root(ss)
            h_hi(range(0, 4))

            def heads2(dst, h, scale):
                bank0((dst[:, h:h + 2, :].rearrange("p h t -> p (h t)"), ps_m[0][:], scale))

            def cmp_exp():
                act.wait_ge(s_csm, 2)
                act.activation(pc[:, :, :, 0:NCMP].rearrange("p t h n -> p (t h) n"),
                               pc[:, :, :, 0:NCMP].rearrange("p t h n -> p (t h) n"), ACT.Exp).then_inc(s_cexp, 1)

            def exps2(u):
                act.wait_ge(s_sm2, u + 1)
                act.activation(sS2[:, u % 2, 0:P], sS2[:, u % 2, 0:P], ACT.Exp, bias=mx2[:, u, 0:1],
                               accum_out=den2[:, u, 0:1])
                act.activation(sS2[:, u % 2, P:], sS2[:, u % 2, P:], ACT.Exp, bias=mx2[:, u, 1:2],
                               accum_out=den2[:, u, 1:2]).then_inc(s_exp2, 1)

            def probs2_copy(u):
                act.wait_ge(s_pt2, u + 1)
                if u >= 2:
                    act.wait_ge(s_pv2, u - 1)
                act.copy(pT2[:, u % 2, :], ps_m[3][:, 0:3 * P]).then_inc(s_pTc2, 1)

            def nsa_slot(i):
                if i - 1 in nsa_units:
                    exps2(nsa_units[i - 1])
                if i - 3 in nsa_units:
                    probs2_copy(nsa_units[i - 3])

            def level_exp(i):
                act.wait_ge(s_gE, i)
                act.activation(E[i % 2][:], E[i % 2][:], ACT.Exp, scale=1.0 / 16.0).then_inc(s_gX, 1)

            def log_sigmoid():
                act.wait_ge(s_t2c, t2[0])
                act.activation(QK[1][:], gz[:], ACT.Abs).then_inc(s_z, 1)
                act.wait_ge(s_z, 1)
                act.activation(QK[1][:], QK[1][:], ACT.Exp, scale=-1.0).then_inc(s_z, 1)
                act.wait_ge(s_z, 2)
                act.activation(QK[1][:], QK[1][:], ACT.Ln, bias=1.0).then_inc(s_z, 1)

            lq1 = G["lq1"]["s0"]
            for g in groups[15:28]:
                for j in range(g["ns"]):
                    split_hi(act, g["s0"] + j + LEAD)
                    here = (g["name"], j)
                    if g["name"] == "nq0" and j < 4:
                        h_hi([j + 4])
                    if here == ("nq0", 7):
                        row_squares()
                    if here == ("nq1", 1):
                        root(ss_q[:, 0])
                    if here == ("nq1", 5):
                        heads2(nqT, 0, colq)
                        heads2(nqT, 2, colq)
                    if here == ("ncmp", 1):
                        root(ss_q[:, 1])
                    if here == ("ncmp", 5):
                        heads2(nqT, 4, colq)
                        heads2(nqT, 6, colq)
                    if here == ("nslc", 3):
                        heads2(kcT, 0, None)
                        heads2(vcT, 0, None)
                    if here == ("nwin", 0):
                        root(ss_k[:, 0])
                    if here == ("nwin", 1):
                        act.wait_ge(s_direct, 8)
                        act.activation(hid[:], ps_m[3][0:2 * NCMP, :], ACT.Silu).then_inc(s_hid, 1)
                    if here == ("nwin", 2):
                        heads2(ksT, 0, col(GKS))
                        bank0((hidTk[:, :, 0:2 * NCMP],
                               ps_m[0][:, 0:64].rearrange("p (a b) -> p a b", a=2)[:, :, 0:2 * NCMP], None))
                        act.wait_ge(s_c2v, HIDTV_CLEARED)
                        bank0(*[(hidTv[:, hk, kv, :, 0:NCMP],
                                 ps_m[0][:, hk * 32 + kv * NCMP:hk * 32 + (kv + 1) * NCMP].unsqueeze(1).to_broadcast([P, 4, NCMP]),
                                 None) for hk in range(2) for kv in range(KVH)])
                    if here == ("nwin", 4):
                        root(ss_c)
                    if here == ("nwin", 6):
                        bank0((kcT15[:], ps_m[0][:, 0:2 * NCMP], col(GKC)))
                    if here == ("glq0", 1):
                        root(ss_k[:, 1])
                    if here == ("glq0", 2):
                        heads2(kwT, 0, col(GKW))
                    if here == ("glq0", 4):
                        cmp_exp()
                    if here == ("glq0", 6):
                        bank0((pTc[:].rearrange("p t k q -> p (t k q)"), ps_m[0][:], None))
                    if here == ("lq1", 1):
                        evacuated(act, G["glq0"])
                        act.activation(gates[:], gates[:], ACT.Sigmoid).then_inc(s_gsig, 1)
                    if here == ("lq1", 3):
                        heads2(qlT, 0, float(DK) ** -0.5)
                    if here == ("lar0", 3):
                        heads2(qlT, 2, float(DK) ** -0.5)
                    if here == ("lk", 2):
                        bank0((aT[:], ps_m[0][0:16, 0:T], None))
                    if here == ("lk", 3):
                        for i in range(2):
                            act.wait_ge(s_t2, t2[0] + 1)
                            for h in (2 * i, 2 * i + 1):
                                last = act.activation(gz[:, h * T:(h + 1) * T], ps_m[0][:, (h % 2) * T:(h % 2 + 1) * T],
                                                      ACT.Identity, bias=col(BGK + h))
                            last.then_inc(s_t2c, 1)
                            t2[0] += 1
                    if here == ("lv0", 2):
                        heads2(klT, 0, None)
                        heads2(klT, 2, None)
                    if g["s0"] + j >= lq1:
                        nsa_slot(g["s0"] + j - lq1)
                    i = g["s0"] + j - lq1
                    if i == 27:
                        log_sigmoid()
                    if i >= 32 and i <= 46 and i % 2 == 0:
                        level_exp((i - 30) // 2)
                    if here == ("lr2", 0):
                        evacuated(act, G["lr1"])
                        evacuated(act, G["lar0"])
                        act.activation(rl[:, :, 0:768], rl[:, :, 0:768], ACT.Silu)
                    if here == ("lr2", 1):
                        root(ss_n)
            root(ss_g)
            act.wait_ge(s_used, G["w2o0"]["s0"])

            def y2_hi(us):
                build_act(act, "y2", A(aH), lambda k: col(GNS) if k < 8 else col(GGL + k % 2), only=us)
            y2_hi(range(0, 4))
            evacuated(act, G["lr2"])
            act.activation(rl[:, :, 768:], rl[:, :, 768:], ACT.Silu).then_inc(s_rl, 1)

            def squares(src, sums, scratch, count):
                for t in range(TT):
                    act.activation(scratch, src[:, t, :], ACT.Square, accum_out=sums[:, t:t + 1]).then_inc(s_sqs, 1)
                    act.wait_ge(s_sqs, count + t + 1)

            for g in groups[28:32]:
                for j in range(g["ns"]):
                    split_hi(act, g["s0"] + j + LEAD)
                    if g["name"] == "w2o0" and j in gla_units:
                        y2_hi(gla_units[j])
                    u = g["s0"] + j - G["w2o2"]["s0"] - 5
                    if 0 <= u < 8:
                        build_act(act, "mem", A(mH), lambda k: col(GME + k), only=[u])
                    if u == 0:
                        squares(memn, ss_m, sq_m[:], 0)
            build_act(act, "mem", A(mH), lambda k: col(GME + k), only=list(range(g["s0"] + 7 - G["w2o2"]["s0"] - 4, 8)))
            root(ss_m)
            evacuated(act, G["w2o3"])
            evacuated(act, G["w2o2"])

            def exps3(u):
                act.wait_ge(s_sm3, u + 1)
                for t in range(TT):
                    last = act.activation(sS3[:, u, t, :], ps_m[2 * (u % 2)][:, t * T:(t + 1) * T], ACT.Exp,
                                          bias=mx3[:, u, t:t + 1], accum_out=den3[:, u, t:t + 1])
                last.then_inc(s_exp3, 1)

            def probs3_copy(u):
                act.wait_ge(s_pt3, u + 1)
                act.copy(pT3[:, u].rearrange("p t m q -> p (t m q)"), ps_m[3][:]).then_inc(s_pTc3, 1)

            for g in groups[32:35]:
                for j in range(g["ns"]):
                    split_hi(act, g["s0"] + j + LEAD)
                    here = (g["name"], j)
                    if g["name"] == "mk" and j >= 1:
                        build_act(act, "hq", A(aH), lambda k: col(GC + k), only=[j - 1])
                    if here == ("mq", 0):
                        build_act(act, "hq", A(aH), lambda k: col(GC + k), only=[7])
                        squares(x, ss_x2, sq_m[:], 2)
                    if here == ("mq", 1):
                        root(ss_x2)
                    if here == ("mq", 3):
                        root(ss_ck)
                    if here == ("mq", 5):
                        heads2(ckT, 0, col(GCK))
                        heads2(ckT, 2, col(GCK))
                    if here == ("mv", 1):
                        root(ss_cq)
                    if here == ("mv", 3):
                        heads2(cqT, 0, colcq)
                        heads2(cqT, 2, colcq)
                    if g["name"] == "mv" and j in (5, 6):
                        exps3(2 * j - 10)
                        exps3(2 * j - 9)
                    if here == ("mv", 7):
                        probs3_copy(0)
            for u in range(1, MH):
                probs3_copy(u)
            build_act(act, "oc", A(ocH))
            for g in groups[35:39]:
                for j in range(g["ns"]):
                    split_hi(act, g["s0"] + j + LEAD)
            build_act(act, "hf", A(aH), lambda k: col(GF + k), only=range(0, 4))

            def gate_up(i, hidden=None, at=None, later=None):
                for j in range(8):
                    split_hi(act, G[f"fg{i}"]["s0"] + j + LEAD, later)
                    if i == 0 and j < 4:
                        build_act(act, "hf", A(aH), lambda k: col(GF + k), only=[j + 4])
                    if i == 0 and j == 5:
                        squares(x, ss_x3, sq_f[:], 4)
                    if i == 0 and j == 7:
                        root(ss_x3)
                    if j == 3 and hidden is not None:
                        build_act(act, f"gu{hidden}", A_at(guH, at), later=later)
                for j in range(8):
                    split_hi(act, G[f"fu{i}"]["s0"] + j + LEAD, later)
                    if j == 0:
                        g = G[f"fg{i}"]
                        psum_ready(act, g, later)
                        act.wait_ge(s_ffs, 1)
                        if i >= 1:
                            evacuated(act, G[f"fu{i - 1}"], later)
                        for t in range(TT):
                            act.activation(sg[:, t, :], ps_g[pair_of(g)][t][:], ACT.Silu, scale=ss_x3[:, t:t + 1]
                                           ).then_inc(s_free[pair_of(g)], 1)

            for part, (g0, n) in enumerate(PARTS):
                gate_up(g0)
                with act.Fori(0, n - 1) as it:
                    gate_up(g0 + 1, g0, it * (NG // P), (it, 2 * KT // STEP))
                build_act(act, f"gu{g0 + n - 1}", A(guH, 4 * (n - 1)))
                first = G[f"fd{part}0"]["s0"] + LEAD
                steps = min(4 * 2 * n, n_steps - first)
                turn = NRAW * CHUNK // STEP
                with act.Fori(0, steps // turn) as it:
                    for j in range(turn):
                        split_hi(act, first + j, (it, turn))
                for j in range(steps // turn * turn, steps):
                    split_hi(act, first + j)

        @block.vector
        def _(dve):
            def link(ins):
                n_dve[0] += 1
                ins.then_inc(s_dve, 1)
                dve.wait_ge(s_dve, n_dve[0])

            build_dve(dve, "x", A(aH), A(aL))
            dve.wait_ge(s_cols, 1)
            link(dve.tensor_copy(cols[:, 0:197], ps_m[2][:, 0:197]))
            for dst, src in ((HG, LNG), (HB, LNB)):
                last = dve.tensor_tensor(cols[:, dst:dst + 16], cols[:, src:src + 16], cols[:, GM:GM + 16], ALU.mult)
            last.then_inc(s_colsb, 1)
            dve.wait_ge(s_cols, 2)
            dve.tensor_copy(convw[:, :, 0:TAPS], ps_m[3][:, 0:256].rearrange("p (c k) -> p c k", c=8)[:, :, 0:TAPS]
                            ).then_inc(s_colsb, 1)

            def gla_masks():
                dve.wait_ge(s_pool, POOL_CONSTS)
                link(dve.tensor_tensor(iot[:, 0, :], iot[:, 0, :], iot[:, 1, :], ALU.bitwise_xor))
                link(dve.tensor_copy(xorf[:], iot[:, 0, :]))
                link(dve.tensor_tensor(xorf[:], xorf[:], tri[:], ALU.mult))
                for l in range(LEVELS + 1):
                    last = dve.tensor_scalar(ge[:, l, :], xorf[:], float(2 ** l), None, ALU.is_ge)
                link(last)
                for l in range(LEVELS):
                    dve.tensor_tensor(lmask[:, l, :], ge[:, l, :], ge[:, l + 1, :], ALU.subtract)
                link(dve.tensor_copy(lmask[:, LEVELS, :], ident[:]))

            def evac(g, dst):
                psum_ready(dve, g)
                b = bias_slot(dve, g["name"])
                for t in range(TT):
                    dve.tensor_tensor(dst(t), ps_g[pair_of(g)][t][:, :g["n"]], b, ALU.add
                                      ).then_inc(s_free[pair_of(g)], 1)

            def evac_stage(i, name):
                g = G[name]
                psum_ready(dve, g)
                b = bias_slot(dve, name)
                if i == 3:
                    dve.wait_ge(s_gat, 4)
                if i == 4:
                    dve.wait_ge(s_gat, 8)
                for t in range(TT):
                    dve.tensor_tensor(stg[:, t, :], ps_g[pair_of(g)][t][:], b, ALU.add).then_inc(s_free[pair_of(g)], 1)

            def glu(j):
                dve.wait_ge(s_stga, j + 1)
                dve.tensor_tensor(c_h[:, :, j * NG:(j + 1) * NG], c_h[:, :, j * NG:(j + 1) * NG], stg[:],
                                  ALU.mult).then_inc(s_ch, 1)

            conv_order = [(half, k, c) for half in range(2) for k in range(TAPS) for c in range(4)]
            conv_at = [0]

            def conv(n):
                for half, k, c in conv_order[conv_at[0]:conv_at[0] + n]:
                    i = conv_at[0]
                    conv_at[0] += 1
                    ct = 4 * half + c
                    if k == 0 and c == 0:
                        dve.wait_ge(s_pad, 1)
                        dve.wait_ge(s_hT, 2 * half + 2)
                    src = hT[:, ct, k:k + T]
                    w = convw[:, ct, k:k + 1]
                    if k == 0:
                        dve.tensor_scalar(cT[:, ct, :], src, w, cols[:, CB + ct:CB + ct + 1], ALU.mult,
                                          ALU.add).then_inc(s_conv, 1)
                    else:
                        dve.wait_ge(s_conv, i - 3)
                        dve.scalar_tensor_tensor(out=cT[:, ct, :], in0=src, scalar=w, in1=cT[:, ct, :],
                                                 op0=ALU.mult, op1=ALU.add).then_inc(s_conv, 1)

            def softmax(u):
                dve.wait_ge(s_sc, u + 1)
                if u >= 2:
                    dve.wait_ge(s_pt, u - 1)
                link(dve.scalar_tensor_tensor(out=sS[:, u % 2, :], in0=ps_m[0][:, 0:3 * P], scalar=HD ** -0.5,
                                              in1=mask1[:], op0=ALU.mult, op1=ALU.add))
                dve.tensor_reduce(mx[:, u, 0:1], sS[:, u % 2, 0:P], AX_X, ALU.max)
                link(dve.tensor_reduce(mx[:, u, 1:2], sS[:, u % 2, P:], AX_X, ALU.max))
                dve.tensor_scalar(mx[:, u, :], mx[:, u, :], sinks[:, u:u + 1], -1.0, ALU.max,
                                  ALU.mult).then_inc(s_sm, 1)

            def normalize(u):
                dve.wait_ge(s_pv, u + 1)
                link(dve.tensor_tensor(den[:, u, :], den[:, u, :], esk[:, u, :], ALU.add))
                link(dve.reciprocal(rden[:, u, :], den[:, u, :]))
                o = (u % 2) * 2 * HD
                for t in range(TT):
                    last = dve.tensor_scalar(q_sb[:, t, u * HD:(u + 1) * HD],
                                             ps_m[3][:, o + t * HD:o + (t + 1) * HD], rden[:, u, t:t + 1], None,
                                             ALU.mult)
                last.then_inc(s_yn, 1)

            def gate_attn(j):
                dve.wait_ge(s_stga, 5 + j)
                dve.wait_ge(s_yn, 8 * (j + 1))
                dve.tensor_tensor(q_sb[:, :, j * NG:(j + 1) * NG], q_sb[:, :, j * NG:(j + 1) * NG], stg[:],
                                  ALU.mult).then_inc(s_yat, 1)

            def layer_norm_sum(i):
                dve.wait_ge(s_lns, i + 1)
                if i == 0:
                    dve.tensor_scalar(mean_sb[:], ps_m[1][:, 0:T], 1.0 / C, None, ALU.mult).then_inc(s_lnc, 1)
                    dve.wait_ge(s_lnc, 1)
                    dve.tensor_tensor(cT[:], cT[:], mean_sb[:].unsqueeze(1).to_broadcast([P, 8, T]),
                                      ALU.subtract).then_inc(s_lnc, 1)
                else:
                    dve.tensor_scalar(rstd_sb[:], ps_m[1][:, 0:T], 1.0 / C, LN_EPS, ALU.mult,
                                      ALU.add).then_inc(s_lnc, 1)
                    dve.wait_ge(s_lna, 2)
                    dve.reciprocal(rstd_sb[:], rstd_sb[:]).then_inc(s_lnc, 1)
                    dve.wait_ge(s_lnc, LNC_READ_SUMS + 1)
                    dve.tensor_tensor(cT[:], cT[:], rstd_sb[:].unsqueeze(1).to_broadcast([P, 8, T]),
                                      ALU.mult).then_inc(s_lnc, 1)

            def half(j):
                return lambda t: c_h[:, t, j * NG:(j + 1) * NG]

            evac(G["cv0"], half(0))
            evac_stage(0, "cg0")
            glu(0)
            conv(40)
            evac(G["cv1"], half(1))
            conv(40)
            dve.wait_ge(s_ch, 1)
            evac_stage(1, "cg1")
            glu(1)
            conv(44)
            evac(G["q0"], lambda t: q_sb[:, t, 0:NG])
            conv(45)
            evac(G["q1"], lambda t: q_sb[:, t, NG:])
            conv(40)
            g = G["kv"]
            psum_ready(dve, g)
            b = bias_slot(dve, "kv")
            for t in range(TT):
                src = ps_g[pair_of(g)][t]
                for d in range(2):
                    dve.tensor_tensor(k_dup[:, t, :, d, :], src[:, 0:P].rearrange("p (k d) -> p k d", k=KVH),
                                      b[:, 0:P].rearrange("p (k d) -> p k d", k=KVH), ALU.add)
                dve.tensor_tensor(v_sb[:, t, :], src[:, P:2 * P], b[:, P:2 * P], ALU.add
                                  ).then_inc(s_free[pair_of(g)], 1)
            for i in range(2, 36):
                if i - 6 in score_slot:
                    normalize(score_slot[i - 6])
                if i in score_slot:
                    softmax(score_slot[i])
                if i < 7:
                    conv(min(8, conv_units - conv_at[0]))
                if i == 7:
                    dve.wait_ge(s_conv, conv_units)
                if i == 8:
                    layer_norm_sum(0)
                    dve.wait_ge(s_ch, 2)
                    evac_stage(2, "ga0")
                if i == 12:
                    layer_norm_sum(1)
                if i == 19:
                    evac_stage(3, "ga1")
                if i == 26:
                    dve.wait_ge(s_gT, 8)
                    dve.wait_ge(s_lna, 3)
                    dve.tensor_tensor(cT[:], cT[:], gT[:], ALU.mult).then_inc(s_lnc, 1)
                if i == 27:
                    evac_stage(4, "ag0")
                if i == 30:
                    gate_attn(0)
                if i == 29:
                    dve.wait_ge(s_ych, 1)
                    dve.tensor_tensor(ycL[:], cT[:], ycH[:].bitcast(F32), ALU.subtract).then_inc(s_ycl, 1)
                if i == 32:
                    dve.wait_ge(s_yat, 1)
                    evac_stage(5, "ag1")
            gate_attn(1)
            build_dve(dve, "yattn", A(aH, 8), A(aL, 8))

            for j in range(4):
                g = G[f"wo{j}"]
                c = slice(j * NG, (j + 1) * NG)
                b = bias_slot(dve, g["name"])
                for t in range(TT):
                    last = dve.scalar_tensor_tensor(out=x[:, t, c], in0=x[:, t, c], scalar=ALPHA, in1=b,
                                                    op0=ALU.mult, op1=ALU.add)
                last.then_inc(bias_used, 1)
                dve.wait_ge(bias_used, j + 1)
                psum_ready(dve, g)
                for t in range(TT):
                    dve.tensor_tensor(x[:, t, c], x[:, t, c], ps_g[pair_of(g)][t][:], ALU.add
                                      ).then_inc(s_free[pair_of(g)], 1)
                evacuated(dve, g)
                for t in range(TT):
                    last = dve.bn_stats(bnst[:, t, j, :], x[:, t, j * NG:(j + 1) * NG])
            link(last)
            for t in range(TT):
                link(dve.bn_aggr(mv[:, t, :], bnst[:, t].rearrange("p a b -> p (a b)")))
            link(dve.tensor_scalar(var_ln, mv[:, :, 1], LN_EPS, None, ALU.add))
            dve.tensor_copy(mean_ln, mv[:, :, 0]).then_inc(s_var, 1)
            roots = [0]

            def rooted(ap):
                roots[0] += 1
                dve.wait_ge(s_sqrt, roots[0])
                link(dve.reciprocal(ap, ap))

            def variance(ap, n, eps=EPS):
                dve.tensor_scalar(ap, ap, 1.0 / n, eps, ALU.mult, ALU.add).then_inc(s_var, 1)

            rooted(var_ln)
            for q in range(4):
                c = slice(q * NG, (q + 1) * NG)
                for t in range(TT):
                    last = dve.tensor_scalar(x[:, t, c], x[:, t, c], mean_ln[:, t:t + 1], var_ln[:, t:t + 1],
                                             ALU.subtract, ALU.mult)
                last.then_inc(s_xn, 1)

            def layer_norm_gain(q):
                c = slice(q * NG, (q + 1) * NG)
                dve.wait_ge(s_xt, built("h", 4 * q + 4))
                for i, op in ((0, ALU.mult), (1, ALU.add)):
                    last = dve.tensor_tensor(x[:, :, c], x[:, :, c],
                                             ln_rows[:, i, c].unsqueeze(1).to_broadcast([P, TT, NG]), op)
                    if i == 0:
                        link(last)
                last.then_inc(s_x1, 1)

            dve.wait_ge(s_xn, 4)
            u0 = builds["h"][0]
            for u in range(8):
                dve.wait_ge(s_xh, u0 + u + 1)
                for k in range(2):
                    last = dve.tensor_scalar(h_lin[:, k * T:(k + 1) * T], build_bank("h", u)[:, k * T:(k + 1) * T],
                                             cols[:, HG + 2 * u + k:HG + 2 * u + k + 1],
                                             cols[:, HB + 2 * u + k:HB + 2 * u + k + 1], ALU.mult, ALU.add)
                link(last)
                dve.tensor_tensor(aL[:, 2 * u:2 * u + 2, :].rearrange("p k t -> p (k t)"), h_lin[:],
                                  aH[:, 2 * u:2 * u + 2, :].rearrange("p k t -> p (k t)").bitcast(F32),
                                  ALU.subtract).then_inc(s_xl, 1)
                dve.wait_ge(s_xl, u0 + u + 1)
                if u in (3, 4, 6, 7):
                    layer_norm_gain((3, 4, 6, 7).index(u))
            link(dve.tensor_scalar(colq, cols[:, GQ:GQ + 1], float(DK) ** -0.5, None, ALU.mult))
            dve.wait_ge(s_ss, 1)
            variance(ss, D)
            rooted(ss)
            r2 = ss

            def take(g, t, dst, a0, a1):
                return dve.tensor_scalar(dst, ps_g[pair_of(g)][t][:, a0:a1], r2[:, t:t + 1], None, ALU.mult)

            def evac_rows(name, dst, a0=0, a1=None):
                g = G[name]
                psum_ready(dve, g)
                for t in range(TT):
                    take(g, t, dst(t), a0, a1 or g["n"]).then_inc(s_free[pair_of(g)], 1)
                evacuated(dve, g)

            def head_squares(rows, scratch, sums):
                link(dve.tensor_tensor(scratch, rows, rows, ALU.mult))
                link(dve.tensor_reduce(sums, scratch, AX_X, ALU.add))

            def q_rows(i):
                evac_rows(f"nq{i}", lambda t: nq[:, t, 4 * i:4 * i + 4, :].rearrange("p h d -> p (h d)"))
                rows = nq[:, :, 4 * i:4 * i + 4, :]
                sums = ss_q[:, i].rearrange("p (t h) -> p t h", t=TT)
                head_squares(rows, stg2[:].rearrange("p t (h d) -> p t h d", h=4), sums)
                variance(ss_q[:, i], DK)
                rooted(ss_q[:, i])
                dve.tensor_tensor(rows, rows, sums.unsqueeze(3).to_broadcast([P, TT, 4, DK]),
                                  ALU.mult).then_inc(s_t2s, 1)

            def kv_rows(i, name, v_):
                g = G[name]
                psum_ready(dve, g)
                for t in range(TT):
                    take(g, t, stg2[:, t, 0:T], 0, T)
                    take(g, t, v_[:, t, :], T, 2 * T).then_inc(s_free[pair_of(g)], 1)
                evacuated(dve, g)
                rows = stg2[:, :, 0:T].rearrange("p t (h d) -> p t h d", h=KVH)
                sums = ss_k[:, i].rearrange("p (t h) -> p t h", t=TT)
                head_squares(rows, stg2[:, :, T:2 * T].rearrange("p t (h d) -> p t h d", h=KVH), sums)
                variance(ss_k[:, i], DK)
                rooted(ss_k[:, i])
                dve.tensor_tensor(rows, rows, sums.unsqueeze(3).to_broadcast([P, TT, KVH, DK]),
                                  ALU.mult).then_inc(s_t2s, 1)

            q_rows(0)
            q_rows(1)
            evac_rows("ncmp", lambda t: stg2[:, t, :])
            dve.memset(hidTv[:], 0.0).then_inc(s_c2v, 1)
            dve.memset(vc_bd[:], 0.0)
            dve.memset(pc[:], 0.0).then_inc(s_t2s, 1)
            dve.wait_ge(s_t2c, 6)
            for i, (src, pe0) in enumerate(((kcT, PEK), (vcT, PEV))):
                for h in range(2):
                    for kv in range(KVH):
                        last = dve.tensor_tensor(
                            kp[:, i, 16 * h:16 * h + 16, kv, :],
                            src[:, kv, 16 * h:16 * h + 16 * NCMP].rearrange("p (n b) -> p b n", b=16),
                            cols[:, pe0 + 16 * h:pe0 + 16 * h + 16].unsqueeze(2).to_broadcast([P, 16, NCMP]), ALU.add)
                last.then_inc(s_kp, 1)
            kv_rows(0, "nslc", vs)
            gla_masks()
            dve.wait_ge(s_c2, 1)
            link(dve.tensor_copy(kcn[:], ps_m[1][0:2 * NCMP, 0:P]))
            dve.wait_ge(s_t2s, 3)
            for kv in range(KVH):
                for r in range(4):
                    last = dve.tensor_copy(vc_bd[32 * r:32 * r + 32, kv, r, :],
                                           ps_m[1][32 * r:32 * r + 32, (1 + kv) * P:(2 + kv) * P])
            last.then_inc(s_c2v, 1)
            link(dve.tensor_tensor(sq_c[:], kcn[:], kcn[:], ALU.mult))
            link(dve.tensor_reduce(ss_c, sq_c[:], AX_X, ALU.add))
            variance(ss_c, DK)
            rooted(ss_c)
            dve.tensor_scalar(kcn[:], kcn[:], ss_c, None, ALU.mult).then_inc(s_t2s, 1)
            dve.wait_ge(s_t2c, 7)
            kv_rows(1, "nwin", vw)
            dve.wait_ge(s_csc, 1)
            src = ps_m[2][:, 0:256].rearrange("p (t h n) -> p t h n", t=TT, h=QH)
            for h in range(QH):
                last = dve.scalar_tensor_tensor(out=pc[:, :, h, 0:NCMP], in0=distc[:, :, 0:NCMP],
                                                scalar=2.0 ** -(h + 1), in1=src[:, :, h, 0:NCMP], op0=ALU.mult,
                                                op1=ALU.add)
            last.then_inc(s_csm, 1)
            dve.wait_ge(s_csm, 1)
            pcv = pc[:, :, :, 0:NCMP].rearrange("p t h n -> p (t h) n")
            link(dve.tensor_reduce(mxc, pcv, AX_X, ALU.max))
            dve.tensor_tensor(pcv, pcv, mxc.unsqueeze(2).to_broadcast([P, TT * QH, NCMP]), ALU.subtract).then_inc(s_csm, 1)
            dve.wait_ge(s_cexp, 1)
            link(dve.tensor_reduce(denc, pcv, AX_X, ALU.add))
            link(dve.reciprocal(rc, denc))
            link(dve.tensor_tensor(rc.rearrange("p (t h) -> p t h", t=TT), rc.rearrange("p (t h) -> p t h", t=TT),
                                   visc[:].unsqueeze(2).to_broadcast([P, TT, QH]), ALU.mult))
            dve.tensor_tensor(pcv, pcv, rc.unsqueeze(2).to_broadcast([P, TT * QH, NCMP]), ALU.mult).then_inc(s_t2s, 1)
            g = G["glq0"]
            psum_ready(dve, g)
            dve.wait_ge(s_t2c, 11)
            for t in range(TT):
                dve.scalar_tensor_tensor(out=gates[:, t, :], in0=ps_g[pair_of(g)][t][:, 0:24], scalar=r2[:, t:t + 1],
                                         in1=bgate[:], op0=ALU.mult, op1=ALU.add)
                last = take(g, t, stg2[:, t, 0:T], 24, 24 + T)
                last.then_inc(s_free[pair_of(g)], 1)
            evacuated(dve, g)
            for i in range(4):
                t, kv = i // KVH, i % KVH
                if i == 0:
                    dve.wait_ge(s_gsig, 1)
                dve.wait_ge(s_cpv, i + 1)
                gt = gates[:, t, :].rearrange("p (h b) -> p h b", b=3)[:, 4 * kv:4 * kv + 4, 0:1]
                dve.tensor_tensor(yn[:, t, 4 * kv:4 * kv + 4, :], ps_m[1][:].rearrange("p (h d) -> p h d", h=4),
                                  gt.to_broadcast([P, 4, DK]), ALU.mult).then_inc(s_cyn, 1)
            dve.wait_ge(s_cyn, 4)

            def softmax2(u):
                br, h = divmod(u, QH)
                dve.wait_ge(s_sc2, u + 1)
                if u >= 2:
                    dve.wait_ge(s_pt2, u - 1)
                link(dve.scalar_tensor_tensor(out=sS2[:, u % 2, :], in0=dist2[:], scalar=2.0 ** -(h + 1),
                                              in1=ps_m[2][:, 0:3 * P], op0=ALU.mult, op1=ALU.add))
                dve.tensor_reduce(mx2[:, u, 0:1], sS2[:, u % 2, 0:P], AX_X, ALU.max, negate=True)
                dve.tensor_reduce(mx2[:, u, 1:2], sS2[:, u % 2, P:], AX_X, ALU.max, negate=True).then_inc(s_sm2, 1)

            def normalize2(u):
                br, h = divmod(u, QH)
                dve.wait_ge(s_pv2, u + 1)
                link(dve.reciprocal(rden2[:, u, :], den2[:, u, :]))
                link(dve.tensor_tensor(rden2[:, u, :], rden2[:, u, :], gates[:, :, 3 * h + 1 + br], ALU.mult))
                if br == 1:
                    dve.wait_ge(s_yn2, u - QH + 1)
                for t in range(TT):
                    last = dve.scalar_tensor_tensor(out=yn[:, t, h, :], in0=ps_m[1][:, t * DK:(t + 1) * DK],
                                                    scalar=rden2[:, u, t:t + 1], in1=yn[:, t, h, :], op0=ALU.mult,
                                                    op1=ALU.add)
                last.then_inc(s_yn2, 1)

            lq1 = G["lq1"]["s0"]
            for i in range(3, 31):
                if i == 29:
                    dve.wait_ge(s_z, 3)
                    link(dve.scalar_tensor_tensor(out=gz[:], in0=gz[:], scalar=0.0, in1=QK[1][:], op0=ALU.min, op1=ALU.subtract))
                    for h in range(GH):
                        last = dve.tensor_tensor_scan(gb[:, h, :], ones[:], gz[:, h * T:(h + 1) * T], 0.0, ALU.mult, ALU.add)
                    link(last)
                if i - 5 in nsa_units:
                    normalize2(nsa_units[i - 5])
                if i in nsa_units:
                    softmax2(nsa_units[i])
                if i == 8:
                    dve.wait_ge(s_t2c, 13)
                    evac_rows("lq1", lambda t: stg2[:, t, 0:T])
                if i == 16:
                    dve.wait_ge(s_t2c, 14)
                    g = G["lar0"]
                    psum_ready(dve, g)
                    for t in range(TT):
                        take(g, t, stg2[:, t, 0:16], 0, 16)
                        take(g, t, rl[:, t, 0:T], 16, 16 + T).then_inc(s_free[pair_of(g)], 1)
                    evacuated(dve, g)
                if i == 24:
                    dve.wait_ge(s_t2c, 15)
                    evac_rows("lk", lambda t: stg2[:, t, :])
            dve.wait_ge(s_yn2, 2 * QH)
            gbf = gb[:].rearrange("p h t -> p (h t)")
            qf, kf = qlT[:].rearrange("p h t -> p (h t)"), klT[:].rearrange("p h t -> p (h t)")

            def halves(ap, L):
                return ap.rearrange("p (m two l) -> p m two l", two=2, l=L)

            def level_size(i):
                return 2 ** (LEVELS - i) if i < 8 else 128

            def level_diff(i):
                L = level_size(i)
                b_, e_ = halves(gbf, L), halves(E[i % 2][:], L)
                m = GH * T // (2 * L)
                ref = b_[:, :, 0, L - 1:L].to_broadcast([P, m, L])
                dve.tensor_tensor(e_[:, :, 0, :], ref, b_[:, :, 0, :], ALU.subtract)
                dve.tensor_tensor(e_[:, :, 1, :], b_[:, :, 1, :], ref, ALU.subtract).then_inc(s_gE, 1)

            def level_operand(i):
                L = level_size(i)
                dve.wait_ge(s_gX, i)
                if i >= 3:
                    dve.wait_ge(s_gP, 2 * (i - 1))
                e_, o_ = halves(E[i % 2][:], L), halves(QK[i % 2][:], L)
                dve.tensor_tensor(o_[:, :, 0, :], e_[:, :, 0, :], halves(kf, L)[:, :, 0, :], ALU.mult)
                dve.tensor_tensor(o_[:, :, 1, :], e_[:, :, 1, :], halves(qf, L)[:, :, 1, :], ALU.mult).then_inc(s_gQ, 1)

            def level_take(i):
                for h in range(TT if i < 8 else 1):
                    dve.wait_ge(s_gP, 2 * i + h + 1)
                    src = ps_m[2 + h][:].rearrange("p (g q) -> p g q", g=GH)
                    if i == 8:
                        dve.tensor_copy(sT[:, 2], src).then_inc(s_gS, 1)
                    else:
                        l = LEVELS if i == 0 else LEVELS - i
                        dve.wait_ge(s_gS, 2 * i + h + 1)
                        dve.copy_predicated(sT[:, h], lmask[:, l, :].unsqueeze(1).to_broadcast([P, GH, P]), src
                                            ).then_inc(s_gS, 1)

            dve.wait_ge(s_t2c, 19)
            level_diff(1)
            dve.memset(sT[:], 0.0).then_inc(s_gS, 1)
            dve.wait_ge(s_gS, 1)
            level_take(0)
            level_diff(2)
            for i in range(1, 9):
                level_operand(i)
                if i + 2 <= 8:
                    dve.wait_ge(s_gQ, i)
                    level_diff(i + 2)
                level_take(i)
                if i == 1:
                    evac_rows("lv0", lambda t: vl[:, t, 0:2, :].rearrange("p h v -> p (h v)"))
                if i in (2, 3):
                    t = i - 2
                    rows = yn[:, t].rearrange("p h d -> p (h d)")
                    sq_n = stg2[:].rearrange("p t n -> p (t n)")
                    link(dve.tensor_tensor(sq_n, rows, rows, ALU.mult))
                    link(dve.tensor_reduce(ss_n[:, 8 * t:8 * t + 8], sq_n.rearrange("p (h d) -> p h d", h=QH), AX_X,
                                           ALU.add))
                    if t == TT - 1:
                        variance(ss_n, DK)
                if i == 5:
                    evac_rows("lv1", lambda t: vl[:, t, 2:4, :].rearrange("p h v -> p (h v)"))
                if i == 8:
                    g = G["lr1"]
                    psum_ready(dve, g)
                    for t in range(TT):
                        take(g, t, rl[:, t, T:T + NG], 0, NG).then_inc(s_free[pair_of(g)], 1)
                    evacuated(dve, g)
            rooted(ss_n)
            dve.tensor_tensor(yn[:], yn[:], ss_n.rearrange("p (t h) -> p t h", t=TT).unsqueeze(3).to_broadcast(
                [P, TT, QH, DK]), ALU.mult).then_inc(s_y2n, 1)
            for i in range(4):
                t, hp = divmod(i, 2)
                dve.wait_ge(s_go, i + 1)
                dve.tensor_copy(yg[:, t, 2 * hp:2 * hp + 2, :].rearrange("p h v -> p (h v)"), ps_m[2 + i % 2][:]
                                ).then_inc(s_goc, 1)
            dve.wait_ge(s_goc, 4)
            head_squares(yg[:], sc8[:], ss_g.rearrange("p (t h) -> p t h", t=TT))
            variance(ss_g, DV)
            evac_rows("lr2", lambda t: rl[:, t, 768:])

            def y2_lo(us):
                build_dve(dve, "y2", A(aH), A(aL),
                          lambda k: cols[:, GNS:GNS + 1] if k < 8 else cols[:, GGL + k % 2:GGL + k % 2 + 1], only=us)
            y2_lo(range(0, 4))
            rooted(ss_g)
            link(dve.tensor_tensor(yg[:], yg[:], ss_g.rearrange("p (t h) -> p t h", t=TT).unsqueeze(3).to_broadcast(
                [P, TT, GH, DV]), ALU.mult))
            dve.wait_ge(s_rl, 1)
            dve.tensor_tensor(yg[:].rearrange("p t h v -> p t (h v)"), yg[:].rearrange("p t h v -> p t (h v)"),
                              rl[:], ALU.mult).then_inc(s_y2g, 1)
            y2_lo(range(4, 8))

            def residual(name, later=None):
                g = G[name]
                j = int(name[-1])
                psum_ready(dve, g, later)
                for t in range(TT):
                    c = x[:, t, bass.ds(j * NG + plus(later, 2 * NG), NG)]
                    dve.tensor_tensor(c, c, ps_g[pair_of(g)][t][:], ALU.add).then_inc(s_free[pair_of(g)], 1)

            def mem_units(us):
                build_dve(dve, "mem", A(mH), A(mL), lambda k: cols[:, GME + k:GME + k + 1], only=us)

            residual("w2o0")
            residual("w2o1")
            mem_units(range(0, 3))
            residual("w2o2")
            mem_units(range(3, 8))
            residual("w2o3")
            dve.wait_ge(s_sqs, 2)
            variance(ss_m, D)
            rooted(ss_m)
            build_dve(dve, "hq", A(aH), A(aL), lambda k: cols[:, GC + k:GC + k + 1])
            dve.wait_ge(s_sqs, 4)
            variance(ss_x2, D)
            rooted(ss_x2)
            link(dve.tensor_scalar(colcq, cols[:, GCQ:GCQ + 1], float(DK) ** -0.5, None, ALU.mult))

            def cross_rows(name, scale, dst, sums, scratch):
                g = G[name]
                psum_ready(dve, g)
                for t in range(TT):
                    dve.tensor_scalar(dst[:, t].rearrange("p h d -> p (h d)"), ps_g[pair_of(g)][t][:], scale[:, t:t + 1],
                                      None, ALU.mult).then_inc(s_free[pair_of(g)], 1)
                evacuated(dve, g)
                head_squares(dst[:], scratch[:], sums.rearrange("p (t h) -> p t h", t=TT))
                variance(sums, DK)
                rooted(sums)
                dve.tensor_tensor(dst[:], dst[:], sums.rearrange("p (t h) -> p t h", t=TT).unsqueeze(3).to_broadcast(
                    [P, TT, MH, DK]), ALU.mult).then_inc(s_ckr, 1)

            cross_rows("mk", ss_m, ckn, ss_ck, scr4)
            cross_rows("mq", ss_x2, cqn, ss_cq, scr4)
            for u in range(MH):
                dve.wait_ge(s_sc3, u + 1)
                dve.tensor_reduce(mx3[:, u, :], ps_m[2 * (u % 2)][:].rearrange("p (t m) -> p t m", t=TT), AX_X, ALU.max,
                                  negate=True).then_inc(s_sm3, 1)
            g = G["mv"]
            psum_ready(dve, g)
            for t in range(TT):
                dve.tensor_scalar(cvn[:, t, :], ps_g[pair_of(g)][t][:], ss_m[:, t:t + 1], None,
                                  ALU.mult).then_inc(s_free[pair_of(g)], 1)
            for u in range(MH):
                dve.wait_ge(s_pv3, u + 1)
                link(dve.reciprocal(den3[:, u, :], den3[:, u, :]))
                for t in range(TT):
                    last = dve.tensor_scalar(ocn[:, t, u, :], ps_m[1 + u % 2][:, t * P:(t + 1) * P], den3[:, u, t:t + 1], None,
                                             ALU.mult)
                last.then_inc(s_on, 1)
            build_dve(dve, "oc", A(ocH), A(ocL))
            for i in range(4):
                residual(f"co{i}")
            build_dve(dve, "hf", A(aH), A(aL), lambda k: cols[:, GF + k:GF + k + 1])
            dve.wait_ge(s_sqs, 6)
            variance(ss_x3, D)
            roots[0] += 1
            dve.wait_ge(s_sqrt, roots[0])
            dve.reciprocal(ss_x3, ss_x3).then_inc(s_ffs, 1)
            dve.wait_ge(s_ffs, 1)

            def gate_up(i, hidden=None, at=None, later=None):
                if hidden is not None:
                    build_dve(dve, f"gu{hidden}", A_at(guH, at), A_at(guL, at), later=later)
                g = G[f"fu{i}"]
                evacuated(dve, G[f"fg{i}"], later)
                psum_ready(dve, g, later)
                if hidden is not None:
                    dve.wait_ge(s_xt, built(f"gu{hidden}", 4) + plus(later, UNITS_GU))
                elif i >= 1:
                    dve.wait_ge(s_xt, built(f"gu{i - 1}", 4))
                for t in range(TT):
                    dve.scalar_tensor_tensor(out=hn[:, t, :], in0=ps_g[pair_of(g)][t][:], scalar=ss_x3[:, t:t + 1],
                                             in1=sg[:, t, :], op0=ALU.mult, op1=ALU.mult
                                             ).then_inc(s_free[pair_of(g)], 1)

            for part, (g0, n) in enumerate(PARTS):
                gate_up(g0)
                with dve.Fori(0, n - 1) as it:
                    gate_up(g0 + 1, g0, it * (NG // P), (it, 2 * KT // STEP))
                build_dve(dve, f"gu{g0 + n - 1}", A(guH, 4 * (n - 1)), A(guL, 4 * (n - 1)))
                with dve.Fori(0, 2) as it:
                    for i in range(2):
                        residual(f"fd{part}{i}", (it, 2 * G[f"fd{part}0"]["ns"]))


_INS = ["x", "w_in", "b_in", "conv_w", "conv_b", "conv_ln_g", "conv_ln_b", "sinks", "w_out", "b_out", "ln_g", "ln_b",
        "mem_2", "g_mix_2", "w_in_2", "b_nsa_gate_2", "g_q_2", "g_kc_2", "g_ks_2", "g_kw_2", "pe_k_2", "pe_v_2",
        "w_ck1_2", "w_ck2_2", "w_cv1_2", "w_cv2_2", "g_nsa_out_2", "w_gk2_2", "b_gk_2", "g_gla_out_2", "w_out_2",
        "g_cross_2", "g_mem_2", "w_cq_2", "w_ck_2", "w_cv_2", "g_cq_2", "g_ck_2", "w_co_2", "g_ffn_2", "w_gu_2",
        "w_down_2"]


def kernel(**inputs):
    import numpy as _np
    import concourse.bacc as _bacc
    from concourse import mybir as _mybir
    from concourse.bass_utils import run_bass_kernel_spmd as _run

    nc = _bacc.Bacc("TRN2", target_bir_lowering=False, num_devices=1)
    arrays, args = {}, {}
    for name in _INS:
        v = _np.ascontiguousarray(inputs[name])
        arrays[f"in_{name}_dram"] = v
        args[name] = nc.dram_tensor(f"in_{name}_dram", v.shape, _mybir.dt.from_np(v.dtype), kind="ExternalInput").ap()
    out = nc.dram_tensor("out_0_dram", (1, T, D), F32, kind="ExternalOutput").ap()
    stack_kernel(nc, args, out)
    r = _run(nc, [arrays], core_ids=[0])
    return r.results[0]["out_0_dram"]
```
